# Optimizing a Trainium2 kernel written in Bass

```python
import jax, jax.numpy as jnp
from jax import lax
import numpy as np
import math
import jax
import jax.numpy as jnp

D_MODEL = 1024
BATCH = 1
SEQ = 256
DEPTH = 2

MEM_LEN = 256
MLA_HEADS = 8
MLA_NOPE = 64
MLA_ROPE = 32
MLA_V = 64
Q_LORA = 384
KV_LORA = 256
ROPE_THETA = 10000.0
Q_BLOCK = 128
HG_HEADS = 4
HG_KDIM = 128
HG_VDIM = 128
HG_CHUNK = 64
MEM_HEADS = 4
MEM_HDIM = 128
D_FF = 2816
N_BRANCH = 3
NORM_EPS = 1e-6

MLA_QK = MLA_NOPE + MLA_ROPE
HG_K = HG_HEADS * HG_KDIM
HG_V = HG_HEADS * HG_VDIM
MEM_W = MEM_HEADS * MEM_HDIM
IN_SPLITS = (Q_LORA, KV_LORA, MLA_ROPE, HG_K, HG_K, HG_V, HG_V, MEM_W, N_BRANCH * D_MODEL)
D_IN = sum(IN_SPLITS)


def rmsnorm(x, g):
    xf = x.astype(jnp.float32)
    y = xf * lax.rsqrt(jnp.mean(xf * xf, axis=-1, keepdims=True) + NORM_EPS)
    return (y * g.astype(jnp.float32)).astype(x.dtype)

def swiglu(x, w_in, w_out):
    a, b = jnp.split(x @ w_in, 2, axis=-1)
    return (jax.nn.silu(a) * b) @ w_out

def split_sizes(z, sizes):
    idx = [int(v) for v in np.cumsum(sizes)[:-1]]
    return jnp.split(z, idx, axis=-1)

def apply_rope(t, cos, sin):
    tf = t.astype(jnp.float32)
    t1, t2 = jnp.split(tf, 2, axis=-1)
    out = jnp.concatenate([t1 * cos - t2 * sin, t2 * cos + t1 * sin], axis=-1)
    return out.astype(t.dtype)

def causal_mla_attention(q_nope, q_rope, k_nope, k_rope, v):
    B, S, H, _ = q_nope.shape
    nb = S // Q_BLOCK
    scale = MLA_QK ** -0.5
    k_pos = jnp.arange(S)

    def to_blocks(t):
        return jnp.moveaxis(t.reshape((B, nb, Q_BLOCK) + t.shape[2:]), 1, 0)

    def block(args):
        i, qn, qr = args
        s = jnp.einsum('bqhd,bkhd->bhqk', qn, k_nope) + jnp.einsum('bqhd,bkd->bhqk', qr, k_rope)
        s = s.astype(jnp.float32) * scale
        q_pos = i * Q_BLOCK + jnp.arange(Q_BLOCK)
        s = jnp.where(q_pos[:, None] >= k_pos[None, :], s, -jnp.inf)
        p = jax.nn.softmax(s, axis=-1).astype(v.dtype)
        return jnp.einsum('bhqk,bkhd->bqhd', p, v)

    o = lax.map(block, (jnp.arange(nb), to_blocks(q_nope), to_blocks(q_rope)))
    return jnp.moveaxis(o, 0, 1).reshape(B, S, H * MLA_V)

def mla_branch(c_q, c_kv, k_r, cos, sin, q_norm_g, kv_norm_g, w_uq, w_uk, w_uv):
    B, S, _ = c_q.shape
    q = (rmsnorm(c_q, q_norm_g) @ w_uq).reshape(B, S, MLA_HEADS, MLA_QK)
    q_nope = q[..., :MLA_NOPE]
    q_rope = apply_rope(q[..., MLA_NOPE:], cos[:, :, None, :], sin[:, :, None, :])
    k_rope = apply_rope(k_r, cos, sin)
    ckv = rmsnorm(c_kv, kv_norm_g)
    k_nope = (ckv @ w_uk).reshape(B, S, MLA_HEADS, MLA_NOPE)
    v = (ckv @ w_uv).reshape(B, S, MLA_HEADS, MLA_V)
    return causal_mla_attention(q_nope, q_rope, k_nope, k_rope, v)

def chunk_gated_recurrence(q, k, v, g):
    B, S, H, K = q.shape
    V = v.shape[-1]
    n = S // HG_CHUNK
    causal = jnp.tril(jnp.ones((HG_CHUNK, HG_CHUNK), dtype=bool))

    def chunks(t):
        return t.reshape(B, n, HG_CHUNK, H, t.shape[-1]).transpose(1, 0, 3, 2, 4)

    def step(state, inp):
        qc, kc, vc, gc = inp
        G = jnp.cumsum(gc, axis=2)
        o_inter = jnp.einsum('bhck,bhkv->bhcv', qc * jnp.exp(G), state)
        diff = G[:, :, :, None, :] - G[:, :, None, :, :]
        decay = jnp.exp(jnp.where(causal[:, :, None], diff, -jnp.inf))
        A = jnp.einsum('bhtsk,bhsk->bhts', qc[:, :, :, None, :] * decay, kc)
        o_intra = jnp.einsum('bhts,bhsv->bhtv', A, vc)
        G_last = G[:, :, -1:, :]
        new_state = jnp.exp(G_last[:, :, 0, :])[..., None] * state + jnp.einsum(
            'bhck,bhcv->bhkv', kc * jnp.exp(G_last - G), vc)
        return new_state, o_inter + o_intra

    s0 = jnp.zeros((B, H, K, V), jnp.float32)
    _, o = lax.scan(step, s0, (chunks(q), chunks(k), chunks(v), chunks(g)))
    return o.transpose(1, 0, 3, 2, 4).reshape(B, S, H, V)

def hgrn2_branch(q, f_logit, i_in, gate, lb, o_norm_g):
    B, S, _ = q.shape
    dt = q.dtype
    qf = jax.nn.silu(q.astype(jnp.float32)).reshape(B, S, HG_HEADS, HG_KDIM)
    z = f_logit.astype(jnp.float32)
    g = jnp.logaddexp(jnp.log(lb), jnp.log1p(-lb) + jax.nn.log_sigmoid(z))
    k = (1.0 - lb) * jax.nn.sigmoid(-z)
    g = g.reshape(B, S, HG_HEADS, HG_KDIM)
    k = k.reshape(B, S, HG_HEADS, HG_KDIM)
    v = i_in.astype(jnp.float32).reshape(B, S, HG_HEADS, HG_VDIM)
    o = chunk_gated_recurrence(qf, k, v, g)
    o = rmsnorm(o, o_norm_g) * jax.nn.silu(gate.astype(jnp.float32).reshape(B, S, HG_HEADS, HG_VDIM))
    return o.reshape(B, S, HG_V).astype(dt)

def memory_branch(q, mem_n, w_mem_kv):
    B, S, _ = q.shape
    M = mem_n.shape[1]
    qh = q.reshape(B, S, MEM_HEADS, MEM_HDIM)
    k, v = jnp.split(mem_n @ w_mem_kv, 2, axis=-1)
    k = k.reshape(B, M, MEM_HEADS, MEM_HDIM)
    v = v.reshape(B, M, MEM_HEADS, MEM_HDIM)
    s = jnp.einsum('bqhd,bmhd->bhqm', qh, k).astype(jnp.float32) * (MEM_HDIM ** -0.5)
    p = jax.nn.softmax(s, axis=-1).astype(v.dtype)
    return jnp.einsum('bhqm,bmhd->bqhd', p, v).reshape(B, S, MEM_W)

def first_inputs(seed: int = 0) -> dict:
    key = jax.random.key(seed)
    ks = jax.random.split(key, 32)
    f32 = jnp.float32

    def w(k, shape, fan_in):
        return jax.random.normal(k, shape, f32) * (fan_in ** -0.5)

    def gain(k, shape):
        return 1.0 + 0.02 * jax.random.normal(k, shape, f32)

    x = jax.random.normal(ks[0], (BATCH, SEQ, D_MODEL), f32)
    mem = jax.random.normal(ks[1], (BATCH, MEM_LEN, D_MODEL), f32)
    offsets = jax.random.randint(ks[2], (BATCH, 1), 0, 1024, dtype=jnp.int32)
    positions = offsets + jnp.arange(SEQ, dtype=jnp.int32)[None, :]
    return {
        "x": x,
        "mem": mem,
        "positions": positions,
        "ffn1_norm": gain(ks[3], (DEPTH, D_MODEL)),
        "w_ffn1_in": w(ks[4], (DEPTH, D_MODEL, 2 * D_FF), D_MODEL),
        "w_ffn1_out": w(ks[5], (DEPTH, D_FF, D_MODEL), D_FF),
        "mix_norm": gain(ks[6], (DEPTH, D_MODEL)),
        "w_in": w(ks[7], (DEPTH, D_MODEL, D_IN), D_MODEL),
        "q_lat_norm": gain(ks[8], (DEPTH, Q_LORA)),
        "kv_lat_norm": gain(ks[9], (DEPTH, KV_LORA)),
        "w_uq": w(ks[10], (DEPTH, Q_LORA, MLA_HEADS * MLA_QK), Q_LORA),
        "w_uk": w(ks[11], (DEPTH, KV_LORA, MLA_HEADS * MLA_NOPE), KV_LORA),
        "w_uv": w(ks[12], (DEPTH, KV_LORA, MLA_HEADS * MLA_V), KV_LORA),
        "w_o_mla": w(ks[13], (DEPTH, MLA_HEADS * MLA_V, D_MODEL), MLA_HEADS * MLA_V),
        "hg_lower_bounds": jax.random.normal(ks[14], (DEPTH, HG_K), f32),
        "hg_out_norm": gain(ks[15], (DEPTH, HG_VDIM)),
        "w_o_hg": w(ks[16], (DEPTH, HG_V, D_MODEL), HG_V),
        "mem_norm": gain(ks[17], (DEPTH, D_MODEL)),
        "w_mem_kv": w(ks[18], (DEPTH, D_MODEL, 2 * MEM_W), D_MODEL),
        "w_o_mem": w(ks[19], (DEPTH, MEM_W, D_MODEL), MEM_W),
        "w_out": w(ks[20], (DEPTH, D_MODEL, D_MODEL), D_MODEL),
        "ffn2_norm": gain(ks[21], (DEPTH, D_MODEL)),
        "w_ffn2_in": w(ks[22], (DEPTH, D_MODEL, 2 * D_FF), D_MODEL),
        "w_ffn2_out": w(ks[23], (DEPTH, D_FF, D_MODEL), D_FF),
        "final_norm": gain(ks[24], (D_MODEL,)),
    }

def first_block(x, mem, positions, ffn1_norm, w_ffn1_in, w_ffn1_out, mix_norm, w_in,
              q_lat_norm, kv_lat_norm, w_uq, w_uk, w_uv, w_o_mla, hg_lower_bounds,
              hg_out_norm, w_o_hg, mem_norm, w_mem_kv, w_o_mem, w_out, ffn2_norm,
              w_ffn2_in, w_ffn2_out, final_norm):
    B, S, D = x.shape
    inv_freq = ROPE_THETA ** (-jnp.arange(0, MLA_ROPE, 2, dtype=jnp.float32) / MLA_ROPE)
    ang = positions.astype(jnp.float32)[..., None] * inv_freq
    cos, sin = jnp.cos(ang), jnp.sin(ang)
    lbs = jnp.cumsum(jax.nn.softmax(hg_lower_bounds.astype(jnp.float32), axis=0), axis=0)
    lbs = lbs - lbs[0:1]

    for l in range(DEPTH):
        x = x + 0.5 * swiglu(rmsnorm(x, ffn1_norm[l]), w_ffn1_in[l], w_ffn1_out[l])
        u = rmsnorm(x, mix_norm[l])
        c_q, c_kv, k_r, hq, hf, hi, hgate, mq, gate_logits = split_sizes(u @ w_in[l], IN_SPLITS)
        y_mla = mla_branch(c_q, c_kv, k_r, cos, sin, q_lat_norm[l], kv_lat_norm[l],
                           w_uq[l], w_uk[l], w_uv[l]) @ w_o_mla[l]
        y_hg = hgrn2_branch(hq, hf, hi, hgate, lbs[l], hg_out_norm[l]) @ w_o_hg[l]
        mem_n = rmsnorm(mem, mem_norm[l])
        y_mem = memory_branch(mq, mem_n, w_mem_kv[l]) @ w_o_mem[l]
        gates = jax.nn.sigmoid(gate_logits.reshape(B, S, N_BRANCH, D))
        merged = gates[:, :, 0] * y_mla + gates[:, :, 1] * y_hg + gates[:, :, 2] * y_mem
        x = x + merged @ w_out[l]
        x = x + 0.5 * swiglu(rmsnorm(x, ffn2_norm[l]), w_ffn2_in[l], w_ffn2_out[l])

    return rmsnorm(x, final_norm)


PLE_DIM = 256
NEG_INF = -1e30
NUM_BUCKETS = 32
MAX_DISTANCE = 128
A_HEADS = 4
A_HEAD_DIM = 64
A_QBLOCK = 128
B_HEADS = 8
B_GROUPS = 2
B_REP = B_HEADS // B_GROUPS
B_HEAD_DIM = 64
B_CMP_LEN = 32
B_CMP_STRIDE = 16
B_CMP_HIDDEN = 256
B_SEL_BLOCK = 64
B_SEL_TOPK = 16
B_WINDOW = 512
B_QBLOCK = 64
B_SEL_FORCE = 1e6
C_HEADS = 8
C_GROUPS = 2
C_REP = C_HEADS // C_GROUPS
C_HEAD_DIM = 64
C_WINDOW = 128
C_QBLOCK = 128

A_WIDTH = A_HEADS * 2 * A_HEAD_DIM
B_WIDTH = B_HEADS * B_HEAD_DIM
B_KV = B_GROUPS * B_HEAD_DIM
C_WIDTH = C_HEADS * C_HEAD_DIM
C_KV = C_GROUPS * C_HEAD_DIM
N_BIAS_HEADS = A_HEADS + B_HEADS + C_HEADS
IN_SPLITS_2 = (A_WIDTH, A_WIDTH, A_WIDTH,
             B_WIDTH, B_KV, B_KV, B_KV, B_KV, B_KV, B_KV, 3 * B_HEADS,
             C_WIDTH, C_KV, C_KV,
             D_MODEL, D_MODEL, D_MODEL)
D_IN_2 = 3 * A_WIDTH + B_WIDTH + 6 * B_KV + 3 * B_HEADS + C_WIDTH + 2 * C_KV + 3 * D_MODEL


def rms_norm(x, g):
    xf = x.astype(jnp.float32)
    y = xf * lax.rsqrt(jnp.mean(xf * xf, axis=-1, keepdims=True) + NORM_EPS)
    return (y * g.astype(jnp.float32)).astype(x.dtype)

def swiglu_2(x, wi, wo):
    gate, up = jnp.split(x @ wi, 2, axis=-1)
    return (jax.nn.silu(gate) * up) @ wo

def split_cols(z, sizes):
    outs, start = [], 0
    for s in sizes:
        outs.append(z[..., start:start + s])
        start += s
    return outs

def rel_bucket(dist):
    n = jnp.maximum(dist, 0)
    max_exact = NUM_BUCKETS // 2
    nf = jnp.maximum(n, 1).astype(jnp.float32)
    large = max_exact + (jnp.log(nf / max_exact) / math.log(MAX_DISTANCE / max_exact)
                         * (NUM_BUCKETS - max_exact)).astype(jnp.int32)
    large = jnp.minimum(large, NUM_BUCKETS - 1)
    return jnp.where(n < max_exact, n, large)

def head_bias(table, dist):
    return jnp.moveaxis(table[rel_bucket(dist)].astype(jnp.float32), -1, 0)

def grouped_head_bias(table, dist, groups, rep):
    b = head_bias(table, dist)
    return b.reshape((groups, rep) + dist.shape)

def masked_softmax(s, mask):
    return jax.nn.softmax(jnp.where(mask, s, NEG_INF), axis=-1) * mask

def diff_attention(q, k, v, bias_table, lam, lam_init, subln_g):
    bsz, seq = q.shape[:2]
    nblk = seq // A_QBLOCK
    scale = A_HEAD_DIM ** -0.5
    qb = q.reshape(bsz, nblk, A_QBLOCK, A_HEADS, 2, A_HEAD_DIM).swapaxes(0, 1)
    kpos = jnp.arange(seq)

    def block(args):
        i, qi = args
        qpos = i * A_QBLOCK + jnp.arange(A_QBLOCK)
        dist = qpos[:, None] - kpos[None, :]
        s = jnp.einsum('bqhcd,bkhcd->bchqk', qi, k, preferred_element_type=jnp.float32) * scale
        s = s + head_bias(bias_table, dist)[None, None]
        pr = masked_softmax(s, dist >= 0)
        attn = pr[:, 0] - lam * pr[:, 1]
        return jnp.einsum('bhqk,bkhe->bqhe', attn.astype(v.dtype), v)

    o = lax.map(block, (jnp.arange(nblk), qb))
    o = o.swapaxes(0, 1).reshape(bsz, seq, A_HEADS, 2 * A_HEAD_DIM)
    o = rms_norm(o, subln_g) * (1.0 - lam_init)
    return o.reshape(bsz, seq, A_WIDTH)

def nsa_attention(q, kc, vc, ks, vs, kw, vw, gates, bias_table, cmp_pos, cmp_w1, cmp_w2):
    bsz, seq = q.shape[:2]
    scale = B_HEAD_DIM ** -0.5
    n_chunk = seq // B_CMP_STRIDE
    n_cmp = n_chunk - 1
    n_sel = seq // B_SEL_BLOCK
    top_k = min(B_SEL_TOPK, n_sel)
    nblk = seq // B_QBLOCK

    def compress(t, pos, w1, w2):
        c = t.reshape(bsz, n_chunk, B_CMP_STRIDE, B_GROUPS, B_HEAD_DIM)
        blk = jnp.concatenate([c[:, :-1], c[:, 1:]], axis=2) + pos[None, None, :, None, :]
        blk = blk.transpose(0, 1, 3, 2, 4).reshape(bsz, n_cmp, B_GROUPS, B_CMP_LEN * B_HEAD_DIM)
        return jax.nn.gelu(blk @ w1) @ w2

    k_cmp = compress(kc, cmp_pos[0], cmp_w1[0], cmp_w2[0])
    v_cmp = compress(vc, cmp_pos[1], cmp_w1[1], cmp_w2[1])
    cmp_start = jnp.arange(n_cmp) * B_CMP_STRIDE
    cmp_end = cmp_start + B_CMP_LEN - 1
    sel_start = jnp.arange(n_sel) * B_SEL_BLOCK
    overlap = ((cmp_start[:, None] < sel_start[None, :] + B_SEL_BLOCK)
               & (cmp_start[:, None] + B_CMP_LEN > sel_start[None, :])).astype(jnp.float32)
    ks_blk = ks.reshape(bsz, n_sel, B_SEL_BLOCK, B_GROUPS, B_HEAD_DIM).transpose(0, 3, 1, 2, 4)
    vs_blk = vs.reshape(bsz, n_sel, B_SEL_BLOCK, B_GROUPS, B_HEAD_DIM).transpose(0, 3, 1, 2, 4)
    kw_pad = jnp.pad(kw, ((0, 0), (B_WINDOW, 0), (0, 0), (0, 0)))
    vw_pad = jnp.pad(vw, ((0, 0), (B_WINDOW, 0), (0, 0), (0, 0)))
    tbg = bias_table.reshape(NUM_BUCKETS, B_GROUPS, B_REP).transpose(1, 0, 2)
    b_idx = jnp.arange(bsz)[:, None, None, None]
    g_idx = jnp.arange(B_GROUPS)[None, :, None, None]
    blk_id = jnp.arange(n_sel)
    qb = q.reshape(bsz, nblk, B_QBLOCK, B_GROUPS, B_REP, B_HEAD_DIM).swapaxes(0, 1)
    gb = gates.reshape(bsz, nblk, B_QBLOCK, B_GROUPS, B_REP, 3).swapaxes(0, 1)

    def block(args):
        i, qi, gi = args
        qpos = i * B_QBLOCK + jnp.arange(B_QBLOCK)
        dist_c = qpos[:, None] - cmp_end[None, :]
        s_c = jnp.einsum('bqgrd,bngd->bgrqn', qi, k_cmp, preferred_element_type=jnp.float32) * scale
        s_c = s_c + grouped_head_bias(bias_table, dist_c, B_GROUPS, B_REP)
        p_c = masked_softmax(s_c, dist_c >= 0)
        o_c = jnp.einsum('bgrqn,bngd->bqgrd', p_c.astype(v_cmp.dtype), v_cmp)
        imp = jnp.einsum('bgrqn,nm->bgqm', p_c, overlap)
        cur = qpos // B_SEL_BLOCK
        forced = (blk_id[None, :] == 0) | (blk_id[None, :] == cur[:, None]) | (blk_id[None, :] == cur[:, None] - 1)
        future = blk_id[None, :] > cur[:, None]
        imp = jnp.where(forced, B_SEL_FORCE, jnp.where(future, -B_SEL_FORCE, imp))
        _, idx = lax.top_k(imp, top_k)
        n_keys = top_k * B_SEL_BLOCK
        k_sel = ks_blk[b_idx, g_idx, idx].reshape(bsz, B_GROUPS, B_QBLOCK, n_keys, B_HEAD_DIM)
        v_sel = vs_blk[b_idx, g_idx, idx].reshape(bsz, B_GROUPS, B_QBLOCK, n_keys, B_HEAD_DIM)
        kpos_s = (idx[..., None] * B_SEL_BLOCK + jnp.arange(B_SEL_BLOCK)).reshape(bsz, B_GROUPS, B_QBLOCK, n_keys)
        dist_s = qpos[None, None, :, None] - kpos_s
        bias_s = tbg[g_idx, rel_bucket(dist_s)].astype(jnp.float32).transpose(0, 1, 4, 2, 3)
        s_s = jnp.einsum('bqgrd,bgqld->bgrql', qi, k_sel, preferred_element_type=jnp.float32) * scale + bias_s
        p_s = masked_softmax(s_s, (dist_s >= 0)[:, :, None])
        o_s = jnp.einsum('bgrql,bgqld->bqgrd', p_s.astype(v_sel.dtype), v_sel)
        start = i * B_QBLOCK
        k_win = lax.dynamic_slice_in_dim(kw_pad, start, B_WINDOW + B_QBLOCK, axis=1)
        v_win = lax.dynamic_slice_in_dim(vw_pad, start, B_WINDOW + B_QBLOCK, axis=1)
        kpos_w = start - B_WINDOW + jnp.arange(B_WINDOW + B_QBLOCK)
        dist_w = qpos[:, None] - kpos_w[None, :]
        mask_w = (dist_w >= 0) & (dist_w < B_WINDOW) & (kpos_w >= 0)[None, :]
        s_w = jnp.einsum('bqgrd,bkgd->bgrqk', qi, k_win, preferred_element_type=jnp.float32) * scale
        s_w = s_w + grouped_head_bias(bias_table, dist_w, B_GROUPS, B_REP)
        p_w = masked_softmax(s_w, mask_w)
        o_w = jnp.einsum('bgrqk,bkgd->bqgrd', p_w.astype(v_win.dtype), v_win)
        return gi[..., 0:1] * o_c + gi[..., 1:2] * o_s + gi[..., 2:3] * o_w

    o = lax.map(block, (jnp.arange(nblk), qb, gb))
    return o.swapaxes(0, 1).reshape(bsz, seq, B_WIDTH)

def swa_sink_attention(q, k, v, bias_table, sinks):
    bsz, seq = q.shape[:2]
    scale = C_HEAD_DIM ** -0.5
    nblk = seq // C_QBLOCK
    k_pad = jnp.pad(k, ((0, 0), (C_WINDOW, 0), (0, 0), (0, 0)))
    v_pad = jnp.pad(v, ((0, 0), (C_WINDOW, 0), (0, 0), (0, 0)))
    qb = q.reshape(bsz, nblk, C_QBLOCK, C_GROUPS, C_REP, C_HEAD_DIM).swapaxes(0, 1)
    sink = jnp.broadcast_to(sinks.astype(jnp.float32).reshape(C_GROUPS, C_REP, 1, 1),
                            (bsz, C_GROUPS, C_REP, C_QBLOCK, 1))

    def block(args):
        i, qi = args
        start = i * C_QBLOCK
        qpos = start + jnp.arange(C_QBLOCK)
        kb = lax.dynamic_slice_in_dim(k_pad, start, C_WINDOW + C_QBLOCK, axis=1)
        vb = lax.dynamic_slice_in_dim(v_pad, start, C_WINDOW + C_QBLOCK, axis=1)
        kpos = start - C_WINDOW + jnp.arange(C_WINDOW + C_QBLOCK)
        dist = qpos[:, None] - kpos[None, :]
        mask = (dist >= 0) & (dist < C_WINDOW) & (kpos >= 0)[None, :]
        s = jnp.einsum('bqgrd,bkgd->bgrqk', qi, kb, preferred_element_type=jnp.float32) * scale
        s = jnp.where(mask, s + grouped_head_bias(bias_table, dist, C_GROUPS, C_REP), NEG_INF)
        pr = jax.nn.softmax(jnp.concatenate([s, sink], axis=-1), axis=-1)[..., :-1]
        return jnp.einsum('bgrqk,bkgd->bqgrd', pr.astype(vb.dtype), vb)

    o = lax.map(block, (jnp.arange(nblk), qb))
    return o.swapaxes(0, 1).reshape(bsz, seq, C_WIDTH)

def second_inputs(seed: int = 0) -> dict:
    key = jax.random.key(seed)
    ks = jax.random.split(key, 20)

    def nrm(k, shape, scale):
        return jax.random.normal(k, shape, jnp.float32) * scale

    return {
        'x': nrm(ks[0], (BATCH, SEQ, D_MODEL), 1.0),
        'p': nrm(ks[1], (DEPTH, BATCH, SEQ, PLE_DIM), 1.0),
        'norm_g': 1.0 + nrm(ks[2], (DEPTH, 4, D_MODEL), 0.05),
        'ffn1_wi': nrm(ks[3], (DEPTH, D_MODEL, 2 * D_FF), D_MODEL ** -0.5),
        'ffn1_wo': nrm(ks[4], (DEPTH, D_FF, D_MODEL), D_FF ** -0.5),
        'w_in': nrm(ks[5], (DEPTH, D_MODEL, D_IN_2), D_MODEL ** -0.5),
        'diff_lambda': nrm(ks[6], (DEPTH, 4, A_HEAD_DIM), 0.1),
        'diff_subln': 1.0 + nrm(ks[7], (DEPTH, 2 * A_HEAD_DIM), 0.05),
        'nsa_cmp_pos': nrm(ks[8], (DEPTH, 2, B_CMP_LEN, B_HEAD_DIM), 0.1),
        'nsa_cmp_w1': nrm(ks[9], (DEPTH, 2, B_CMP_LEN * B_HEAD_DIM, B_CMP_HIDDEN), (B_CMP_LEN * B_HEAD_DIM) ** -0.5),
        'nsa_cmp_w2': nrm(ks[10], (DEPTH, 2, B_CMP_HIDDEN, B_HEAD_DIM), B_CMP_HIDDEN ** -0.5),
        'swa_sinks': nrm(ks[11], (DEPTH, C_HEADS), 0.5),
        'w_branch': nrm(ks[12], (DEPTH, 3, A_WIDTH, D_MODEL), A_WIDTH ** -0.5),
        'w_out': nrm(ks[13], (DEPTH, D_MODEL, D_MODEL), D_MODEL ** -0.5),
        'ffn2_wi': nrm(ks[14], (DEPTH, D_MODEL, 2 * D_FF), D_MODEL ** -0.5),
        'ffn2_wo': nrm(ks[15], (DEPTH, D_FF, D_MODEL), D_FF ** -0.5),
        'w_ple': nrm(ks[16], (DEPTH, PLE_DIM, D_MODEL), PLE_DIM ** -0.5),
        'w_ple_gate': nrm(ks[17], (DEPTH, D_MODEL, D_MODEL), D_MODEL ** -0.5),
        'rel_bias': nrm(ks[18], (NUM_BUCKETS, N_BIAS_HEADS), 0.5),
        'final_norm': 1.0 + nrm(ks[19], (D_MODEL,), 0.05),
    }

def second_block(x, p, norm_g, ffn1_wi, ffn1_wo, w_in, diff_lambda, diff_subln, nsa_cmp_pos,
              nsa_cmp_w1, nsa_cmp_w2, swa_sinks, w_branch, w_out, ffn2_wi, ffn2_wo,
              w_ple, w_ple_gate, rel_bias, final_norm):
    bsz, seq, _ = x.shape
    bias_a = rel_bias[:, :A_HEADS]
    bias_b = rel_bias[:, A_HEADS:A_HEADS + B_HEADS]
    bias_c = rel_bias[:, A_HEADS + B_HEADS:]
    h = x
    for i in range(DEPTH):
        h = h + 0.5 * swiglu_2(rms_norm(h, norm_g[i, 0]), ffn1_wi[i], ffn1_wo[i])
        n = rms_norm(h, norm_g[i, 1])
        (aq, ak, av, bq, bkc, bvc, bks, bvs, bkw, bvw, bgate,
         cq, ck, cv, ga, gb, gc) = split_cols(n @ w_in[i], IN_SPLITS_2)
        lam_init = 0.8 - 0.6 * math.exp(-0.3 * i)
        lp = diff_lambda[i].astype(jnp.float32)
        lam = jnp.exp(jnp.sum(lp[0] * lp[1])) - jnp.exp(jnp.sum(lp[2] * lp[3])) + lam_init
        ya = diff_attention(aq.reshape(bsz, seq, A_HEADS, 2, A_HEAD_DIM),
                            ak.reshape(bsz, seq, A_HEADS, 2, A_HEAD_DIM),
                            av.reshape(bsz, seq, A_HEADS, 2 * A_HEAD_DIM),
                            bias_a, lam, lam_init, diff_subln[i])
        kvb = lambda t: t.reshape(bsz, seq, B_GROUPS, B_HEAD_DIM)
        yb = nsa_attention(bq.reshape(bsz, seq, B_GROUPS, B_REP, B_HEAD_DIM),
                           kvb(bkc), kvb(bvc), kvb(bks), kvb(bvs), kvb(bkw), kvb(bvw),
                           jax.nn.sigmoid(bgate.reshape(bsz, seq, B_GROUPS, B_REP, 3)),
                           bias_b, nsa_cmp_pos[i], nsa_cmp_w1[i], nsa_cmp_w2[i])
        yc = swa_sink_attention(cq.reshape(bsz, seq, C_GROUPS, C_REP, C_HEAD_DIM),
                                ck.reshape(bsz, seq, C_GROUPS, C_HEAD_DIM),
                                cv.reshape(bsz, seq, C_GROUPS, C_HEAD_DIM),
                                bias_c, swa_sinks[i])
        merged = (jax.nn.sigmoid(ga) * (ya @ w_branch[i, 0])
                  + jax.nn.sigmoid(gb) * (yb @ w_branch[i, 1])
                  + jax.nn.sigmoid(gc) * (yc @ w_branch[i, 2]))
        h = h + merged @ w_out[i]
        h = h + 0.5 * swiglu_2(rms_norm(h, norm_g[i, 2]), ffn2_wi[i], ffn2_wo[i])
        h = h + jax.nn.sigmoid(rms_norm(h, norm_g[i, 3]) @ w_ple_gate[i]) * (p[i] @ w_ple[i])
    return rms_norm(h, final_norm)


def setup_inputs(seed=0):
    out = dict(first_inputs(seed))
    for name, value in second_inputs(seed + 1).items():
        if name != "x":
            out[name + "_2"] = value
    return out


def reference(
    x, mem, positions, ffn1_norm, w_ffn1_in, w_ffn1_out, mix_norm, w_in, q_lat_norm,
    kv_lat_norm, w_uq, w_uk, w_uv, w_o_mla, hg_lower_bounds, hg_out_norm, w_o_hg, mem_norm,
    w_mem_kv, w_o_mem, w_out, ffn2_norm, w_ffn2_in, w_ffn2_out, final_norm, p_2, norm_g_2,
    ffn1_wi_2, ffn1_wo_2, w_in_2, diff_lambda_2, diff_subln_2, nsa_cmp_pos_2, nsa_cmp_w1_2,
    nsa_cmp_w2_2, swa_sinks_2, w_branch_2, w_out_2, ffn2_wi_2, ffn2_wo_2, w_ple_2, w_ple_gate_2,
    rel_bias_2, final_norm_2,
):
    x = first_block(
        x, mem, positions, ffn1_norm, w_ffn1_in, w_ffn1_out, mix_norm, w_in, q_lat_norm,
        kv_lat_norm, w_uq, w_uk, w_uv, w_o_mla, hg_lower_bounds, hg_out_norm, w_o_hg, mem_norm,
        w_mem_kv, w_o_mem, w_out, ffn2_norm, w_ffn2_in, w_ffn2_out, final_norm,
    )
    return second_block(
        x, p_2, norm_g_2, ffn1_wi_2, ffn1_wo_2, w_in_2, diff_lambda_2, diff_subln_2,
        nsa_cmp_pos_2, nsa_cmp_w1_2, nsa_cmp_w2_2, swa_sinks_2, w_branch_2, w_out_2, ffn2_wi_2,
        ffn2_wo_2, w_ple_2, w_ple_gate_2, rel_bias_2, final_norm_2,
    )


_drawn_inputs = setup_inputs


def setup_inputs(seed=0):
    import zlib

    import numpy as np

    out = dict(_drawn_inputs(seed))
    spreads = {}
    factors = {'ffn1_norm': 4.054,
     'mix_norm': 3.247,
     'q_lat_norm': 8.0,
     'kv_lat_norm': 8.0,
     'hg_out_norm': 6.089,
     'mem_norm': 8.0,
     'ffn2_norm': 4.488,
     'diff_subln_2': 2.749,
     'nsa_cmp_pos_2': 2.927,
     'swa_sinks_2': 8.0}
    for name, (base, spread) in spreads.items():
        noise = np.random.default_rng([zlib.crc32(name.encode()), seed]).standard_normal(out[name].shape)
        drawn = base * np.exp(spread * noise) if base else spread * noise
        out[name] = jnp.asarray(drawn.astype(out[name].dtype))
    for name, factor in factors.items():
        out[name] = (out[name] * factor).astype(out[name].dtype)
    return out
```

```python
import numpy as np
import concourse.bass as bass
from concourse import mybir
from concourse.alu_op_type import AluOpType as ALU
from contextlib import ExitStack

FP = mybir.dt.float32
I32 = mybir.dt.int32
ACT = mybir.ActivationFunctionType
AX = mybir.AxisListType

P = 128
T = 256
NT = T // P
D = 1024
DK = D // P
FF = 2816
FK = FF // P
DEPTH = 2
EPS = 1e-6
NEG = -1e30

MLA_H, NOPE, ROPE = 8, 64, 32
QK = NOPE + ROPE
Q_LORA, KV_LORA = 384, 256
HG_H, CHUNK = 4, 64
MEM_H = 4
LEVELS = 8
A_H = 4
N_CMP, CMP_STRIDE, CMP_LEN = 15, 16, 32
BUCKETS, BIAS_H = 32, 20

LAM_INIT = [0.8 - 0.6 * float(np.exp(-0.3 * l)) for l in range(DEPTH)]
TURN = (6.28125, 0.001934051513671875, 2.0 * float(np.pi) - 6.28125 - 0.001934051513671875)
NORMED_1 = DEPTH * (4 * DK + 3 + 2 + 1) + DK

BANKS = 8
SLOTS = 4
SLOT = 2048

C_Q, C_KV, C_KR, C_HQ, C_HF, C_HI, C_HG, C_MQ, C_GATE = 0, 384, 640, 672, 1184, 1696, 2208, 2720, 3232
(D_AQ, D_AK, D_AV, D_BQ, D_BKC, D_BVC, D_BKS, D_BVS, D_BKW, D_BVW, D_BG, D_CQ, D_CK, D_CV,
 D_GATE) = (0, 512, 1024, 1536, 2048, 2176, 2304, 2432, 2560, 2688, 2816, 2840, 3352, 3480, 3608)


def blocks(qt):
    return min(N_CMP, ((qt + 1) * P - CMP_LEN) // CMP_STRIDE + 1)


class Tally:

    def __init__(self):
        self.n = {}

    def add(self, name, k=1):
        before = self.n.get(name, 0)
        self.n[name] = before + k
        return before


def constants():
    parts, at, n = [], {}, 0

    def put(name, a):
        nonlocal n
        full = np.zeros((P, a.shape[1]), np.float32)
        full[:a.shape[0]] = a
        parts.append(full)
        at[name] = n
        n += a.shape[1]

    put("ident", np.eye(P, dtype=np.float32))
    put("ones", np.ones((P, P), np.float32))
    s, t = np.arange(P)[:, None], np.arange(P)[None, :]
    put("pair0", (s == t).astype(np.float32))
    for l in range(LEVELS - 1):
        put(f"pair{l + 1}", ((s >> (l + 1) == t >> (l + 1)) & (s >> l & 1 == 0) & (t >> l & 1 == 1)).astype(np.float32))
    j = np.arange(2 * P)[None, :]
    put("causal", np.where(s - j + P >= 0, 0.0, NEG).astype(np.float32))
    swap = np.zeros((P, ROPE), np.float32)
    for i in range(ROPE // 2):
        swap[64 + ROPE // 2 + i, i] = -1.0
        swap[64 + i, ROPE // 2 + i] = 1.0
    put("swap", swap)
    freq = np.zeros((P, 1), np.float32)
    inv = (np.float32(10000.0) ** (-np.arange(0, ROPE, 2, dtype=np.float32) / np.float32(ROPE))).astype(np.float32)
    freq[64:96, 0] = np.concatenate([inv, inv])
    put("freq", freq)
    i = np.arange(2 * T)
    d = 255 - i
    m = np.maximum(d, 0)
    half = BUCKETS // 2
    large = half + (np.log(np.maximum(m, 1).astype(np.float32) / np.float32(half)) / np.float32(np.log(P / half))
                    * np.float32(BUCKETS - half)).astype(np.int32)
    bucket = np.where(m < half, m, np.minimum(large, BUCKETS - 1))
    hot = np.zeros((BUCKETS + 2, 2 * T), np.float32)
    hot[bucket, i] = 1.0
    hot[BUCKETS] = np.where(d < 0, NEG, 0.0)
    hot[BUCKETS + 1] = np.where((d >= P), NEG, 0.0)
    put("hot", hot)
    rows = np.zeros((2, BIAS_H), np.float32)
    rows[0] = 1.0
    rows[1, 12:] = 1.0
    mask_rows = np.zeros((P, BIAS_H), np.float32)
    mask_rows[BUCKETS:BUCKETS + 2] = rows
    put("mask_rows", mask_rows)
    put("sees", (np.arange(P) >= CMP_LEN - 1).astype(np.float32)[:, None])
    return np.concatenate(parts, axis=1), at


def constant_places():
    return constants()[1]


VECS = {}


def pack_vectors(v):
    parts, n = [], 0

    def put(name, a):
        nonlocal n
        a = np.asarray(a, np.float32)
        full = np.zeros((P, a.shape[1]), np.float32)
        full[:a.shape[0]] = a
        parts.append(full)
        VECS[name] = n
        n += a.shape[1]

    def cols(a):
        return np.asarray(a).reshape(-1, P).T

    for l in range(DEPTH):
        for name in ("ffn1_norm", "mix_norm", "q_lat_norm", "kv_lat_norm", "hg_out_norm", "mem_norm", "ffn2_norm"):
            put(f"{name}{l}", cols(v[name][l]))
        for k in range(4):
            put(f"norm_g{l}{k}", cols(v["norm_g_2"][l, k]))
        put(f"subln{l}", cols(v["diff_subln_2"][l]))
        put(f"lambda{l}", np.broadcast_to(np.asarray(v["diff_lambda_2"][l]).reshape(1, 256), (P, 256)))
        put(f"sinks{l}", np.broadcast_to(np.asarray(v["swa_sinks_2"][l]).reshape(1, 2, 4).transpose(0, 2, 1).reshape(1, 8), (P, 8)))
        for kv in range(2):
            put(f"pos{l}{kv}", np.asarray(v["nsa_cmp_pos_2"][l, kv]).reshape(16, P).T)
        put(f"lb{l}", cols(v["hg_lower_bounds"][l]))
    put("rel_bias", np.asarray(v["rel_bias_2"]))
    put("final1", cols(v["final_norm"]))
    put("final2", cols(v["final_norm_2"]))
    return np.concatenate(parts, axis=1)


class Plan:

    def __init__(self):
        self.first = {}
        self.total = 0
        self.slab_first = {}
        self.slab_last = []
        self.slab_in = []

    def products(self, name, n):
        self.first[name] = self.total
        self.total += n

    def slabs(self, name, per_slab, dmas=1):
        if name not in self.first:
            self.products(name, 0)
            self.slab_first[name] = len(self.slab_last)
        for n in per_slab:
            self.total += n
            before = self.slab_in[-SLOTS] if len(self.slab_in) >= SLOTS else 0
            self.slab_in.append(before + 16 * dmas)
            self.slab_last.append(self.total - 1 if n else self.total)


WIN1 = ([(C_Q, 256, 2), (C_Q + 256, 128, 1), (C_KV, 256, 2), (C_KR, 32, 1)]
        + [(c + 256 * i, 256, 2) for c in (C_HQ, C_HF, C_HI, C_HG, C_MQ) for i in range(2)]
        + [(C_GATE + 256 * i, 256, 2) for i in range(12)])
WIN2 = ([("tiles", c + 256 * i, 256, 2) for c in (D_AQ, D_AK) for i in range(2)]
        + [("tokens", D_AV + 256 * i, 256, 2) for i in range(2)]
        + [("pairs", D_BQ + 128 * i, 256, 2) for i in range(2)]
        + [("shift", D_BKC, 256, 2), ("kv", D_BKS, 256, 2), ("kv", D_BKW, 256, 2), ("gate", D_BG, 24, 1)]
        + [("pairs", D_CQ + 128 * i, 256, 2) for i in range(2)]
        + [("kv", D_CK, 256, 2)]
        + [("tiles", D_GATE + 256 * i, 256, 2) for i in range(12)])
ATTN = {"mla": (8, 1, 1, 1), "mem": (4, 1, 1, 1), "A": (8, 2, 1, 1), "B": (8, 6, 3, 3), "C": (8, 2, 1, 1)}


def attention_numbers(first, units, n_s, n_t):
    s, t, o, n = [0] * units, [0] * units, [0] * units, first
    for i in range(-2, units):
        if i >= 0:
            t[i] = n
            n += n_t
        if i + 2 < units:
            s[i + 2] = n
            n += n_s
        if i >= 0:
            o[i] = n
            n += 1
    return s, t, o, n - first


def make_plan():
    pl = Plan()

    def ffn(name):
        pl.products(name + ".norm", 1)
        pl.slabs(name + ".in", [2] * FK, dmas=2)
        pl.slabs(name + ".out", [0, 1] * DK)

    def attention(name, kind):
        units, n_s, n_t, _ = ATTN[kind]
        pl.products(name, attention_numbers(0, units, n_s, n_t)[3])

    for l in range(DEPTH):
        L = f"1.{l}."
        ffn(L + "ffn1")
        pl.products(L + "mix.norm", 1)
        pl.slabs(L + "win", [n for _, _, n in WIN1])
        pl.products(L + "q.norm", 1)
        pl.products(L + "kv.norm", 1)
        pl.slabs(L + "uq", [4, 4])
        pl.slabs(L + "uk", [8])
        pl.slabs(L + "uv", [2])
        pl.products(L + "swap", 5)
        attention(L + "mla", "mla")
        pl.slabs(L + "mla.out", [4, 4])
        pl.products(L + "pairs", 2 * LEVELS + 1)
        pl.products(L + "hg.o", 2)
        pl.products(L + "hg.norm", 2)
        pl.slabs(L + "hg.out", [4, 4])
        pl.products(L + "mem.norm", 1)
        pl.slabs(L + "mem.kv", [2] * 4)
        attention(L + "mem", "mem")
        pl.slabs(L + "mem.out", [4, 4])
        pl.slabs(L + "wout", [2] * 4)
        ffn(L + "ffn2")
    pl.products("1.final.norm", 1)
    pl.products("bias", 1)
    for l in range(DEPTH):
        L = f"2.{l}."
        ffn(L + "ffn1")
        pl.products(L + "mix.norm", 1)
        for (kind, _, _, n) in WIN2:
            pl.slabs(L + "win", [n], dmas=2 if kind == "pairs" else 1)
        pl.slabs(L + "cmp", [0, 1, 0, 1])
        pl.slabs(L + "cmp", [2], dmas=2)
        attention(L + "A", "A")
        pl.products(L + "A.norm", 2)
        pl.slabs(L + "A.out", [4, 4])
        attention(L + "B", "B")
        pl.slabs(L + "B.out", [4, 4], dmas=2)
        attention(L + "C", "C")
        pl.slabs(L + "C.out", [4, 4], dmas=2)
        pl.slabs(L + "wout", [2] * 4)
        ffn(L + "ffn2")
        pl.products(L + "ple.norm", 1)
        pl.slabs(L + "ple.p", [8])
        pl.slabs(L + "ple.gate", [2] * 4)
    pl.products("2.final.norm", 1)
    return pl


def build(nc, w, vec_places, out, scratch_rows):
    pl = make_plan()
    first, slab_first = pl.first, pl.slab_first
    cst = constant_places()
    n_cst, n_vec = w["cst"].shape[1], w["vec"].shape[1]
    block1 = [f"1.{l}." for l in range(DEPTH)]
    block2 = [f"2.{l}." for l in range(DEPTH)]

    ctx = ExitStack()
    with ctx:
        def sb(name, shape, dt=FP):
            return ctx.enter_context(nc.sbuf_tensor(name, shape, dt))

        def sem(name):
            return ctx.enter_context(nc.semaphore(name))

        cst_sb = sb("cst_sb", [P, n_cst])
        vec_sb = sb("vec_sb", [P, n_vec])
        X = sb("X", [P, DK, T])
        U = sb("U", [P, DK, T])
        SQ = sb("SQ", [P, DK, T])
        RING = sb("RING", [P, SLOTS, SLOT])
        V = sb("V", [P, T])
        RSTD = sb("RSTD", [P, T])
        COS = sb("COS", [P, T])
        SIN = sb("SIN", [P, T])
        SILU = sb("SILU", [P, 2, T])
        TMP = sb("TMP", [P, 2, 512])
        LB = sb("LB", [P, 6, HG_H])
        LAM = sb("LAM", [P, 6, DEPTH])
        TAB = sb("TAB", [P, BIAS_H])
        MX = sb("MX", [P, 2, 3, 2])
        SUM = sb("SUM", [P, 2, 3, 2])
        REGION = sb("REGION", [P, 31600])
        used = [0]

        def region(*shape):
            n = int(np.prod(shape))
            a = REGION[:, used[0]:used[0] + n]
            used[0] += n
            assert used[0] <= 31600, used[0]
            if len(shape) == 2:
                return a.rearrange("p (a b) -> p a b", b=shape[1])
            if len(shape) == 3:
                return a.rearrange("p (a b c) -> p a b c", b=shape[1], c=shape[2])
            if len(shape) == 4:
                return a.rearrange("p (a b c d) -> p a b c d", b=shape[1], c=shape[2], d=shape[3])
            return a

        H = region(FK, T)
        used[0] = 0
        GATE = region(3 * DK, T)
        MRG = region(DK, T)
        OT = region(4, T)
        PT = region(3, 2, 512)
        S = region(3, 2, 2, 260)
        both = used[0]
        used[0] = both - 3 * 2 * 2 * 260 - 2 * 2 * 512
        MK, MV = region(4, T), region(NT, 512)
        used[0] = both - 2 * 2 * 2 * 260
        Z, HK = region(HG_H * T), region(HG_H * T)
        used[0] = both
        CQ, CKV = region(3, T), region(2, T)
        QH, KH = region(MLA_H, T), region(MLA_H, T)
        VM = region(NT, 512)
        MQ = region(4, T)
        HQ, HGT, VH = region(HG_H, T), region(HG_H, T), region(NT, 512)
        GS = region(HG_H * T)
        HX = region(2, HG_H * T)
        AT = region(HG_H, 3, P)
        KR = SILU
        used[0] = both
        AQ, AK, AV = region(4, T), region(4, T), region(NT, 512)
        BQ, CQ2 = region(4, T), region(4, T)
        KC2, VC2 = region(2, T), region(2, T)
        BKS, BKW, CK2 = region(T), region(T), region(T)
        BVS, BVW, CV2 = region(NT, P), region(NT, P), region(NT, P)
        BG = region(NT, 24)
        BLK = region(16, 30)
        GX, GY, HID, HID2 = region(2, 30), region(2, 30), region(2, 30), region(2, 30)
        BLK2 = region(16, 30)
        KCMP, VCMP = region(16), region(2, 64)
        WIN = region(BIAS_H, T)
        PLE = GATE[:, 0:DK]
        PIN = region(2, T)

        ps = ctx.enter_context(nc.psum_tensor("ps", [P, BANKS, 512], FP))
        RESET = sb("RESET", [P, HG_H * T])
        ROWS = sb("ROWS", [P, 512])

        product_done = sem("product_done")
        evicted = [sem(f"evicted{b}") for b in range(BANKS)]
        weights_in = [sem(f"weights_in{i}") for i in range(SLOTS)]
        inputs_in = sem("inputs_in")
        mem_in = sem("mem_in")
        layer_in = sem("layer_in")
        windows_in = sem("windows_in")
        scratch_out = sem("scratch_out")
        result_out = sem("result_out")
        setup_done = sem("setup_done")
        angle_ready = sem("angle_ready")
        rope_ready = sem("rope_ready")
        lambda_ready = sem("lambda_ready")
        squares_ready = sem("squares_ready")
        mean_ready = sem("mean_ready")
        rstd_ready = sem("rstd_ready")
        normed = sem("normed")
        hidden_ready = sem("hidden_ready")
        max_ready = sem("max_ready")
        exp_done = sem("exp_done")
        probs_ready = sem("probs_ready")
        merged_ready = sem("merged_ready")
        roped = sem("roped")
        hg_vec = sem("hg_vec")
        hg_act = sem("hg_act")
        pair_ready = sem("pair_ready")
        pairs_summed = sem("pairs_summed")
        result_ready = sem("result_ready")
        blocks_ready = sem("blocks_ready")
        gelu_vec = sem("gelu_vec")
        gelu_act = sem("gelu_act")
        vec_step = sem("vec_step")
        act_step = sem("act_step")

        block = ctx.enter_context(nc.Block())

        def con(name, n, rows=slice(0, P)):
            return cst_sb[rows, cst[name]:cst[name] + n]

        def vec(name, n, rows=slice(0, P)):
            return vec_sb[rows, vec_places[name]:vec_places[name] + n]

        def bank(n, *cols):
            return ps[:, n % BANKS, :] if not cols else ps[:, n % BANKS, cols[0]:cols[1]]

        def wait_product(eng, n, r=0):
            eng.wait_ge(product_done, r * BANKS + n + 1)

        def wait_evicted(eng, n, r=0):
            eng.wait_ge(evicted[n % BANKS], r + n // BANKS + 1)

        def wait_room(eng, n, r=0):
            if n >= BANKS or not isinstance(r, int):
                eng.wait_ge(evicted[n % BANKS], r + n // BANKS)

        def wait_weights(eng, s, r=0):
            eng.wait_ge(weights_in[s % SLOTS], r * 32 + pl.slab_in[s])

        def slot(s, kt, width):
            return RING[:, s % SLOTS, 0:kt * width].rearrange("p (k n) -> p k n", n=width)

        def rounds(eng, n, body):
            for j in range(SLOTS):
                body(0, j)
            with eng.Fori(1, n // SLOTS) as r:
                for j in range(SLOTS):
                    body(r, j)
            for j in range(n // SLOTS * SLOTS, n):
                body(0, j)

        def wide(a, shape):
            return a.broadcast_to(shape)

        @block.sync
        def _(sp):
            sp.dma_start(cst_sb[:], w["cst"]).then_inc(inputs_in, 16)
            sp.dma_start(vec_sb[:], w["vec"]).then_inc(inputs_in, 16)
            sp.dma_start(X[:], w["xT"].rearrange("(k p) t -> p k t", p=P)).then_inc(inputs_in, 16)
            sp.dma_start(COS[64:96, :].bitcast(I32), w["pos"]).then_inc(inputs_in, 16)

            def room(s, r=0):
                if s >= SLOTS:
                    sp.wait_ge(product_done, r * BANKS + pl.slab_last[s - SLOTS] + 1)

            def load(s, *pairs):
                room(s)
                for dst, src in pairs:
                    sp.dma_start(dst, src).then_inc(weights_in[s % SLOTS], 16)

            def rows(a):
                return a.rearrange("(k p) n -> p k n", p=P)

            def ffn(name, wi, wo):
                s0, p0 = slab_first[name + ".in"], first[name + ".in"]

                def pair(r, j):
                    s = s0 + j
                    if isinstance(r, int):
                        room(s)
                    else:
                        sp.wait_ge(product_done, r * BANKS + p0 + 2 * (j - SLOTS) + 2)
                    dst = slot(s, DK, 256)
                    for side in range(2):
                        sp.dma_start(dst[:, :, side * P:(side + 1) * P],
                                     rows(wi[:, bass.ds(r * (SLOTS * P) + (j * P + side * FF), P)]))\
                          .then_inc(weights_in[s % SLOTS], 16)

                rounds(sp, FK, pair)
                for i in range(2 * DK):
                    m, half = i // 2, i % 2
                    k0 = half * (FK // 2)
                    load(slab_first[name + ".out"] + i,
                         (slot(slab_first[name + ".out"] + i, FK // 2, P),
                          rows(wo[k0 * P:(k0 + FK // 2) * P, m * P:(m + 1) * P])))

            def halves(name, a, kt):
                n = a.shape[1] // 2
                for i in range(2):
                    s = slab_first[name] + i
                    load(s, (slot(s, kt, n), rows(a[:, i * n:(i + 1) * n])))

            def quarters(name, a):
                for i in range(4):
                    s = slab_first[name] + i
                    load(s, (slot(s, DK, 256), rows(a[:, i * 256:(i + 1) * 256])))

            for l, L in enumerate(block1):
                ffn(L + "ffn1", w["w_ffn1_in"][l], w["w_ffn1_out"][l])
                for i, (c, n, _) in enumerate(WIN1):
                    s = slab_first[L + "win"] + i
                    load(s, (slot(s, DK, n), rows(w["w_in"][l][:, c:c + n])))
                halves(L + "uq", w["w_uq"][l], 3)
                s = slab_first[L + "uk"]
                load(s, (slot(s, 2, 512), rows(w["w_uk"][l])))
                s = slab_first[L + "uv"]
                load(s, (slot(s, 2, 512), rows(w["w_uv"][l])))
                halves(L + "mla.out", w["w_o_mla"][l], 4)
                halves(L + "hg.out", w["w_o_hg"][l], 4)
                quarters(L + "mem.kv", w["w_mem_kv"][l])
                halves(L + "mem.out", w["w_o_mem"][l], 4)
                quarters(L + "wout", w["w_out"][l])
                ffn(L + "ffn2", w["w_ffn2_in"][l], w["w_ffn2_out"][l])
            for l, L in enumerate(block2):
                ffn(L + "ffn1", w["ffn1_wi_2"][l], w["ffn1_wo_2"][l])
                wi = w["w_in_2"][l]
                for i, (kind, c, n, _) in enumerate(WIN2):
                    s = slab_first[L + "win"] + i
                    dst = slot(s, DK, n)
                    if kind == "pairs":
                        d4 = dst.rearrange("p k (g n) -> p k g n", g=2)
                        load(s, *[(d4[:, :, g, :], rows(wi[:, c + 256 * g:c + 256 * g + P])) for g in range(2)])
                    else:
                        load(s, (dst, rows(wi[:, c:c + n])))
                for i in range(4):
                    s = slab_first[L + "cmp"] + i
                    load(s, (slot(s, DK, 256), rows(w["nsa_cmp_w1_2"][l, i // 2][i % 2 * D:(i % 2 + 1) * D, :])))
                s = slab_first[L + "cmp"] + 4
                w2 = slot(s, 4, 64)
                load(s, *[(w2[:, 2 * kv:2 * kv + 2, :], rows(w["nsa_cmp_w2_2"][l, kv])) for kv in range(2)])
                halves(L + "A.out", w["w_branch_2"][l, 0], 4)
                for b, name in ((1, "B.out"), (2, "C.out")):
                    for i in range(2):
                        s = slab_first[L + name] + i
                        dst = slot(s, 4, 512)
                        src = w["w_branch_2"][l, b][:, i * 512:(i + 1) * 512].rearrange("(g j d) n -> g d j n", g=2, j=4)
                        load(s, *[(dst[64 * g:64 * g + 64], src[g]) for g in range(2)])
                quarters(L + "wout", w["w_out_2"][l])
                ffn(L + "ffn2", w["ffn2_wi_2"][l], w["ffn2_wo_2"][l])
                s = slab_first[L + "ple.p"]
                load(s, (slot(s, 2, D), rows(w["w_ple_2"][l])))
                quarters(L + "ple.gate", w["w_ple_gate_2"][l])
            sp.wait_ge(result_ready, DK)
            sp.dma_start(out.rearrange("(k p) t -> p k t", p=P), U[:]).then_inc(result_out, 16)
            sp.wait_ge(result_out, 16)

        @block.gpsimd
        def _(pool):
            for l, L in enumerate(block1):
                wait_product(pool, first[L + "pairs"] + 2 * LEVELS)
                pool.dma_start(HX, w["memT"].rearrange("(k p) t -> p k t", p=P)).then_inc(mem_in, 16)
            wait_evicted(pool, first["bias"])
            pool.dma_start(scratch_rows.rearrange("r h i -> h r i"),
                           ROWS[0:BIAS_H, :].unsqueeze(1).broadcast_to([BIAS_H, P, 2 * T])).then_inc(scratch_out, 16)
            pool.wait_ge(scratch_out, 16)
            wait_product(pool, first["1.final.norm"])
            wins = bass.AP(tensor=scratch_rows.tensor, offset=P - 1, ap=[[BIAS_H * 2 * T - 1, P], [2 * T, BIAS_H], [1, T]])
            for l, L in enumerate(block2):
                wait_product(pool, first[L + "mix.norm"])
                if l == 0:
                    pool.dma_start(WIN, wins).then_inc(windows_in, 16)
                wait_product(pool, first[L + "ple.norm"])
                pool.dma_start(PIN, w["pT"][l].rearrange("(k p) t -> p k t", p=P)).then_inc(layer_in, 16)

        @block.tensor
        def _(pe):
            tally = Tally()
            ones = con("ones", P)
            ident = con("ident", P)

            def product(n, groups, after=None):
                wait_room(pe, n)
                for o, terms in groups:
                    for i, (a, b) in enumerate(terms):
                        last = nc.tensor.matmul(o, a, b, start=i == 0, stop=i == len(terms) - 1)
                last.then_inc(product_done, 1)

            def norm(n, kt, tiles, width=T):
                pe.wait_ge(squares_ready, tally.add("squares_ready") + 1)
                tally.add("normed", tiles)
                product(n, [(bank(n, 0, width), [(ones, SQ[:, k, :]) for k in range(kt)])])

            def ffn(name):
                norm(first[name + ".norm"], DK, DK)
                ready = tally.n["normed"] - DK
                s0, p0 = slab_first[name + ".in"], first[name + ".in"]

                def pair(r, j):
                    wait_weights(pe, s0 + j, r)
                    wv = slot(s0 + j, DK, 256)
                    for side in range(2):
                        n = p0 + 2 * j + side
                        wait_room(pe, n, r)
                        for k in range(DK):
                            if isinstance(r, int) and j == 0 and side == 0:
                                pe.wait_ge(normed, ready + k + 1)
                            last = nc.tensor.matmul(bank(n, 0, T), wv[:, k, side * P:(side + 1) * P], U[:, k, :],
                                                    start=k == 0, stop=k == DK - 1)
                        last.then_inc(product_done, 1)

                rounds(pe, FK, pair)
                for m in range(DK):
                    n = first[name + ".out"] + m
                    wait_room(pe, n)
                    for k in range(FK):
                        s = slab_first[name + ".out"] + 2 * m + k // (FK // 2)
                        if k % (FK // 2) == 0:
                            wait_weights(pe, s)
                        if m == 0:
                            wait_evicted(pe, p0 + 2 * k + 1)
                        last = nc.tensor.matmul(bank(n, 0, T), slot(s, FK // 2, P)[:, k % (FK // 2), :], H[:, k, :],
                                                start=k == 0, stop=k == FK - 1)
                    last.then_inc(product_done, 1)

            def halves(name, kt, act, waits):
                for n in waits:
                    wait_evicted(pe, n)
                for i in range(2):
                    s = slab_first[name] + i
                    wait_weights(pe, s)
                    for m in range(4):
                        n = first[name] + 4 * i + m
                        product(n, [(bank(n, 0, T),
                                     [(slot(s, kt, 512)[:, k, m * P:(m + 1) * P], act[:, k, :]) for k in range(kt)])])

            def quarters(name, act):
                for i in range(4):
                    s = slab_first[name] + i
                    wait_weights(pe, s)
                    for m in range(2):
                        n = first[name] + 2 * i + m
                        product(n, [(bank(n, 0, T),
                                     [(slot(s, DK, 256)[:, k, m * P:(m + 1) * P], act[:, k, :]) for k in range(DK)])])

            def tokens(n, parts, act, kt):
                product(n, [(o, [(act[:, k, tt * P:(tt + 1) * P], wk(k)) for k in range(kt)]) for o, wk, tt in parts])

            def attention(name, kind, scores, values):
                units, n_s, n_t, n_b = ATTN[kind]
                s, t, o, _ = attention_numbers(first[name], units, n_s, n_t)
                base = tally.add("probs_ready", units)
                for i in range(-2, units):
                    if i >= 0:
                        pe.wait_ge(probs_ready, base + i + 1)
                        qt, par = i % 2, i % 2
                        for b in range(n_t):
                            groups = 1 if kind == "A" else 2
                            cmp = kind == "B" and b == 0
                            keys = [(0, blocks(qt))] if cmp else [(k * P, P) for k in range(NT if kind == "mem" else qt + 1)]
                            gr = []
                            for g in range(groups):
                                for k, (k0, kn) in enumerate(keys):
                                    c = (g * len(keys) + k) * P
                                    gr.append((S[:, b, par, g, k0:k0 + kn], bank(t[i] + b)[0:kn, c:c + P]))
                            wait_room(pe, t[i] + b)
                            for src, dst in gr:
                                last = nc.tensor.transpose(dst, src, ident)
                            last.then_inc(product_done, 1)
                    if i + 2 < units:
                        for b, groups in enumerate(scores(i + 2)):
                            if n_s == n_b:
                                n = s[i + 2] + b
                                product(n, [(bank(n)[:, g * T:g * T + k.shape[-1]], [(q, k)]) for g, (q, k) in enumerate(groups)])
                            else:
                                for g, (q, k) in enumerate(groups):
                                    n = s[i + 2] + 2 * b + g
                                    product(n, [(bank(n, 0, k.shape[-1]), [(q, k)])])
                    if i >= 0:
                        for b in range(n_t):
                            wait_evicted(pe, t[i] + b)
                        wait_room(pe, o[i])
                        for rows, c, terms in values(i):
                            for j, (v, b, c0, kn) in enumerate(terms):
                                last = nc.tensor.matmul(bank(o[i])[rows, c:c + P], v, PT[0:kn, b, par, c0:c0 + P],
                                                        start=j == 0, stop=j == len(terms) - 1)
                        last.then_inc(product_done, 1)

            pe.wait_ge(inputs_in, 64)
            for l, L in enumerate(block1):
                ffn(L + "ffn1")
                norm(first[L + "mix.norm"], DK, DK)
                pe.wait_ge(normed, tally.n["normed"])
                n = first[L + "win"]
                for i, (c, width, count) in enumerate(WIN1):
                    s = slab_first[L + "win"] + i
                    wait_weights(pe, s)
                    wv = slot(s, DK, width)
                    for m in range(count):
                        if C_HI <= c < C_HG:
                            tokens(n, [(bank(n, 0, 256), lambda k: wv[:, k, :], m)], U, DK)
                        elif c == C_KR:
                            product(n, [(bank(n)[64:96, 0:T], [(wv[:, k, :], U[:, k, :]) for k in range(DK)])])
                        else:
                            product(n, [(bank(n, 0, T), [(wv[:, k, m * P:(m + 1) * P], U[:, k, :]) for k in range(DK)])])
                        n += 1
                norm(first[L + "q.norm"], 3, 3)
                norm(first[L + "kv.norm"], 2, 2)
                pe.wait_ge(normed, tally.n["normed"] - 2)
                for i in range(2):
                    s = slab_first[L + "uq"] + i
                    wait_weights(pe, s)
                    for m in range(4):
                        n = first[L + "uq"] + 4 * i + m
                        product(n, [(bank(n)[0:QK, 0:T], [(slot(s, 3, 384)[:, k, m * QK:(m + 1) * QK], CQ[:, k, :]) for k in range(3)])])
                pe.wait_ge(normed, tally.n["normed"])
                s = slab_first[L + "uk"]
                wait_weights(pe, s)
                for m in range(MLA_H):
                    n = first[L + "uk"] + m
                    product(n, [(bank(n)[0:NOPE, 0:T], [(slot(s, 2, 512)[:, k, m * NOPE:(m + 1) * NOPE], CKV[:, k, :]) for k in range(2)])])
                s = slab_first[L + "uv"]
                wait_weights(pe, s)
                for m in range(NT):
                    tokens(first[L + "uv"] + m, [(bank(first[L + "uv"] + m), lambda k: slot(s, 2, 512)[:, k, :], m)], CKV, 2)
                swap = con("swap", ROPE, slice(64, 96))
                for h in range(MLA_H):
                    wait_evicted(pe, first[L + "uq"] + h)
                for m in range(4):
                    n = first[L + "swap"] + m
                    product(n, [(bank(n)[64:96, :], [(swap, QH[64:96, 2 * m:2 * m + 2, :])])])
                n = first[L + "swap"] + 4
                product(n, [(bank(n)[64:96, 0:T], [(swap, KR[64:96, 0, :])])])
                pe.wait_ge(roped, l + 1)
                for m in range(MLA_H):
                    wait_evicted(pe, first[L + "uk"] + m)
                for m in range(NT):
                    wait_evicted(pe, first[L + "uv"] + m)
                attention(L + "mla", "mla",
                          lambda i: [[(QH[0:QK, h, i % 2 * P:(i % 2 + 1) * P], KH[0:QK, h, 0:(i % 2 + 1) * P])
                                      for h in (i // 2 * 2, i // 2 * 2 + 1)]],
                          lambda i: [(slice(64 * g, 64 * g + 64), 0,
                                      [(VM[:, k, (i // 2 * 2 + g) * 64:(i // 2 * 2 + g + 1) * 64], 0, (g * (i % 2 + 1) + k) * P, P)
                                       for k in range(i % 2 + 1)]) for g in range(2)])
                mla_o = attention_numbers(first[L + "mla"], *ATTN["mla"][:3])[2]
                halves(L + "mla.out", 4, OT, mla_o)
                n = first[L + "pairs"]
                pe.wait_ge(pair_ready, l * (LEVELS + 1) + 1)
                for level in range(LEVELS + 1):
                    pe.wait_ge(pair_ready, l * (LEVELS + 1) + level + 1)
                    if level == 0:
                        left, right = HK.rearrange("p (h t) -> p h t", t=T), HQ
                    else:
                        left = right = HX[:, (level - 1) % 2, :].rearrange("p (h t) -> p h t", t=T)
                    for tt in ((0, 1) if level < LEVELS else (0,)):
                        q = slice(tt * P, tt * P + P) if level < LEVELS else slice(P, 2 * P)
                        product(n, [(bank(n, h * P, h * P + P), [(left[:, h, tt * P:tt * P + P], right[:, h, q])])
                                    for h in range(HG_H)])
                        n += 1
                pe.wait_ge(pairs_summed, l + 1)
                for i in range(2):
                    n = first[L + "hg.o"] + i
                    wait_room(pe, n)
                    for g in range(2):
                        h = 2 * i + g
                        nc.tensor.matmul(bank(n, g * T, g * T + T), VH[:, 0, h * P:h * P + P], AT[:, h, 0:2, :], start=True, stop=False)
                        last = nc.tensor.matmul(bank(n, g * T + P, g * T + T), VH[:, 1, h * P:h * P + P], AT[:, h, 2, :], start=False, stop=True)
                    last.then_inc(product_done, 1)
                pe.wait_ge(squares_ready, tally.add("squares_ready") + 1)
                for i in range(2):
                    n = first[L + "hg.norm"] + i
                    product(n, [(bank(n), [(ones, SQ[:, 2 * i:2 * i + 2, :])])])
                tally.add("normed", 1)
                pe.wait_ge(normed, tally.n["normed"])
                halves(L + "hg.out", 4, OT, [])
                norm(first[L + "mem.norm"], DK, DK)
                pe.wait_ge(normed, tally.n["normed"])
                for i in range(4):
                    s = slab_first[L + "mem.kv"] + i
                    wait_weights(pe, s)
                    wv = slot(s, DK, 256)
                    for m in range(2):
                        n = first[L + "mem.kv"] + 2 * i + m
                        if i < 2:
                            product(n, [(bank(n, 0, T), [(wv[:, k, m * P:(m + 1) * P], U[:, k, :]) for k in range(DK)])])
                        else:
                            tokens(n, [(bank(n, 0, 256), lambda k: wv[:, k, :], m)], U, DK)
                for m in range(8):
                    wait_evicted(pe, first[L + "mem.kv"] + m)
                attention(L + "mem", "mem",
                          lambda i: [[(MQ[:, h, i % 2 * P:(i % 2 + 1) * P], MK[:, h, :]) for h in (i // 2 * 2, i // 2 * 2 + 1)]],
                          lambda i: [(slice(0, P), g * P,
                                      [(MV[:, k, (i // 2 * 2 + g) * P:(i // 2 * 2 + g + 1) * P], 0, (g * 2 + k) * P, P) for k in range(2)])
                                     for g in range(2)])
                halves(L + "mem.out", 4, OT, attention_numbers(first[L + "mem"], *ATTN["mem"][:3])[2])
                pe.wait_ge(merged_ready, tally.add("merged_ready", 1) + 1)
                quarters(L + "wout", MRG)
                ffn(L + "ffn2")
            norm(first["1.final.norm"], DK, DK)

            pe.wait_ge(setup_done, 1)
            n = first["bias"]
            hot = con("hot", 2 * T, slice(0, BUCKETS + 2))
            product(n, [(bank(n)[0:BIAS_H, :], [(TAB[0:BUCKETS + 2, :], hot)])])

            for l, L in enumerate(block2):
                ffn(L + "ffn1")
                norm(first[L + "mix.norm"], DK, DK)
                pe.wait_ge(normed, tally.n["normed"])
                n = first[L + "win"]
                for i, (kind, c, width, count) in enumerate(WIN2):
                    s = slab_first[L + "win"] + i
                    wait_weights(pe, s)
                    wv = slot(s, DK, width)
                    if kind == "tiles":
                        for m in range(2):
                            product(n + m, [(bank(n + m, 0, T), [(wv[:, k, m * P:(m + 1) * P], U[:, k, :]) for k in range(DK)])])
                    elif kind == "pairs":
                        w5 = wv.rearrange("p k (g j d) -> p k j g d", g=2, j=2)
                        for m in range(2):
                            product(n + m, [(bank(n + m)[64 * g:64 * g + 64, 0:T], [(w5[:, k, m, g, :], U[:, k, :]) for k in range(DK)])
                                            for g in range(2)])
                    elif kind == "tokens":
                        for m in range(NT):
                            tokens(n + m, [(bank(n + m, 0, 256), lambda k: wv[:, k, :], m)], U, DK)
                    elif kind == "gate":
                        tokens(n, [(bank(n, 24 * m, 24 * m + 24), lambda k: wv[:, k, :], m) for m in range(NT)], U, DK)
                    elif kind == "kv":
                        product(n, [(bank(n, 0, T), [(wv[:, k, 0:P], U[:, k, :]) for k in range(DK)])])
                        tokens(n + 1, [(bank(n + 1, P * m, P * m + P), lambda k: wv[:, k, P:2 * P], m) for m in range(NT)], U, DK)
                    elif kind == "shift":
                        for m in range(2):
                            product(n + m, [(bank(n + m)[64 * half:64 * half + 64, g * T:(g + 1) * T],
                                             [(wv[:, k, m * P + 64 * g:m * P + 64 * g + 64], U[:, k, :]) for k in range(DK)])
                                            for half in range(2) for g in range(2)])
                    n += count
                for kv in range(2):
                    pe.wait_ge(blocks_ready, 2 * l + kv + 1)
                    n, s = first[L + "cmp"] + kv, slab_first[L + "cmp"] + 2 * kv
                    wait_weights(pe, s)
                    wait_weights(pe, s + 1)
                    product(n, [(bank(n, 30 * half, 30 * half + 30),
                                 [(slot(s + i // 8, DK, 256)[:, i % 8, half * P:half * P + P], (BLK, BLK2)[kv][:, i, :]) for i in range(16)])
                                for half in range(2)])
                s = slab_first[L + "cmp"] + 4
                wait_weights(pe, s)
                w2 = slot(s, 4, 64)
                n = first[L + "cmp"] + 2
                pe.wait_ge(hidden_ready, 2 * l + 1)
                product(n, [(bank(n)[64 * g:64 * g + 64, 0:15], [(w2[:, half, :], HID[:, half, 15 * g:15 * g + 15]) for half in range(2)])
                            for g in range(2)])
                pe.wait_ge(hidden_ready, 2 * l + 2)
                product(n + 1, [(bank(n + 1)[0:15, 64 * g:64 * g + 64], [(HID2[:, half, 15 * g:15 * g + 15], w2[:, 2 + half, :]) for half in range(2)])
                                for g in range(2)])
                for m in range(sum(x[3] for x in WIN2[:6])):
                    wait_evicted(pe, first[L + "win"] + m)
                attention(L + "A", "A",
                          lambda i: [[(AQ[64 * g:64 * g + 64, i // 2, i % 2 * P:(i % 2 + 1) * P], AK[64 * g:64 * g + 64, i // 2, 0:(i % 2 + 1) * P])
                                      for g in range(2)]],
                          lambda i: [(slice(0, P), 0, [(AV[:, k, i // 2 * P:(i // 2 + 1) * P], 0, k * P, P) for k in range(i % 2 + 1)])])
                pe.wait_ge(squares_ready, tally.add("squares_ready") + 1)
                for i in range(2):
                    n = first[L + "A.norm"] + i
                    product(n, [(bank(n), [(ones, SQ[:, 2 * i:2 * i + 2, :])])])
                tally.add("normed", 1)
                pe.wait_ge(normed, tally.n["normed"])
                halves(L + "A.out", 4, OT, [])
                for m in range(sum(x[3] for x in WIN2[:11])):
                    wait_evicted(pe, first[L + "win"] + m)
                wait_evicted(pe, first[L + "cmp"] + 2)
                wait_evicted(pe, first[L + "cmp"] + 3)

                def b_scores(i):
                    q = [BQ[64 * g:64 * g + 64, i // 2, i % 2 * P:(i % 2 + 1) * P] for g in range(2)]
                    n = (i % 2 + 1) * P
                    return [[(q[g], kk[64 * g:64 * g + 64, 0:m]) for g in range(2)] for kk, m in ((KCMP, blocks(i % 2)), (BKS, n), (BKW, n))]

                def b_values(i):
                    out = []
                    for g in range(2):
                        nb = blocks(i % 2)
                        terms = [(VCMP[0:nb, g, :], 0, g * P, nb)]
                        for b, vv in ((1, BVS), (2, BVW)):
                            terms += [(vv[:, k, 64 * g:64 * g + 64], b, (g * (i % 2 + 1) + k) * P, P) for k in range(i % 2 + 1)]
                        out.append((slice(64 * g, 64 * g + 64), 0, terms))
                    return out

                attention(L + "B", "B", b_scores, b_values)
                halves(L + "B.out", 4, OT, attention_numbers(first[L + "B"], *ATTN["B"][:3])[2])
                for m in range(sum(x[3] for x in WIN2[:14])):
                    wait_evicted(pe, first[L + "win"] + m)
                attention(L + "C", "C",
                          lambda i: [[(CQ2[64 * g:64 * g + 64, i // 2, i % 2 * P:(i % 2 + 1) * P], CK2[64 * g:64 * g + 64, 0:(i % 2 + 1) * P])
                                      for g in range(2)]],
                          lambda i: [(slice(64 * g, 64 * g + 64), 0,
                                      [(CV2[:, k, 64 * g:64 * g + 64], 0, (g * (i % 2 + 1) + k) * P, P) for k in range(i % 2 + 1)])
                                     for g in range(2)])
                halves(L + "C.out", 4, OT, attention_numbers(first[L + "C"], *ATTN["C"][:3])[2])
                pe.wait_ge(merged_ready, tally.add("merged_ready", 1) + 1)
                quarters(L + "wout", MRG)
                ffn(L + "ffn2")
                norm(first[L + "ple.norm"], DK, DK)
                s = slab_first[L + "ple.p"]
                wait_weights(pe, s)
                pe.wait_ge(layer_in, 16 * (l + 1))
                for m in range(DK):
                    n = first[L + "ple.p"] + m
                    product(n, [(bank(n, 0, T), [(slot(s, 2, D)[:, k, m * P:(m + 1) * P], PIN[:, k, :]) for k in range(2)])])
                pe.wait_ge(normed, tally.n["normed"])
                quarters(L + "ple.gate", U)
            norm(first["2.final.norm"], DK, DK)

        @block.scalar
        def _(act):
            tally = Tally()

            def link(ins):
                ins.then_inc(act_step, 1)
                act.wait_ge(act_step, tally.add("act_step") + 1)

            def evict(n, dst, src, func=ACT.Copy):
                wait_product(act, n)
                nc.scalar.activation(dst, src, func).then_inc(evicted[n % BANKS], 1)

            def norm(v=V, r=RSTD):
                act.wait_ge(mean_ready, tally.add("mean_ready") + 1)
                link(nc.scalar.activation(r, v, ACT.Ln))
                nc.scalar.activation(r, r, ACT.Exp, scale=-0.5).then_inc(rstd_ready, 1)

            def ffn(name):
                norm(V[:], RSTD[:])
                p0 = first[name + ".in"]

                def pair(r, j):
                    n = p0 + 2 * j
                    wait_product(act, n, r)
                    if not isinstance(r, int) or j >= 2:
                        wait_evicted(act, n - 3, r)
                    nc.scalar.activation(SILU[:, j % 2, :], bank(n, 0, T), ACT.Silu).then_inc(evicted[n % BANKS], 1)

                rounds(act, FK, pair)

            def attention(name, kind, scale=1.0):
                units, n_s, n_t, n_b = ATTN[kind]
                s, t, o, _ = attention_numbers(first[name], units, n_s, n_t)
                base = tally.add("max_ready", units)
                for i in range(units + 1):
                    if i < units:
                        qt = par = i % 2
                        act.wait_ge(max_ready, base + i + 1)
                        for b in range(n_b):
                            cmp = kind == "B" and b == 0
                            nk = blocks(qt) if cmp else T if kind == "mem" else (qt + 1) * P
                            nk += kind == "C"
                            for g in range(2):
                                src = bank(s[i])[:, g * T:(g + 1) * T] if kind == "mem" else S[:, b, par, g, 0:nk]
                                last = nc.scalar.activation(S[:, b, par, g, 0:nk], src, ACT.Exp, bias=MX[:, par, b, g:g + 1],
                                                            scale=scale, accum_out=SUM[:, par, b, g:g + 1])
                        last.then_inc(evicted[s[i] % BANKS] if kind == "mem" else exp_done, 1)
                    if i >= 1:
                        u = i - 1
                        if u >= 2:
                            wait_product(act, o[u - 2])
                        for b in range(n_t):
                            cmp = kind == "B" and b == 0
                            keys = 1 if cmp else NT if kind == "mem" else u % 2 + 1
                            c = (1 if kind == "A" else 2) * keys * P
                            rows = slice(0, blocks(u % 2)) if cmp else slice(0, P)
                            evict(t[u] + b, PT[rows, b, u % 2, 0:c], bank(t[u] + b)[rows, 0:c])

            act.wait_ge(angle_ready, 1)
            nc.scalar.activation(SIN[64:96, :], SIN[64:96, :], ACT.Sin)
            nc.scalar.activation(COS[64:96, :], COS[64:96, :], ACT.Sin).then_inc(rope_ready, 1)
            act.wait_ge(angle_ready, 2)
            link(nc.scalar.activation(LB[:, 2, :], LB[:, 1, :], ACT.Exp, scale=-1.0))
            nc.scalar.activation(LB[:, 2, :], LB[:, 2, :], ACT.Ln, bias=1.0).then_inc(rope_ready, 1)
            act.wait_ge(angle_ready, 3)
            nc.scalar.activation(LAM[:, 2:4, :], LAM[:, 0:2, :], ACT.Exp).then_inc(lambda_ready, 1)

            for l, L in enumerate(block1):
                ffn(L + "ffn1")
                norm(V[:], RSTD[:])
                n = first[L + "win"]
                for c, width, count in WIN1:
                    for m in range(count):
                        if c == C_KR:
                            evict(n, KR[64:96, 0, :], bank(n)[64:96, 0:T])
                        elif C_HI <= c < C_HG:
                            evict(n, VH[:, m, c - C_HI:c - C_HI + 256], bank(n, 0, 256))
                        else:
                            for c0, dst, func in ((C_GATE, GATE, ACT.Sigmoid), (C_MQ, MQ, ACT.Copy), (C_HG, HGT, ACT.Silu),
                                                  (C_HF, Z.rearrange("p (h t) -> p h t", t=T), ACT.Copy),
                                                  (C_HQ, HQ, ACT.Silu), (C_KV, CKV, ACT.Copy), (C_Q, CQ, ACT.Copy)):
                                if c >= c0:
                                    evict(n, dst[:, (c - c0) // P + m, :], bank(n, 0, T), func)
                                    break
                        n += 1
                norm(V[:], RSTD[:])
                norm(V[:], RSTD[:])
                for h in range(MLA_H):
                    evict(first[L + "uq"] + h, QH[0:QK, h, :], bank(first[L + "uq"] + h)[0:QK, 0:T])
                for h in range(MLA_H):
                    evict(first[L + "uk"] + h, KH[0:NOPE, h, :], bank(first[L + "uk"] + h)[0:NOPE, 0:T])
                for m in range(NT):
                    evict(first[L + "uv"] + m, VM[:, m, :], bank(first[L + "uv"] + m))
                attention(L + "mla", "mla")
                HA, HB = HX[:, 0, :], HX[:, 1, :]
                act.wait_ge(hg_vec, tally.add("hg_vec") + 1)
                link(nc.scalar.activation(HB, HA, ACT.Exp, scale=-1.0))
                nc.scalar.activation(HB, HB, ACT.Ln, bias=1.0).then_inc(hg_act, 1)
                act.wait_ge(hg_vec, tally.add("hg_vec") + 1)
                if l == 0:
                    nc.scalar.activation(HK, HK, ACT.Exp).then_inc(hg_act, 1)
                else:
                    for h in range(HG_H):
                        k = HK[:, h * T:(h + 1) * T]
                        last = nc.scalar.activation(k, k, ACT.Exp, bias=LB[:, 4, h:h + 1])
                    last.then_inc(hg_act, 1)
                    act.wait_ge(hg_vec, tally.add("hg_vec") + 1)
                    link(nc.scalar.activation(HB, HA, ACT.Exp, scale=-1.0))
                    nc.scalar.activation(HB, HB, ACT.Ln, bias=1.0).then_inc(hg_act, 1)
                for level in range(LEVELS):
                    act.wait_ge(hg_vec, tally.add("hg_vec") + 1)
                    nc.scalar.activation(HX[:, level % 2, :], HX[:, level % 2, :], ACT.Exp).then_inc(hg_act, 1)
                for i in range(2):
                    evict(first[L + "hg.o"] + i, OT[:, 2 * i:2 * i + 2, :], bank(first[L + "hg.o"] + i))
                norm(TMP[:], TMP[:])
                norm(V[:], RSTD[:])
                for i in range(8):
                    n = first[L + "mem.kv"] + i
                    if i < 4:
                        evict(n, MK[:, i, :], bank(n, 0, T))
                    else:
                        c = (i - 4) // 2 * 256
                        evict(n, MV[:, i % 2, c:c + 256], bank(n, 0, 256))
                attention(L + "mem", "mem", P ** -0.5)
                ffn(L + "ffn2")
            norm(V[:], RSTD[:])
            evict(first["bias"], ROWS[0:BIAS_H, :], bank(first["bias"])[0:BIAS_H, :])

            for l, L in enumerate(block2):
                ffn(L + "ffn1")
                norm(V[:], RSTD[:])
                n = first[L + "win"]
                for kind, c, width, count in WIN2:
                    if kind in ("tiles", "pairs"):
                        for c0, dst, func in ((D_GATE, GATE, ACT.Sigmoid), (D_CQ, CQ2, ACT.Copy), (D_BQ, BQ, ACT.Copy),
                                              (D_AK, AK, ACT.Copy), (D_AQ, AQ, ACT.Copy)):
                            if c >= c0:
                                tile = (c - c0) // (64 if kind == "pairs" else P)
                                for m in range(2):
                                    evict(n + m, dst[:, tile + m, :], bank(n + m, 0, T), func)
                                break
                    elif kind == "tokens":
                        for m in range(NT):
                            evict(n + m, AV[:, m, c - D_AV:c - D_AV + 256], bank(n + m, 0, 256))
                    elif kind == "gate":
                        evict(n, BG, bank(n, 0, 24 * NT).rearrange("p (m c) -> p m c", m=NT), ACT.Sigmoid)
                    elif kind == "kv":
                        kd, vd = {D_BKS: (BKS, BVS), D_BKW: (BKW, BVW), D_CK: (CK2, CV2)}[c]
                        evict(n, kd, bank(n, 0, T))
                        evict(n + 1, vd, bank(n + 1, 0, NT * P).rearrange("p (m c) -> p m c", m=NT))
                    elif kind == "shift":
                        for m, dst in enumerate((KC2, VC2)):
                            b3 = bank(n + m).rearrange("p (g t) -> p g t", g=2)
                            wait_product(act, n + m)
                            nc.scalar.activation(dst[0:64, :, :], b3[0:64], ACT.Copy)
                            nc.scalar.activation(dst[64:128, :, 0:T - 1], b3[64:128, :, 1:T], ACT.Copy)\
                              .then_inc(evicted[(n + m) % BANKS], 1)
                    n += count
                for kv in range(2):
                    act.wait_ge(gelu_vec, tally.add("gelu_vec") + 1)
                    nc.scalar.activation(GY, GY, ACT.Exp, scale=-2.0 * (2.0 / np.pi) ** 0.5).then_inc(gelu_act, 1)
                n = first[L + "cmp"] + 2
                evict(n, KCMP[:, 0:15], bank(n, 0, 15))
                evict(n + 1, VCMP[0:15, :, :], bank(n + 1)[0:15, 0:P].rearrange("p (g d) -> p g d", g=2))
                attention(L + "A", "A")
                norm(TMP[:], TMP[:])
                attention(L + "B", "B")
                attention(L + "C", "C")
                ffn(L + "ffn2")
                norm(V[:], RSTD[:])
                for m in range(DK):
                    evict(first[L + "ple.p"] + m, PLE[:, m, :], bank(first[L + "ple.p"] + m, 0, T))
                for m in range(DK):
                    evict(first[L + "ple.gate"] + m, GATE[:, DK + m, :], bank(first[L + "ple.gate"] + m, 0, T), ACT.Sigmoid)
            norm(V[:], RSTD[:])

        @block.vector
        def _(dve):
            tally = Tally()
            v_ = nc.vector

            def link(ins):
                ins.then_inc(vec_step, 1)
                dve.wait_ge(vec_step, tally.add("vec_step") + 1)

            def norm_mean(n, width, count, v):
                wait_product(dve, n)
                v_.tensor_scalar(v, bank(n, 0, width), 1.0 / count, EPS, ALU.mult, ALU.add)\
                  .then_inc(evicted[n % BANKS], 1)

            def norm(n, src, kt, gain, dst, done=normed):
                v_.tensor_tensor(SQ[:, 0:kt, :], src, src, ALU.mult).then_inc(squares_ready, 1)
                wait_product(dve, n)
                v_.tensor_scalar(V[:], bank(n, 0, T), 1.0 / (kt * P), EPS, ALU.mult, ALU.add)\
                  .then_inc(evicted[n % BANKS], 1)
                wait_evicted(dve, n)
                v_.tensor_copy(V[:], V[:]).then_inc(mean_ready, 1)
                dve.wait_ge(rstd_ready, tally.add("rstd_ready") + 1)
                for k in range(kt):
                    v_.scalar_tensor_tensor(dst[:, k, :], src[:, k, :], gain[:, k:k + 1], RSTD[:], ALU.mult, ALU.mult)\
                      .then_inc(done, 1)

            def add_to_x(name, factor):
                for m in range(DK):
                    n = first[name] + m
                    wait_product(dve, n)
                    v_.scalar_tensor_tensor(X[:, m, :], bank(n, 0, T), factor, X[:, m, :], ALU.mult, ALU.add)\
                      .then_inc(evicted[n % BANKS], 1)
                for m in range(DK):
                    wait_evicted(dve, first[name] + m)

            def ffn(name, gain):
                norm(first[name + ".norm"], X[:], DK, gain, U[:])
                p0 = first[name + ".in"]

                def pair(r, j):
                    n = p0 + 2 * j
                    wait_evicted(dve, n, r)
                    wait_product(dve, n + 1, r)
                    h = H[:, bass.ds(r * SLOTS + j, 1), :].rearrange("p a t -> p (a t)")
                    v_.tensor_tensor(h, SILU[:, j % 2, :], bank(n + 1, 0, T), ALU.mult)\
                      .then_inc(evicted[(n + 1) % BANKS], 1)

                rounds(dve, FK, pair)
                add_to_x(name + ".out", 0.5)

            def merge(name, branch):
                for m in range(DK):
                    n = first[name] + m
                    g = GATE[:, branch * DK + m, :]
                    wait_product(dve, n)
                    if branch == 0:
                        v_.tensor_tensor(MRG[:, m, :], bank(n, 0, T), g, ALU.mult).then_inc(evicted[n % BANKS], 1)
                    else:
                        v_.tensor_tensor(TMP[:, m % 2, 0:T], bank(n, 0, T), g, ALU.mult).then_inc(evicted[n % BANKS], 1)
                        wait_evicted(dve, n)
                        link(v_.tensor_tensor(MRG[:, m, :], MRG[:, m, :], TMP[:, m % 2, 0:T], ALU.add))
                if branch == 2:
                    v_.tensor_copy(MRG[:, DK - 1, T - 1:T], MRG[:, DK - 1, T - 1:T]).then_inc(merged_ready, 1)
                else:
                    for m in range(DK):
                        wait_evicted(dve, first[name] + m)

            def attention(name, kind, scale, window=None, lam=None, sinks=None):
                units, n_s, n_t, n_b = ATTN[kind]
                s, t, o, _ = attention_numbers(first[name], units, n_s, n_t)
                exps = tally.add("exp_done", 0 if kind == "mem" else units)

                def scores(i):
                    qt = par = i % 2
                    for b in range(n_b):
                        n = s[i] + b
                        cmp = kind == "B" and b == 0
                        nk = blocks(qt) if cmp else T if kind == "mem" else (qt + 1) * P
                        if kind == "mem":
                            wait_product(dve, n)
                            sc = bank(n).rearrange("p (g t) -> p g t", g=2)[:, :, 0:nk]
                            link(v_.reduce_max(MX[:, par, b, :], sc, AX.X))
                            continue
                        if i >= 2:
                            wait_product(dve, t[i - 2] + b)
                        if n_s == n_b:
                            wait_product(dve, n)
                            sc = bank(n).rearrange("p (g t) -> p g t", g=2)[:, :, 0:nk]
                            v_.scalar_tensor_tensor(S[:, b, par, :, 0:nk], sc, scale, window(i, b), ALU.mult, ALU.add)\
                              .then_inc(evicted[n % BANKS], 1)
                        else:
                            for g in range(2):
                                n = s[i] + 2 * b + g
                                wait_product(dve, n)
                                v_.scalar_tensor_tensor(S[:, b, par, g, 0:nk], bank(n, 0, nk), scale, window(i, b)[:, g, :],
                                                        ALU.mult, ALU.add).then_inc(evicted[n % BANKS], 1)
                            wait_evicted(dve, n - 1)
                        if kind == "C":
                            link(v_.tensor_copy(S[:, b, par, :, nk:nk + 1], sinks[:, i // 2 * 2:i // 2 * 2 + 2].unsqueeze(2)))
                            nk += 1
                        wait_evicted(dve, n)
                        link(v_.reduce_max(MX[:, par, b, :], S[:, b, par, :, 0:nk], AX.X))
                    v_.tensor_scalar(MX[:, par, 0:n_b, :], MX[:, par, 0:n_b, :], -scale if kind == "mem" else -1.0, None, ALU.mult)\
                      .then_inc(max_ready, 1)

                def scale_probs(i):
                    qt = par = i % 2
                    if kind == "mem":
                        wait_evicted(dve, s[i])
                    else:
                        dve.wait_ge(exp_done, exps + i + 1)
                    link(v_.reciprocal(SUM[:, par, 0:n_b, :], SUM[:, par, 0:n_b, :]))
                    if kind == "A":
                        link(v_.tensor_scalar(SUM[:, par, 0, 1:2], SUM[:, par, 0, 1:2], lam, None, ALU.mult))
                        p0, p1 = S[:, 0, par, 0, 0:(qt + 1) * P], S[:, 0, par, 1, 0:(qt + 1) * P]
                        link(v_.tensor_scalar(p0, p0, SUM[:, par, 0, 0:1], None, ALU.mult))
                        v_.scalar_tensor_tensor(p0, p1, SUM[:, par, 0, 1:2], p0, ALU.mult, ALU.add).then_inc(probs_ready, 1)
                        return
                    if kind == "B":
                        gates = BG[:, qt, :].rearrange("p (g j b) -> p j b g", g=2, j=4)[:, i // 2]
                        link(v_.tensor_tensor(SUM[:, par, :, :], SUM[:, par, :, :], gates, ALU.mult))
                        if qt == 0:
                            link(v_.tensor_scalar(SUM[:, par, 0, :], SUM[:, par, 0, :], con("sees", 1), None, ALU.mult))
                    for b in range(n_b):
                        nk = blocks(qt) if kind == "B" and b == 0 else T if kind == "mem" else (qt + 1) * P
                        for g in range(2):
                            p = S[:, b, par, g, 0:nk]
                            last = v_.tensor_scalar(p, p, SUM[:, par, b, g:g + 1], None, ALU.mult)
                    last.then_inc(probs_ready, 1)

                def outputs(i):
                    wait_product(dve, o[i])
                    j, q = i // 2, slice(i % 2 * P, i % 2 * P + P)
                    if kind == "mem":
                        dst, src = OT[:, 2 * j:2 * j + 2, q], bank(o[i], 0, 2 * P).rearrange("p (g t) -> p g t", g=2)
                    else:
                        dst, src = OT[:, j, q], bank(o[i], 0, P)
                    v_.tensor_copy(dst, src).then_inc(evicted[o[i] % BANKS], 1)

                scores(0)
                for i in range(units):
                    if i + 1 < units:
                        scores(i + 1)
                    scale_probs(i)
                    if i >= 1:
                        outputs(i - 1)
                outputs(units - 1)
                return o

            def group_norm(name, count):
                v_.tensor_tensor(SQ[:, 0:4, :], OT, OT, ALU.mult).then_inc(squares_ready, 1)
                for i in range(2):
                    n = first[name] + i
                    wait_product(dve, n)
                    v_.tensor_scalar(TMP[:, i, :], bank(n), 1.0 / count, EPS, ALU.mult, ALU.add)\
                      .then_inc(evicted[n % BANKS], 1)
                    wait_evicted(dve, n)
                v_.tensor_copy(TMP[:, 0, 0:1], TMP[:, 0, 0:1]).then_inc(mean_ready, 1)
                dve.wait_ge(rstd_ready, tally.add("rstd_ready") + 1)

            dve.wait_ge(inputs_in, 64)
            link(v_.tensor_copy(V[64:96, :], COS[64:96, :].bitcast(I32)))
            link(v_.tensor_scalar(V[64:96, :], V[64:96, :], con("freq", 1, slice(64, 96)), None, ALU.mult))
            for table, turn in ((SIN, 0.0), (COS, 0.25)):
                a, n, r = V[64:96, :], RSTD[64:96, :], table[64:96, :]
                link(v_.tensor_scalar(n, a, 1.0 / (2.0 * np.pi), turn, ALU.mult, ALU.add))
                link(v_.tensor_scalar(n, n, 12582912.0, None, ALU.add))
                link(v_.tensor_scalar(n, n, -12582912.0, None, ALU.add))
                link(v_.scalar_tensor_tensor(r, n, -TURN[0], a, ALU.mult, ALU.add))
                link(v_.scalar_tensor_tensor(r, n, -TURN[1], r, ALU.mult, ALU.add))
                link(v_.scalar_tensor_tensor(r, n, -TURN[2], r, ALU.mult, ALU.add))
                link(v_.tensor_scalar(r, r, turn * 2.0 * np.pi, None, ALU.add))
                link(v_.tensor_scalar(r, r, 3.1415925, -3.1415925, ALU.min, ALU.max))
            v_.memset(RESET[:], 1.0).then_inc(angle_ready, 1)
            link(v_.tensor_tensor(LB[:, 0, :], vec("lb1", HG_H), vec("lb0", HG_H), ALU.subtract))
            v_.scalar_tensor_tensor(LB[:, 1, :], LB[:, 0, :], -1.0, LB[:, 0, :], ALU.mult, ALU.max).then_inc(angle_ready, 1)
            dve.wait_ge(rope_ready, 2)
            link(v_.scalar_tensor_tensor(LB[:, 3, :], LB[:, 0, :], 0.0, LB[:, 2, :], ALU.min, ALU.subtract))
            link(v_.tensor_tensor(LB[:, 4, :], LB[:, 3, :], LB[:, 0, :], ALU.subtract))
            link(v_.tensor_tensor(LB[:, 5, :], LB[:, 4, :], LB[:, 3, :], ALU.subtract))
            for l in range(DEPTH):
                pairs = vec(f"lambda{l}", 256).rearrange("p (a b d) -> p a b d", a=2, b=2)
                prod = TMP[:, l, 0:P].rearrange("p (a d) -> p a d", a=2)
                link(v_.tensor_tensor(prod, pairs[:, :, 0, :], pairs[:, :, 1, :], ALU.mult))
                link(v_.reduce_sum(LAM[:, 0:2, l], prod, AX.X))
            v_.memset(RESET[:].rearrange("p (c t) -> p c t", t=CHUNK)[:, :, 0:1], 0.0).then_inc(angle_ready, 1)
            dve.wait_ge(lambda_ready, 1)
            link(v_.tensor_tensor(LAM[:, 4, :], LAM[:, 3, :], LAM[:, 2, :], ALU.subtract))
            for l in range(DEPTH):
                link(v_.tensor_scalar(LAM[:, 5, l:l + 1], LAM[:, 4, l:l + 1], -LAM_INIT[l], None, ALU.add))
            v_.tensor_copy(TAB[0:BUCKETS, :], vec("rel_bias", BIAS_H, slice(0, BUCKETS)))
            v_.tensor_copy(TAB[BUCKETS:BUCKETS + 2, :], con("mask_rows", BIAS_H, slice(BUCKETS, BUCKETS + 2))).then_inc(setup_done, 1)

            heads = "p (h t) -> p h t"
            for l, L in enumerate(block1):
                ffn(L + "ffn1", vec(f"ffn1_norm{l}", DK))
                norm(first[L + "mix.norm"], X[:], DK, vec(f"mix_norm{l}", DK), U[:])
                n = first[L + "win"]
                for m in range(3):
                    wait_evicted(dve, n + m)
                norm(first[L + "q.norm"], CQ, 3, vec(f"q_lat_norm{l}", 3), CQ)
                for m in range(3, 5):
                    wait_evicted(dve, n + m)
                norm(first[L + "kv.norm"], CKV, 2, vec(f"kv_lat_norm{l}", 2), CKV)
                cos2 = COS[64:96, :].unsqueeze(1).broadcast_to([ROPE, 2, T])
                sin2 = SIN[64:96, :].unsqueeze(1).broadcast_to([ROPE, 2, T])
                for m in range(4):
                    n = first[L + "swap"] + m
                    q = QH[64:96, 2 * m:2 * m + 2, :]
                    turned = TMP[64:96, m % 2, :].rearrange("p (g t) -> p g t", g=2)
                    wait_product(dve, n)
                    v_.tensor_tensor(turned, bank(n)[64:96, :].rearrange("p (g t) -> p g t", g=2), sin2, ALU.mult)\
                      .then_inc(evicted[n % BANKS], 1)
                    wait_evicted(dve, n)
                    link(v_.tensor_tensor(q, q, cos2, ALU.mult))
                    link(v_.tensor_tensor(q, q, turned, ALU.add))
                n = first[L + "swap"] + 4
                wait_product(dve, n)
                v_.tensor_tensor(TMP[64:96, 0, 0:T], bank(n)[64:96, 0:T], SIN[64:96, :], ALU.mult).then_inc(evicted[n % BANKS], 1)
                link(v_.tensor_tensor(KR[64:96, 1, :], KR[64:96, 0, :], COS[64:96, :], ALU.mult))
                wait_evicted(dve, n)
                link(v_.tensor_tensor(KR[64:96, 1, :], KR[64:96, 1, :], TMP[64:96, 0, 0:T], ALU.add))
                v_.tensor_copy(KH[64:96, :, :], KR[64:96, 1, :].unsqueeze(1).broadcast_to([ROPE, MLA_H, T])).then_inc(roped, 1)
                causal = con("causal", 2 * P)

                def own(i, b):
                    return causal[:, (1 - i % 2) * P:2 * P].unsqueeze(1).broadcast_to([P, 2, (i % 2 + 1) * P])

                attention(L + "mla", "mla", QK ** -0.5, own)
                merge(L + "mla.out", 0)

                HA, HB = HX[:, 0, :], HX[:, 1, :]
                w0 = first[L + "win"]
                for m in range(6, 14):
                    wait_evicted(dve, w0 + m)
                v_.scalar_tensor_tensor(HA, Z, -1.0, Z, ALU.mult, ALU.max).then_inc(hg_vec, 1)
                dve.wait_ge(hg_act, tally.add("hg_act") + 1)
                link(v_.scalar_tensor_tensor(GS, Z, 0.0, HB, ALU.min, ALU.subtract))
                v_.tensor_tensor(HK, GS, Z, ALU.subtract).then_inc(hg_vec, 1)
                dve.wait_ge(hg_act, tally.add("hg_act") + 1)
                g = GS
                if l > 0:
                    for h in range(HG_H):
                        c = slice(h * T, (h + 1) * T)
                        link(v_.tensor_scalar(Z[:, c], GS[:, c], LB[:, 5, h:h + 1], None, ALU.add))
                    v_.scalar_tensor_tensor(HA, Z, -1.0, Z, ALU.mult, ALU.max).then_inc(hg_vec, 1)
                    dve.wait_ge(hg_act, tally.add("hg_act") + 1)
                    link(v_.scalar_tensor_tensor(Z, Z, 0.0, HB, ALU.max, ALU.add))
                    for h in range(HG_H):
                        c = slice(h * T, (h + 1) * T)
                        link(v_.tensor_scalar(Z[:, c], Z[:, c], LB[:, 3, h:h + 1], None, ALU.add))
                    src, GC = Z, GS
                else:
                    src, GC = GS, Z
                v_.tensor_tensor_scan(GC, RESET[:], src, 0.0, ALU.mult, ALU.add).then_inc(pair_ready, 1)
                dve.wait_ge(pair_ready, l * (LEVELS + 1) + 1)

                def exponents(level):
                    x = HX[:, level % 2, :]
                    if level < 6:
                        n = 1 << level
                        gv = GC.rearrange("p (b two n) -> p b two n", two=2, n=n)
                        xv = x.rearrange("p (b two n) -> p b two n", two=2, n=n)
                        pivot = gv[:, :, 0, n - 1:n].broadcast_to([P, HG_H * T // (2 * n), n])
                        v_.tensor_tensor(xv[:, :, 1, :], gv[:, :, 1, :], pivot, ALU.subtract)
                        v_.tensor_tensor(xv[:, :, 0, :], pivot, gv[:, :, 0, :], ALU.subtract).then_inc(hg_vec, 1)
                        return
                    gv = GC.rearrange("p (h c n) -> p h c n", h=HG_H, n=CHUNK)
                    xv = x.rearrange("p (h c n) -> p h c n", h=HG_H, n=CHUNK)

                    def end(c):
                        return gv[:, :, c, CHUNK - 1:CHUNK].broadcast_to([P, HG_H, CHUNK])

                    if level == 6:
                        v_.tensor_copy(xv[:, :, 1, :], gv[:, :, 1, :])
                        v_.tensor_copy(xv[:, :, 3, :], gv[:, :, 3, :])
                        v_.tensor_tensor(xv[:, :, 0, :], end(0), gv[:, :, 0, :], ALU.subtract)
                        v_.tensor_tensor(xv[:, :, 2, :], end(2), gv[:, :, 2, :], ALU.subtract).then_inc(hg_vec, 1)
                    else:
                        link(v_.tensor_tensor(xv[:, :, 0, :], end(0), gv[:, :, 0, :], ALU.subtract))
                        v_.tensor_copy(xv[:, :, 2, :], gv[:, :, 2, :])
                        v_.tensor_tensor(xv[:, :, 3, :], gv[:, :, 3, :], end(2), ALU.add)
                        v_.tensor_tensor(xv[:, :, 1, :], end(1), gv[:, :, 1, :], ALU.subtract)
                        v_.tensor_tensor(xv[:, :, 0, :], xv[:, :, 0, :], end(1), ALU.add).then_inc(hg_vec, 1)

                def factors(level):
                    dve.wait_ge(hg_act, tally.add("hg_act") + 1)
                    n = 1 << level
                    xv = HX[:, level % 2, :].rearrange("p (b two n) -> p b two n", two=2, n=n)
                    kv = HK.rearrange("p (b two n) -> p b two n", two=2, n=n)
                    qv = HQ.rearrange("p h t -> p (h t)").rearrange("p (b two n) -> p b two n", two=2, n=n)
                    v_.tensor_tensor(xv[:, :, 0, :], xv[:, :, 0, :], kv[:, :, 0, :], ALU.mult)
                    v_.tensor_tensor(xv[:, :, 1, :], xv[:, :, 1, :], qv[:, :, 1, :], ALU.mult).then_inc(pair_ready, 1)

                def masked(level):
                    for tt in ((0, 1) if level < LEVELS else (0,)):
                        n = first[L + "pairs"] + 2 * level + tt
                        wait_product(dve, n)
                        a4 = bank(n).rearrange(heads, t=P)
                        dst = AT[:, :, 1, :] if level == LEVELS else AT[:, :, 2 * tt, :]
                        if level == LEVELS:
                            v_.tensor_copy(dst, a4).then_inc(evicted[n % BANKS], 1)
                            continue
                        mask = con(f"pair{level}", P).unsqueeze(1).broadcast_to([P, HG_H, P])
                        tmp = TMP[:, tt, :].rearrange(heads, t=P)
                        v_.tensor_tensor(dst if level == 0 else tmp, a4, mask, ALU.mult).then_inc(evicted[n % BANKS], 1)
                        wait_evicted(dve, n)
                        if level:
                            link(v_.tensor_tensor(dst, dst, tmp, ALU.add))

                for level in range(LEVELS + 1):
                    if level < LEVELS:
                        if level >= 2:
                            wait_product(dve, first[L + "pairs"] + 2 * (level - 1) + 1)
                        exponents(level)
                    masked(level)
                    if level < LEVELS:
                        factors(level)
                wait_evicted(dve, first[L + "pairs"] + 2 * LEVELS)
                v_.tensor_copy(AT[:, 0, 0, 0:1], AT[:, 0, 0, 0:1]).then_inc(pairs_summed, 1)
                wait_evicted(dve, first[L + "hg.o"])
                wait_evicted(dve, first[L + "hg.o"] + 1)
                group_norm(L + "hg.norm", P)
                link(v_.scalar_tensor_tensor(OT, OT, vec(f"hg_out_norm{l}", 1), TMP[:].rearrange("p a (b t) -> p (a b) t", t=T), ALU.mult, ALU.mult))
                for m in range(18, 22):
                    wait_evicted(dve, w0 + m)
                v_.tensor_tensor(OT, OT, HGT, ALU.mult).then_inc(normed, 1)
                merge(L + "hg.out", 1)

                dve.wait_ge(mem_in, 16 * (l + 1))
                norm(first[L + "mem.norm"], HX.rearrange("p a (b t) -> p (a b) t", t=T), DK, vec(f"mem_norm{l}", DK), U[:])
                attention(L + "mem", "mem", P ** -0.5)
                merge(L + "mem.out", 2)
                add_to_x(L + "wout", 1.0)
                ffn(L + "ffn2", vec(f"ffn2_norm{l}", DK))
            norm(first["1.final.norm"], X[:], DK, vec("final1", DK), X[:])
            dve.wait_ge(normed, NORMED_1)

            for l, L in enumerate(block2):
                ffn(L + "ffn1", vec(f"norm_g{l}0", DK))
                norm(first[L + "mix.norm"], X[:], DK, vec(f"norm_g{l}1", DK), U[:])
                w0 = first[L + "win"]
                for kv in range(2):
                    wait_evicted(dve, w0 + 16 + kv)
                    src = (KC2, VC2)[kv]
                    for half in range(2):
                        dst = (BLK, BLK2)[kv][:, 8 * half:8 * half + 8, :].rearrange("p l (g n) -> p l g n", g=2)
                        tok = src[:, :, 16 * half:16 * half + 240].rearrange("p g (n l two) -> p l g n two", l=8, two=2)[:, :, :, :, 0]
                        pos = vec(f"pos{l}{kv}", 16)[:, 8 * half:8 * half + 8].unsqueeze(2).unsqueeze(3).broadcast_to([P, 8, 2, 15])
                        last = v_.tensor_tensor(dst, tok, pos, ALU.add)
                    last.then_inc(blocks_ready, 1)
                for kv in range(2):
                    n = first[L + "cmp"] + kv
                    if 2 * l + kv:
                        dve.wait_ge(hidden_ready, 2 * l + kv)
                    wait_product(dve, n)
                    v_.tensor_copy(GX, bank(n, 0, 60).rearrange("p (a b) -> p a b", a=2)).then_inc(evicted[n % BANKS], 1)
                    wait_evicted(dve, n)
                    link(v_.tensor_tensor(GY, GX, GX, ALU.mult))
                    link(v_.tensor_scalar(GY, GY, 0.044715, 1.0, ALU.mult, ALU.add))
                    v_.tensor_tensor(GY, GY, GX, ALU.mult).then_inc(gelu_vec, 1)
                    dve.wait_ge(gelu_act, tally.add("gelu_act") + 1)
                    link(v_.tensor_scalar(GY, GY, 1.0, None, ALU.add))
                    link(v_.reciprocal(GY, GY))
                    v_.tensor_tensor((HID, HID2)[kv], GX, GY, ALU.mult).then_inc(hidden_ready, 1)
                if l == 0:
                    dve.wait_ge(windows_in, 16)

                def pair_window(h0):
                    def get(i, b):
                        if h0 == 4 and b == 0:
                            h = h0 + i // 2
                            return WIN[:, h:h + 5:4, (CMP_LEN - 1 + P * (1 - i % 2)):2 * P:CMP_STRIDE]
                        h = h0 + i // 2
                        return WIN[:, h:h + 5:4, (1 - i % 2) * P:2 * P]
                    return get

                def head_window(i, b):
                    return WIN[:, i // 2, (1 - i % 2) * P:2 * P].unsqueeze(1).broadcast_to([P, 2, (i % 2 + 1) * P])

                o = attention(L + "A", "A", 64 ** -0.5, head_window, lam=LAM[:, 5, l:l + 1])
                for i in range(6, 8):
                    wait_evicted(dve, o[i])
                group_norm(L + "A.norm", P)
                link(v_.tensor_scalar(OT, OT, vec(f"subln{l}", 1), 1.0 - LAM_INIT[l], ALU.mult, ALU.mult))
                v_.tensor_tensor(OT, OT, TMP[:].rearrange("p a (b t) -> p (a b) t", t=T), ALU.mult).then_inc(normed, 1)
                merge(L + "A.out", 0)
                wait_evicted(dve, w0 + sum(x[3] for x in WIN2[:12]) - 1)
                attention(L + "B", "B", 64 ** -0.5, pair_window(4))
                merge(L + "B.out", 1)
                attention(L + "C", "C", 64 ** -0.5, pair_window(12), sinks=vec(f"sinks{l}", 8))
                merge(L + "C.out", 2)
                add_to_x(L + "wout", 1.0)
                ffn(L + "ffn2", vec(f"norm_g{l}2", DK))
                norm(first[L + "ple.norm"], X[:], DK, vec(f"norm_g{l}3", DK), U[:])
                for m in range(DK):
                    wait_evicted(dve, first[L + "ple.gate"] + m)
                    link(v_.tensor_tensor(GATE[:, DK + m, :], GATE[:, DK + m, :], PLE[:, m, :], ALU.mult))
                    link(v_.tensor_tensor(X[:, m, :], X[:, m, :], GATE[:, DK + m, :], ALU.add))
            norm(first["2.final.norm"], X[:], DK, vec("final2", DK), U[:], done=result_ready)


_WEIGHTS = ["w_ffn1_in", "w_ffn1_out", "w_in", "w_uq", "w_uk", "w_uv", "w_o_mla", "w_o_hg", "w_mem_kv", "w_o_mem",
            "w_out", "w_ffn2_in", "w_ffn2_out", "ffn1_wi_2", "ffn1_wo_2", "w_in_2", "nsa_cmp_w1_2", "nsa_cmp_w2_2",
            "w_branch_2", "w_out_2", "ffn2_wi_2", "ffn2_wo_2", "w_ple_2", "w_ple_gate_2"]


def kernel(**inputs):
    import concourse.bacc as _bacc
    from concourse.bass_utils import run_bass_kernel_spmd as _run

    arrays = {name: np.ascontiguousarray(inputs[name]) for name in _WEIGHTS}
    arrays["cst"] = constants()[0]
    arrays["vec"] = pack_vectors(inputs)
    arrays["xT"] = np.ascontiguousarray(np.asarray(inputs["x"])[0].T)
    arrays["memT"] = np.ascontiguousarray(np.asarray(inputs["mem"])[0].T)
    arrays["pT"] = np.ascontiguousarray(np.asarray(inputs["p_2"])[:, 0].transpose(0, 2, 1))
    arrays["pos"] = np.ascontiguousarray(np.broadcast_to(np.asarray(inputs["positions"]), (ROPE, T)))

    nc = _bacc.Bacc("TRN2", target_bir_lowering=False, num_devices=1)
    w = {name: nc.dram_tensor(f"in_{name}", a.shape, mybir.dt.from_np(a.dtype), kind="ExternalInput").ap()
         for name, a in arrays.items()}
    out = nc.dram_tensor("out_xT", [D, T], FP, kind="ExternalOutput").ap()
    scratch_rows = nc.dram_tensor("bias_rows", [P, BIAS_H, 2 * T], FP, kind="Internal").ap()
    build(nc, w, VECS, out, scratch_rows)
    r = _run(nc, [{f"in_{name}": a for name, a in arrays.items()}], core_ids=[0])
    return np.ascontiguousarray(r.results[0]["out_xT"].T).reshape(1, T, D)
```

```python
import numpy as np
import concourse.bass as bass
from concourse import mybir
from concourse.alu_op_type import AluOpType as ALU
from contextlib import ExitStack

FP = mybir.dt.float32
FR = mybir.dt.float32r
I32 = mybir.dt.int32
ACT = mybir.ActivationFunctionType
AX = mybir.AxisListType

P = 128
T = 256
NT = T // P
D = 1024
DK = D // P
FF = 2816
FK = FF // P
DEPTH = 2
EPS = 1e-6
NEG = -1e30

MLA_H, NOPE, ROPE = 8, 64, 32
QK = NOPE + ROPE
Q_LORA, KV_LORA = 384, 256
HG_H, CHUNK = 4, 64
MEM_H = 4
LEVELS = 8
A_H = 4
N_CMP, CMP_STRIDE, CMP_LEN = 15, 16, 32
BUCKETS, BIAS_H = 32, 20

LAM_INIT = [0.8 - 0.6 * float(np.exp(-0.3 * l)) for l in range(DEPTH)]
TURN = (6.28125, 0.001934051513671875, 2.0 * float(np.pi) - 6.28125 - 0.001934051513671875)
NORMED_1 = DEPTH * (2 * DK + 3 + 2 + 1) + DK

BANKS = 8
SLOTS = 4
SLOT = 2048

C_Q, C_KV, C_KR, C_HQ, C_HF, C_HI, C_HG, C_MQ, C_GATE = 0, 384, 640, 672, 1184, 1696, 2208, 2720, 3232
(D_AQ, D_AK, D_AV, D_BQ, D_BKC, D_BVC, D_BKS, D_BVS, D_BKW, D_BVW, D_BG, D_CQ, D_CK, D_CV,
 D_GATE) = (0, 512, 1024, 1536, 2048, 2176, 2304, 2432, 2560, 2688, 2816, 2840, 3352, 3480, 3608)


def blocks(qt):
    return min(N_CMP, ((qt + 1) * P - CMP_LEN) // CMP_STRIDE + 1)


class Tally:

    def __init__(self):
        self.n = {}

    def add(self, name, k=1):
        before = self.n.get(name, 0)
        self.n[name] = before + k
        return before


def constants():
    parts, at, n = [], {}, 0

    def put(name, a):
        nonlocal n
        full = np.zeros((P, a.shape[1]), np.float32)
        full[:a.shape[0]] = a
        parts.append(full)
        at[name] = n
        n += a.shape[1]

    put("ident", np.eye(P, dtype=np.float32))
    put("ones", np.ones((P, P), np.float32))
    s, t = np.arange(P)[:, None], np.arange(P)[None, :]
    put("pair0", (s == t).astype(np.float32))
    for l in range(LEVELS - 1):
        put(f"pair{l + 1}", ((s >> (l + 1) == t >> (l + 1)) & (s >> l & 1 == 0) & (t >> l & 1 == 1)).astype(np.float32))
    j = np.arange(2 * P)[None, :]
    put("causal", np.where(s - j + P >= 0, 0.0, NEG).astype(np.float32))
    swap = np.zeros((P, ROPE), np.float32)
    for i in range(ROPE // 2):
        swap[64 + ROPE // 2 + i, i] = -1.0
        swap[64 + i, ROPE // 2 + i] = 1.0
    put("swap", swap)
    freq = np.zeros((P, 1), np.float32)
    inv = (np.float32(10000.0) ** (-np.arange(0, ROPE, 2, dtype=np.float32) / np.float32(ROPE))).astype(np.float32)
    freq[64:96, 0] = np.concatenate([inv, inv])
    put("freq", freq)
    i = np.arange(2 * T)
    d = 255 - i
    m = np.maximum(d, 0)
    half = BUCKETS // 2
    large = half + (np.log(np.maximum(m, 1).astype(np.float32) / np.float32(half)) / np.float32(np.log(P / half))
                    * np.float32(BUCKETS - half)).astype(np.int32)
    bucket = np.where(m < half, m, np.minimum(large, BUCKETS - 1))
    hot = np.zeros((BUCKETS + 2, 2 * T), np.float32)
    hot[bucket, i] = 1.0
    hot[BUCKETS] = np.where(d < 0, NEG, 0.0)
    hot[BUCKETS + 1] = np.where((d >= P), NEG, 0.0)
    put("hot", hot)
    rows = np.zeros((2, BIAS_H), np.float32)
    rows[0] = 1.0
    rows[1, 12:] = 1.0
    mask_rows = np.zeros((P, BIAS_H), np.float32)
    mask_rows[BUCKETS:BUCKETS + 2] = rows
    put("mask_rows", mask_rows)
    put("eps", np.full((P, 1), EPS, np.float32))
    put("sees", (np.arange(P) >= CMP_LEN - 1).astype(np.float32)[:, None])
    return np.concatenate(parts, axis=1), at


def constant_places():
    return constants()[1]


VECS = {}


def pack_vectors(v):
    parts, n = [], 0

    def put(name, a):
        nonlocal n
        a = np.asarray(a, np.float32)
        full = np.zeros((P, a.shape[1]), np.float32)
        full[:a.shape[0]] = a
        parts.append(full)
        VECS[name] = n
        n += a.shape[1]

    def cols(a):
        return np.asarray(a).reshape(-1, P).T

    for l in range(DEPTH):
        for name in ("ffn1_norm", "mix_norm", "q_lat_norm", "kv_lat_norm", "hg_out_norm", "mem_norm", "ffn2_norm"):
            put(f"{name}{l}", cols(v[name][l]))
        for k in range(4):
            put(f"norm_g{l}{k}", cols(v["norm_g_2"][l, k]))
        put(f"subln{l}", cols(v["diff_subln_2"][l]))
        put(f"lambda{l}", np.broadcast_to(np.asarray(v["diff_lambda_2"][l]).reshape(1, 256), (P, 256)))
        put(f"sinks{l}", np.broadcast_to(np.asarray(v["swa_sinks_2"][l]).reshape(1, 2, 4).transpose(0, 2, 1).reshape(1, 8), (P, 8)))
        for kv in range(2):
            put(f"pos{l}{kv}", np.asarray(v["nsa_cmp_pos_2"][l, kv]).reshape(16, P).T)
        put(f"lb{l}", cols(v["hg_lower_bounds"][l]))
    put("rel_bias", np.asarray(v["rel_bias_2"]))
    put("final1", cols(v["final_norm"]))
    put("final2", cols(v["final_norm_2"]))
    return np.concatenate(parts, axis=1)


class Plan:

    def __init__(self):
        self.first = {}
        self.total = 0
        self.slab_first = {}
        self.slab_last = []
        self.slab_in = []

    def products(self, name, n):
        self.first[name] = self.total
        self.total += n

    def slab(self, last, dmas=1):
        before = self.slab_in[-SLOTS] if len(self.slab_in) >= SLOTS else 0
        self.slab_in.append(before + 16 * dmas)
        self.slab_last.append(last)

    def slabs(self, name, per_slab, dmas=1):
        if name not in self.first:
            self.products(name, 0)
            self.slab_first[name] = len(self.slab_last)
        for n in per_slab:
            self.total += n
            self.slab(self.total - 1 if n else self.total, dmas)


WIN1 = ([(c + 256 * i, 256, 2) for c in (C_HQ, C_HF) for i in range(2)]
        + [(C_Q, 256, 2), (C_Q + 256, 128, 1), (C_KV, 256, 2), (C_KR, 32, 1)]
        + [(c + 256 * i, 256, 2) for c in (C_HI, C_HG, C_MQ) for i in range(2)])
PAIRS_AFTER = len(WIN1) - LEVELS
LATENTS_AFTER = 9
WIN2 = ([("tiles", c + 256 * i, 256, 2) for c in (D_AQ, D_AK) for i in range(2)]
        + [("tokens", D_AV + 256 * i, 256, 2) for i in range(2)]
        + [("pairs", D_BQ + 128 * i, 256, 2) for i in range(2)]
        + [("shift", D_BKC, 256, 2), ("kv", D_BKS, 256, 2), ("kv", D_BKW, 256, 2), ("gate", D_BG, 24, 1)]
        + [("pairs", D_CQ + 128 * i, 256, 2) for i in range(2)]
        + [("kv", D_CK, 256, 2)])
CMP_AFTER = 11
BRANCH = {"mla": 0, "hg": 1, "mem": 2, "A": 0, "B": 1, "C": 2}
ATTN = {"mla": (8, 1, 1, 1), "mem": (4, 1, 1, 1), "A": (8, 2, 1, 1), "B": (8, 6, 3, 3), "C": (8, 2, 1, 1)}


def attention_numbers(first, kind):
    units, n_s, n_t, _ = ATTN[kind]
    n_f = DK // units
    s, t, f, o, n = [0] * units, [0] * units, [0] * units, [0] * units, first
    for i in range(-2, units):
        if i >= 0:
            t[i] = n
            n += n_t
        if i + 2 < units:
            s[i + 2] = n
            n += n_s
        if i >= 0:
            f[i] = n
            n += n_f
            o[i] = n
            n += 1
    return s, t, f, o, n - first


def make_plan():
    pl = Plan()

    def ffn(name):
        pl.products(name + ".norm", 1)
        pl.slabs(name + ".in", [2] * FK, dmas=2)
        pl.slabs(name + ".out", [0, 1] * DK)

    def attention(name, kind):
        _, _, f, _, n = attention_numbers(pl.total, kind)
        pl.slab_first[name] = len(pl.slab_last)
        for m in range(1, DK, 2):
            pl.slab(f[m * ATTN[kind][0] // DK] + m % (DK // ATTN[kind][0]))
        pl.products(name, n)

    for l in range(DEPTH):
        L = f"1.{l}."
        ffn(L + "ffn1")
        pl.products(L + "mix.norm", 1)
        for i, (_, _, n) in enumerate(WIN1):
            pl.slabs(L + f"win{i}", [n])
            if i == LATENTS_AFTER:
                pl.products(L + "latent.norm", 2)
            if i >= PAIRS_AFTER:
                pl.products(L + f"pairs{i - PAIRS_AFTER}", 2)
        if l == 0:
            pl.products("bias", 1)
        pl.slabs(L + "uq", [4, 4])
        pl.products(L + f"pairs{LEVELS}", 1)
        pl.slabs(L + "uk", [8])
        pl.slabs(L + "uv", [2])
        pl.products(L + "swap", 5)
        pl.products(L + "hg.o", 2)
        pl.slabs(L + "hg.gate0", [2] * 2)
        pl.products(L + "hg.norm", 2)
        pl.slabs(L + "hg.gate1", [2] * 2)
        pl.slabs(L + "hg.out", [4, 4])
        attention(L + "mla", "mla")
        pl.products(L + "mem.norm", 1)
        pl.slabs(L + "mla.out", [4, 4])
        pl.slabs(L + "mem.kv", [2] * 4)
        attention(L + "mem", "mem")
        pl.slabs(L + "mem.out", [4, 4])
        pl.slabs(L + "wout", [2] * 4)
        ffn(L + "ffn2")
    pl.products("1.final.norm", 1)
    for l in range(DEPTH):
        L = f"2.{l}."
        ffn(L + "ffn1")
        pl.products(L + "mix.norm", 1)
        for i, (kind, _, _, n) in enumerate(WIN2):
            pl.slabs(L + f"win{i}", [n], dmas=2 if kind == "pairs" else 1)
            if i == CMP_AFTER:
                pl.slabs(L + "cmp", [0, 1, 0, 1])
        pl.slabs(L + "cmp2", [2], dmas=2)
        attention(L + "A", "A")
        pl.products(L + "A.norm", 2)
        pl.slabs(L + "A.out", [4, 4])
        attention(L + "B", "B")
        pl.slabs(L + "B.out", [4, 4], dmas=2)
        attention(L + "C", "C")
        pl.slabs(L + "C.out", [4, 4], dmas=2)
        pl.slabs(L + "wout", [2] * 4)
        ffn(L + "ffn2")
        pl.products(L + "ple.norm", 1)
        pl.slabs(L + "ple.p", [8])
        pl.slabs(L + "ple.gate", [2] * 4)
    pl.products("2.final.norm", 1)
    return pl


def build(nc, w, vec_places, out, scratch_rows):
    pl = make_plan()
    first, slab_first = pl.first, pl.slab_first
    cst = constant_places()
    n_cst, n_vec = w["cst"].shape[1], w["vec"].shape[1]
    block1 = [f"1.{l}." for l in range(DEPTH)]
    block2 = [f"2.{l}." for l in range(DEPTH)]

    ctx = ExitStack()
    with ctx:
        def sb(name, shape, dt=FP):
            return ctx.enter_context(nc.sbuf_tensor(name, shape, dt))

        def sem(name):
            return ctx.enter_context(nc.semaphore(name))

        cst_sb = sb("cst_sb", [P, n_cst])
        vec_sb = sb("vec_sb", [P, n_vec])
        X = sb("X", [P, DK, T])
        U = sb("U", [P, DK, T])
        SQ = sb("SQ", [P, DK, T])
        RING = sb("RING", [P, SLOTS, SLOT])
        V = sb("V", [P, T])
        RSTD = sb("RSTD", [P, T])
        COS = sb("COS", [P, T])
        SIN = sb("SIN", [P, T])
        SILU = sb("SILU", [P, 2, T])
        TMP = sb("TMP", [P, 2, 512])
        LB = sb("LB", [P, 6, HG_H])
        LAM = sb("LAM", [P, 6, DEPTH])
        TAB = sb("TAB", [P, BIAS_H])
        MX = sb("MX", [P, 2, 3, 2])
        SUM = sb("SUM", [P, 2, 3, 2])
        region_base = (nc.sbuf_base + 31) // 32 * 32
        REGION = sb("REGION", [P, 31600])
        used = [0]

        def region(*shape):
            n = int(np.prod(shape))
            a = REGION[:, used[0]:used[0] + n]
            used[0] += n
            assert used[0] <= 31600, used[0]
            if len(shape) == 2:
                return a.rearrange("p (a b) -> p a b", b=shape[1])
            if len(shape) == 3:
                return a.rearrange("p (a b c) -> p a b c", b=shape[1], c=shape[2])
            if len(shape) == 4:
                return a.rearrange("p (a b c d) -> p a b c d", b=shape[1], c=shape[2], d=shape[3])
            return a

        def overlay(name, shape, at):
            return nc.alloc_sbuf_tensor_at(name, shape, FR, offset=region_base + 4 * at)

        UH, UL = overlay("UH", [P, DK, T], 0), overlay("UL", [P, DK, T], DK * T)
        HH, HL = overlay("HH", [P, FK, T], 2 * DK * T), overlay("HL", [P, FK, T], (2 * DK + FK) * T)
        w_at = (2 * DK + 2 * FK) * T
        WH, WL = overlay("WH", [P, 2, SLOT], w_at), overlay("WL", [P, 2, SLOT], w_at + 2 * SLOT)
        HF = SQ[:, 0:2, :]
        ACC, SQX = SQ[:, DK - 1, :], SQ[:, DK - 2, :]
        used[0] = 0
        GATE = region(3 * DK, T)
        MRG = region(DK, T)
        OT = region(4, T)
        PT = region(3, 2, 512)
        S = region(3, 2, 2, 260)
        both = used[0]
        used[0] = both - 3 * 2 * 2 * 260 - 2 * 2 * 512
        MK, MV = region(4, T), region(NT, 512)
        used[0] = both - 2 * 2 * 2 * 260
        Z, HK = region(HG_H * T), region(HG_H * T)
        used[0] = both
        CQ, CKV = region(3, T), region(2, T)
        QH, KH = region(MLA_H, T), region(MLA_H, T)
        VM = region(NT, 512)
        MQ = region(4, T)
        HQ, HGT, VH = region(HG_H, T), region(HG_H, T), region(NT, 512)
        GS = region(HG_H * T)
        HX = region(2, HG_H * T)
        MEM = HX.rearrange("p a (b t) -> p (a b) t", t=T)
        AT = region(HG_H, 3, P)
        KR = SILU
        used[0] = both
        AQ, AK, AV = region(4, T), region(4, T), region(NT, 512)
        BQ, CQ2 = region(4, T), region(4, T)
        KC2, VC2 = region(2, T), region(2, T)
        BKS, BKW, CK2 = region(T), region(T), region(T)
        BVS, BVW, CV2 = region(NT, P), region(NT, P), region(NT, P)
        BG = region(NT, 24)
        BLK = region(16, 30)
        GX, GY, HID, HID2 = region(2, 30), region(2, 30), region(2, 30), region(2, 30)
        BLK2 = region(16, 30)
        KCMP, VCMP = region(16), region(2, 64)
        WIN = region(BIAS_H, T)
        PLE = GATE[:, 0:DK]
        PIN = region(2, T)

        ps = ctx.enter_context(nc.psum_tensor("ps", [P, BANKS, 512], FP))
        RESET = sb("RESET", [P, HG_H * T])
        ROWS = sb("ROWS", [P, 512])

        product_done = sem("product_done")
        evicted = [sem(f"evicted{b}") for b in range(BANKS)]
        weights_in = [sem(f"weights_in{i}") for i in range(SLOTS)]
        inputs_in = sem("inputs_in")
        mem_in = sem("mem_in")
        layer_in = sem("layer_in")
        windows_in = sem("windows_in")
        scratch_out = sem("scratch_out")
        result_out = sem("result_out")
        setup_done = sem("setup_done")
        angle_ready = sem("angle_ready")
        rope_ready = sem("rope_ready")
        lambda_ready = sem("lambda_ready")
        squares_ready = sem("squares_ready")
        weights_high = sem("weights_high")
        weights_low = sem("weights_low")
        u_full = sem("u_full")
        u_high = sem("u_high")
        u_low = sem("u_low")
        hidden_high = sem("hidden_high")
        hidden_low = sem("hidden_low")
        half_read = sem("half_read")
        mean_ready = sem("mean_ready")
        rstd_ready = sem("rstd_ready")
        normed = sem("normed")
        hidden_ready = sem("hidden_ready")
        max_ready = sem("max_ready")
        exp_done = sem("exp_done")
        probs_ready = sem("probs_ready")
        merged_ready = sem("merged_ready")
        roped = sem("roped")
        hg_vec = sem("hg_vec")
        hg_act = sem("hg_act")
        pair_ready = sem("pair_ready")
        pairs_summed = sem("pairs_summed")
        result_ready = sem("result_ready")
        blocks_ready = sem("blocks_ready")
        gelu_vec = sem("gelu_vec")
        gelu_act = sem("gelu_act")
        vec_step = sem("vec_step")
        act_step = sem("act_step")

        block = ctx.enter_context(nc.Block())

        def con(name, n, rows=slice(0, P)):
            return cst_sb[rows, cst[name]:cst[name] + n]

        def vec(name, n, rows=slice(0, P)):
            return vec_sb[rows, vec_places[name]:vec_places[name] + n]

        def bank(n, *cols):
            return ps[:, n % BANKS, :] if not cols else ps[:, n % BANKS, cols[0]:cols[1]]

        def wait_product(eng, n, r=0):
            eng.wait_ge(product_done, r * BANKS + n + 1)

        def wait_evicted(eng, n, r=0):
            eng.wait_ge(evicted[n % BANKS], r + n // BANKS + 1)

        def wait_room(eng, n, r=0):
            if n >= BANKS or not isinstance(r, int):
                eng.wait_ge(evicted[n % BANKS], r + n // BANKS)

        def wait_weights(eng, s, r=0):
            eng.wait_ge(weights_in[s % SLOTS], r * 32 + pl.slab_in[s])

        def slot(s, kt, width):
            return RING[:, s % SLOTS, 0:kt * width].rearrange("p (k n) -> p k n", n=width)

        def rounds(eng, n, body):
            for j in range(SLOTS):
                body(0, j)
            with eng.Fori(1, n // SLOTS) as r:
                for j in range(SLOTS):
                    body(r, j)
            for j in range(n // SLOTS * SLOTS, n):
                body(0, j)

        def parts(j, kt, width):
            return tuple(x[:, j % 2, 0:kt * width].rearrange("p (k n) -> p k n", n=width) for x in (WH, WL))

        def ffn_words(j):
            return DK * 2 * P if j < FK else FK // 2 * P

        def wide(a, shape):
            return a.broadcast_to(shape)

        @block.sync
        def _(sp):
            sp.dma_start(cst_sb[:], w["cst"]).then_inc(inputs_in, 16)
            sp.dma_start(vec_sb[:], w["vec"]).then_inc(inputs_in, 16)
            sp.dma_start(X[:], w["xT"].rearrange("(k p) t -> p k t", p=P)).then_inc(inputs_in, 16)
            sp.dma_start(COS[64:96, :].bitcast(I32), w["pos"]).then_inc(inputs_in, 16)

            def room(s, r=0):
                if s >= SLOTS:
                    sp.wait_ge(product_done, r * BANKS + pl.slab_last[s - SLOTS] + 1)

            def load(s, *pairs):
                room(s)
                for dst, src in pairs:
                    sp.dma_start(dst, src).then_inc(weights_in[s % SLOTS], 16)

            def rows(a):
                return a.rearrange("(k p) n -> p k n", p=P)

            def ffn(name, wi, wo):
                s0, p0 = slab_first[name + ".in"], first[name + ".in"]

                def pair(r, j):
                    s = s0 + j
                    if isinstance(r, int):
                        room(s)
                    else:
                        sp.wait_ge(product_done, r * BANKS + p0 + 2 * (j - SLOTS) + 2)
                    dst = slot(s, DK, 256)
                    for side in range(2):
                        sp.dma_start(dst[:, :, side * P:(side + 1) * P],
                                     rows(wi[:, bass.ds(r * (SLOTS * P) + (j * P + side * FF), P)]))\
                          .then_inc(weights_in[s % SLOTS], 16)

                rounds(sp, FK, pair)
                for i in range(2 * DK):
                    m, half = i // 2, i % 2
                    k0 = half * (FK // 2)
                    load(slab_first[name + ".out"] + i,
                         (slot(slab_first[name + ".out"] + i, FK // 2, P),
                          rows(wo[k0 * P:(k0 + FK // 2) * P, m * P:(m + 1) * P])))

            def halves(name, a, kt):
                n = a.shape[1] // 2
                for i in range(2):
                    s = slab_first[name] + i
                    load(s, (slot(s, kt, n), rows(a[:, i * n:(i + 1) * n])))

            def quarters(name, a, count=4):
                for i in range(count):
                    s = slab_first[name] + i
                    load(s, (slot(s, DK, 256), rows(a[:, i * 256:(i + 1) * 256])))

            for l, L in enumerate(block1):
                ffn(L + "ffn1", w["w_ffn1_in"][l], w["w_ffn1_out"][l])
                for i, (c, n, _) in enumerate(WIN1):
                    s = slab_first[L + f"win{i}"]
                    load(s, (slot(s, DK, n), rows(w["w_in"][l][:, c:c + n])))
                halves(L + "uq", w["w_uq"][l], 3)
                s = slab_first[L + "uk"]
                load(s, (slot(s, 2, 512), rows(w["w_uk"][l])))
                s = slab_first[L + "uv"]
                load(s, (slot(s, 2, 512), rows(w["w_uv"][l])))
                gate = [w["w_in"][l][:, C_GATE + b * D:C_GATE + (b + 1) * D] for b in range(3)]
                quarters(L + "hg.gate0", gate[1][:, 0:D // 2], 2)
                quarters(L + "hg.gate1", gate[1][:, D // 2:D], 2)
                halves(L + "hg.out", w["w_o_hg"][l], 4)
                quarters(L + "mla", gate[0])
                halves(L + "mla.out", w["w_o_mla"][l], 4)
                quarters(L + "mem.kv", w["w_mem_kv"][l])
                quarters(L + "mem", gate[2])
                halves(L + "mem.out", w["w_o_mem"][l], 4)
                quarters(L + "wout", w["w_out"][l])
                ffn(L + "ffn2", w["w_ffn2_in"][l], w["w_ffn2_out"][l])
            for l, L in enumerate(block2):
                ffn(L + "ffn1", w["ffn1_wi_2"][l], w["ffn1_wo_2"][l])
                wi = w["w_in_2"][l]
                for i, (kind, c, n, _) in enumerate(WIN2):
                    s = slab_first[L + f"win{i}"]
                    dst = slot(s, DK, n)
                    if kind == "pairs":
                        d4 = dst.rearrange("p k (g n) -> p k g n", g=2)
                        load(s, *[(d4[:, :, g, :], rows(wi[:, c + 256 * g:c + 256 * g + P])) for g in range(2)])
                    else:
                        load(s, (dst, rows(wi[:, c:c + n])))
                    if i == CMP_AFTER:
                        for j in range(4):
                            s = slab_first[L + "cmp"] + j
                            load(s, (slot(s, DK, 256), rows(w["nsa_cmp_w1_2"][l, j // 2][j % 2 * D:(j % 2 + 1) * D, :])))
                s = slab_first[L + "cmp2"]
                w2 = slot(s, 4, 64)
                load(s, *[(w2[:, 2 * kv:2 * kv + 2, :], rows(w["nsa_cmp_w2_2"][l, kv])) for kv in range(2)])
                gate = [wi[:, D_GATE + b * D:D_GATE + (b + 1) * D] for b in range(3)]
                quarters(L + "A", gate[0])
                halves(L + "A.out", w["w_branch_2"][l, 0], 4)
                for b, name in ((1, "B"), (2, "C")):
                    quarters(L + name, gate[b])
                    for i in range(2):
                        s = slab_first[L + name + ".out"] + i
                        dst = slot(s, 4, 512)
                        src = w["w_branch_2"][l, b][:, i * 512:(i + 1) * 512].rearrange("(g j d) n -> g d j n", g=2, j=4)
                        load(s, *[(dst[64 * g:64 * g + 64], src[g]) for g in range(2)])
                quarters(L + "wout", w["w_out_2"][l])
                ffn(L + "ffn2", w["ffn2_wi_2"][l], w["ffn2_wo_2"][l])
                s = slab_first[L + "ple.p"]
                load(s, (slot(s, 2, D), rows(w["w_ple_2"][l])))
                quarters(L + "ple.gate", w["w_ple_gate_2"][l])
            sp.wait_ge(result_ready, DK)
            sp.dma_start(out.rearrange("(k p) t -> p k t", p=P), U[:]).then_inc(result_out, 16)
            sp.wait_ge(result_out, 16)

        @block.gpsimd
        def _(pool):
            for l, L in enumerate(block1):
                wait_product(pool, first[L + f"pairs{LEVELS}"])
                pool.dma_start(HX, w["memT"].rearrange("(k p) t -> p k t", p=P)).then_inc(mem_in, 16)
                if l == 0:
                    wait_evicted(pool, first["bias"])
                    pool.dma_start(scratch_rows.rearrange("r h i -> h r i"),
                                   ROWS[0:BIAS_H, :].unsqueeze(1).broadcast_to([BIAS_H, P, 2 * T])).then_inc(scratch_out, 16)
            pool.wait_ge(scratch_out, 16)
            wait_product(pool, first["1.final.norm"])
            wins = bass.AP(tensor=scratch_rows.tensor, offset=P - 1, ap=[[BIAS_H * 2 * T - 1, P], [2 * T, BIAS_H], [1, T]])
            for l, L in enumerate(block2):
                wait_product(pool, first[L + "mix.norm"])
                if l == 0:
                    pool.dma_start(WIN, wins).then_inc(windows_in, 16)
                wait_product(pool, first[L + "ple.norm"])
                pool.dma_start(PIN, w["pT"][l].rearrange("(k p) t -> p k t", p=P)).then_inc(layer_in, 16)

        @block.tensor
        def _(pe):
            tally = Tally()
            ones = con("ones", P)
            ident = con("ident", P)

            def product(n, groups, after=None):
                wait_room(pe, n)
                for o, terms in groups:
                    for i, (a, b) in enumerate(terms):
                        last = nc.tensor.matmul(o, a, b, start=i == 0, stop=i == len(terms) - 1)
                last.then_inc(product_done, 1)

            def norm(n, k0, kt):
                pe.wait_ge(squares_ready, tally.add("squares_ready") + 1)
                tally.add("normed", kt)
                product(n, [(bank(n, 0, T), [(ones, SQ[:, k0 + k, :]) for k in range(kt)])])

            def norm_x(n, tiles=DK):
                pe.wait_ge(squares_ready, tally.add("squares_ready") + 1)
                tally.add("normed", tiles)
                product(n, [(bank(n, 0, T), [(ones, ACC)])])

            def ffn(name):
                norm_x(first[name + ".norm"], 0)
                s0, p0 = slab_first[name + ".in"], first[name + ".in"]
                u = tally.add("u", DK)
                hidden = tally.add("hidden", FK)
                slabs = tally.add("weights_low", FK + 2 * DK)

                def pair(r, j):
                    wh, wl = parts(j, DK, 256)
                    peeled = isinstance(r, int) and j == 0
                    pe.wait_ge(weights_high, r * SLOTS + slabs + j + 1)
                    if not peeled:
                        pe.wait_ge(weights_low, r * SLOTS + slabs + j + 1)
                    for side in range(2):
                        n = p0 + 2 * j + side
                        wait_room(pe, n, r)
                        terms = [(a, b) for a, b in ((wh, UH), (wl, UH), (wh, UL))]
                        for i, (a, b) in enumerate(terms):
                            if peeled and side == 0 and i == 1:
                                pe.wait_ge(weights_low, slabs + 1)
                            for k in range(DK):
                                if peeled and side == 0 and i != 1:
                                    pe.wait_ge(u_high if i == 0 else u_low, u + k + 1)
                                last = nc.tensor.matmul(bank(n, 0, T), a[:, k, side * P:(side + 1) * P], b[:, k, :],
                                                        start=i == 0 and k == 0, stop=i == 2 and k == DK - 1)
                        last.then_inc(product_done, 1)

                rounds(pe, FK, pair)
                for m in range(DK):
                    n = first[name + ".out"] + m
                    wait_room(pe, n)
                    for half in range(2):
                        j = FK + 2 * m + half
                        wh, wl = parts(j, FK // 2, P)
                        pe.wait_ge(weights_low, slabs + j + 1)
                        for k in range(FK // 2):
                            kk = half * (FK // 2) + k
                            if m == 0:
                                pe.wait_ge(hidden_low, hidden + kk + 1)
                            for a, b in ((wh, HH), (wl, HH), (wh, HL)):
                                last = nc.tensor.matmul(bank(n, 0, T), a[:, k, :], b[:, kk, :],
                                                        start=kk == 0 and a is wh and b is HH, stop=kk == FK - 1 and b is HL)
                        last.then_inc(half_read if half == 0 else product_done, 1)

            def halves(name, kt, act, waits):
                for n in waits:
                    wait_evicted(pe, n)
                for i in range(2):
                    s = slab_first[name] + i
                    wait_weights(pe, s)
                    for m in range(4):
                        n = first[name] + 4 * i + m
                        product(n, [(bank(n, 0, T),
                                     [(slot(s, kt, 512)[:, k, m * P:(m + 1) * P], act[:, k, :]) for k in range(kt)])])

            def quarters(name, act, count=4):
                for i in range(count):
                    s = slab_first[name] + i
                    wait_weights(pe, s)
                    for m in range(2):
                        n = first[name] + 2 * i + m
                        product(n, [(bank(n, 0, T),
                                     [(slot(s, DK, 256)[:, k, m * P:(m + 1) * P], act[:, k, :]) for k in range(DK)])])

            def tokens(n, parts, act, kt):
                product(n, [(o, [(act[:, k, tt * P:(tt + 1) * P], wk(k)) for k in range(kt)]) for o, wk, tt in parts])

            def attention(name, kind, scores, values):
                units, n_s, n_t, n_b = ATTN[kind]
                s, t, f, o, _ = attention_numbers(first[name], kind)
                base = tally.add("probs_ready", units)
                for i in range(-2, units):
                    if i >= 0:
                        pe.wait_ge(probs_ready, base + i + 1)
                        qt, par = i % 2, i % 2
                        for b in range(n_t):
                            groups = 1 if kind == "A" else 2
                            cmp = kind == "B" and b == 0
                            keys = [(0, blocks(qt))] if cmp else [(k * P, P) for k in range(NT if kind == "mem" else qt + 1)]
                            gr = []
                            for g in range(groups):
                                for k, (k0, kn) in enumerate(keys):
                                    c = (g * len(keys) + k) * P
                                    gr.append((S[:, b, par, g, k0:k0 + kn], bank(t[i] + b)[0:kn, c:c + P]))
                            wait_room(pe, t[i] + b)
                            for src, dst in gr:
                                last = nc.tensor.transpose(dst, src, ident)
                            last.then_inc(product_done, 1)
                    if i + 2 < units:
                        for b, groups in enumerate(scores(i + 2)):
                            if n_s == n_b:
                                n = s[i + 2] + b
                                product(n, [(bank(n)[:, g * T:g * T + k.shape[-1]], [(q, k)]) for g, (q, k) in enumerate(groups)])
                            else:
                                for g, (q, k) in enumerate(groups):
                                    n = s[i + 2] + 2 * b + g
                                    product(n, [(bank(n, 0, k.shape[-1]), [(q, k)])])
                    if i >= 0:
                        for j in range(DK // units):
                            m = i * (DK // units) + j
                            sl = slab_first[name] + m // 2
                            wait_weights(pe, sl)
                            product(f[i] + j, [(bank(f[i] + j, 0, T),
                                                [(slot(sl, DK, 256)[:, k, m % 2 * P:(m % 2 + 1) * P], U[:, k, :]) for k in range(DK)])])
                        for b in range(n_t):
                            wait_evicted(pe, t[i] + b)
                        wait_room(pe, o[i])
                        for rows, c, terms in values(i):
                            for j, (v, b, c0, kn) in enumerate(terms):
                                last = nc.tensor.matmul(bank(o[i])[rows, c:c + P], v, PT[0:kn, b, par, c0:c0 + P],
                                                        start=j == 0, stop=j == len(terms) - 1)
                        last.then_inc(product_done, 1)

            pe.wait_ge(inputs_in, 64)
            for l, L in enumerate(block1):
                ffn(L + "ffn1")
                norm_x(first[L + "mix.norm"])
                pe.wait_ge(normed, tally.n["normed"])
                def pairs(level):
                    pe.wait_ge(pair_ready, l * (LEVELS + 1) + level + 1)
                    if level == 0:
                        left, right = HK.rearrange("p (h t) -> p h t", t=T), HQ
                    else:
                        left = right = HX[:, (level - 1) % 2, :].rearrange("p (h t) -> p h t", t=T)
                    for tt in ((0, 1) if level < LEVELS else (0,)):
                        n = first[L + f"pairs{level}"] + tt
                        q = slice(tt * P, tt * P + P) if level < LEVELS else slice(P, 2 * P)
                        product(n, [(bank(n, h * P, h * P + P), [(left[:, h, tt * P:tt * P + P], right[:, h, q])])
                                    for h in range(HG_H)])

                for i, (c, width, count) in enumerate(WIN1):
                    n, s = first[L + f"win{i}"], slab_first[L + f"win{i}"]
                    wait_weights(pe, s)
                    wv = slot(s, DK, width)
                    for m in range(count):
                        if C_HI <= c < C_HG:
                            tokens(n + m, [(bank(n + m, 0, 256), lambda k: wv[:, k, :], m)], U, DK)
                        elif c == C_KR:
                            product(n, [(bank(n)[64:96, 0:T], [(wv[:, k, :], U[:, k, :]) for k in range(DK)])])
                        else:
                            product(n + m, [(bank(n + m, 0, T), [(wv[:, k, m * P:(m + 1) * P], U[:, k, :]) for k in range(DK)])])
                    if i == LATENTS_AFTER:
                        norm(first[L + "latent.norm"], 0, 3)
                        norm(first[L + "latent.norm"] + 1, 3, 2)
                    if i >= PAIRS_AFTER:
                        pairs(i - PAIRS_AFTER)
                if l == 0:
                    pe.wait_ge(setup_done, 1)
                    n = first["bias"]
                    hot = con("hot", 2 * T, slice(0, BUCKETS + 2))
                    product(n, [(bank(n)[0:BIAS_H, :], [(TAB[0:BUCKETS + 2, :], hot)])])
                pe.wait_ge(normed, tally.n["normed"] - 2)
                for i in range(2):
                    s = slab_first[L + "uq"] + i
                    wait_weights(pe, s)
                    for m in range(4):
                        n = first[L + "uq"] + 4 * i + m
                        product(n, [(bank(n)[0:QK, 0:T], [(slot(s, 3, 384)[:, k, m * QK:(m + 1) * QK], CQ[:, k, :]) for k in range(3)])])
                pairs(LEVELS)
                pe.wait_ge(normed, tally.n["normed"])
                s = slab_first[L + "uk"]
                wait_weights(pe, s)
                for m in range(MLA_H):
                    n = first[L + "uk"] + m
                    product(n, [(bank(n)[0:NOPE, 0:T], [(slot(s, 2, 512)[:, k, m * NOPE:(m + 1) * NOPE], CKV[:, k, :]) for k in range(2)])])
                s = slab_first[L + "uv"]
                wait_weights(pe, s)
                for m in range(NT):
                    tokens(first[L + "uv"] + m, [(bank(first[L + "uv"] + m), lambda k: slot(s, 2, 512)[:, k, :], m)], CKV, 2)
                swap = con("swap", ROPE, slice(64, 96))
                for h in range(MLA_H):
                    wait_evicted(pe, first[L + "uq"] + h)
                for m in range(4):
                    n = first[L + "swap"] + m
                    product(n, [(bank(n)[64:96, :], [(swap, QH[64:96, 2 * m:2 * m + 2, :])])])
                n = first[L + "swap"] + 4
                product(n, [(bank(n)[64:96, 0:T], [(swap, KR[64:96, 0, :])])])
                pe.wait_ge(pairs_summed, l + 1)
                for i in range(2):
                    n = first[L + "hg.o"] + i
                    wait_room(pe, n)
                    for g in range(2):
                        h = 2 * i + g
                        nc.tensor.matmul(bank(n, g * T, g * T + T), VH[:, 0, h * P:h * P + P], AT[:, h, 0:2, :], start=True, stop=False)
                        last = nc.tensor.matmul(bank(n, g * T + P, g * T + T), VH[:, 1, h * P:h * P + P], AT[:, h, 2, :], start=False, stop=True)
                    last.then_inc(product_done, 1)
                quarters(L + "hg.gate0", U, 2)
                pe.wait_ge(squares_ready, tally.add("squares_ready") + 1)
                for i in range(2):
                    n = first[L + "hg.norm"] + i
                    product(n, [(bank(n), [(ones, SQ[:, 2 * i:2 * i + 2, :])])])
                quarters(L + "hg.gate1", U, 2)
                tally.add("normed", 1)
                pe.wait_ge(normed, tally.n["normed"])
                halves(L + "hg.out", 4, OT, [])
                pe.wait_ge(roped, l + 1)
                for m in range(MLA_H):
                    wait_evicted(pe, first[L + "uk"] + m)
                for m in range(NT):
                    wait_evicted(pe, first[L + "uv"] + m)
                attention(L + "mla", "mla",
                          lambda i: [[(QH[0:QK, h, i % 2 * P:(i % 2 + 1) * P], KH[0:QK, h, 0:(i % 2 + 1) * P])
                                      for h in (i // 2 * 2, i // 2 * 2 + 1)]],
                          lambda i: [(slice(64 * g, 64 * g + 64), 0,
                                      [(VM[:, k, (i // 2 * 2 + g) * 64:(i // 2 * 2 + g + 1) * 64], 0, (g * (i % 2 + 1) + k) * P, P)
                                       for k in range(i % 2 + 1)]) for g in range(2)])
                norm(first[L + "mem.norm"], 0, DK)
                halves(L + "mla.out", 4, OT, attention_numbers(first[L + "mla"], "mla")[3])
                pe.wait_ge(normed, tally.n["normed"])
                for i in range(4):
                    s = slab_first[L + "mem.kv"] + i
                    wait_weights(pe, s)
                    wv = slot(s, DK, 256)
                    for m in range(2):
                        n = first[L + "mem.kv"] + 2 * i + m
                        if i < 2:
                            product(n, [(bank(n, 0, T), [(wv[:, k, m * P:(m + 1) * P], MEM[:, k, :]) for k in range(DK)])])
                        else:
                            tokens(n, [(bank(n, 0, 256), lambda k: wv[:, k, :], m)], MEM, DK)
                for m in range(8):
                    wait_evicted(pe, first[L + "mem.kv"] + m)
                attention(L + "mem", "mem",
                          lambda i: [[(MQ[:, h, i % 2 * P:(i % 2 + 1) * P], MK[:, h, :]) for h in (i // 2 * 2, i // 2 * 2 + 1)]],
                          lambda i: [(slice(0, P), g * P,
                                      [(MV[:, k, (i // 2 * 2 + g) * P:(i // 2 * 2 + g + 1) * P], 0, (g * 2 + k) * P, P) for k in range(2)])
                                     for g in range(2)])
                halves(L + "mem.out", 4, OT, attention_numbers(first[L + "mem"], "mem")[3])
                pe.wait_ge(merged_ready, tally.add("merged_ready", 1) + 1)
                quarters(L + "wout", MRG)
                ffn(L + "ffn2")
            norm_x(first["1.final.norm"])

            for l, L in enumerate(block2):
                ffn(L + "ffn1")
                norm_x(first[L + "mix.norm"])
                pe.wait_ge(normed, tally.n["normed"])
                for i, (kind, c, width, count) in enumerate(WIN2):
                    n, s = first[L + f"win{i}"], slab_first[L + f"win{i}"]
                    wait_weights(pe, s)
                    wv = slot(s, DK, width)
                    if kind == "tiles":
                        for m in range(2):
                            product(n + m, [(bank(n + m, 0, T), [(wv[:, k, m * P:(m + 1) * P], U[:, k, :]) for k in range(DK)])])
                    elif kind == "pairs":
                        w5 = wv.rearrange("p k (g j d) -> p k j g d", g=2, j=2)
                        for m in range(2):
                            product(n + m, [(bank(n + m)[64 * g:64 * g + 64, 0:T], [(w5[:, k, m, g, :], U[:, k, :]) for k in range(DK)])
                                            for g in range(2)])
                    elif kind == "tokens":
                        for m in range(NT):
                            tokens(n + m, [(bank(n + m, 0, 256), lambda k: wv[:, k, :], m)], U, DK)
                    elif kind == "gate":
                        tokens(n, [(bank(n, 24 * m, 24 * m + 24), lambda k: wv[:, k, :], m) for m in range(NT)], U, DK)
                    elif kind == "kv":
                        product(n, [(bank(n, 0, T), [(wv[:, k, 0:P], U[:, k, :]) for k in range(DK)])])
                        tokens(n + 1, [(bank(n + 1, P * m, P * m + P), lambda k: wv[:, k, P:2 * P], m) for m in range(NT)], U, DK)
                    elif kind == "shift":
                        for m in range(2):
                            product(n + m, [(bank(n + m)[64 * half:64 * half + 64, g * T:(g + 1) * T],
                                             [(wv[:, k, m * P + 64 * g:m * P + 64 * g + 64], U[:, k, :]) for k in range(DK)])
                                            for half in range(2) for g in range(2)])
                    if i == CMP_AFTER:
                        for kv in range(2):
                            pe.wait_ge(blocks_ready, 2 * l + kv + 1)
                            n, s = first[L + "cmp"] + kv, slab_first[L + "cmp"] + 2 * kv
                            wait_weights(pe, s)
                            wait_weights(pe, s + 1)
                            product(n, [(bank(n, 30 * half, 30 * half + 30),
                                         [(slot(s + j // 8, DK, 256)[:, j % 8, half * P:half * P + P], (BLK, BLK2)[kv][:, j, :]) for j in range(16)])
                                        for half in range(2)])
                s = slab_first[L + "cmp2"]
                wait_weights(pe, s)
                w2 = slot(s, 4, 64)
                n = first[L + "cmp2"]
                pe.wait_ge(hidden_ready, 2 * l + 1)
                product(n, [(bank(n)[64 * g:64 * g + 64, 0:15], [(w2[:, half, :], HID[:, half, 15 * g:15 * g + 15]) for half in range(2)])
                            for g in range(2)])
                pe.wait_ge(hidden_ready, 2 * l + 2)
                product(n + 1, [(bank(n + 1)[0:15, 64 * g:64 * g + 64], [(HID2[:, half, 15 * g:15 * g + 15], w2[:, 2 + half, :]) for half in range(2)])
                                for g in range(2)])
                def win_evicted(steps):
                    for i in steps:
                        for m in range(WIN2[i][3]):
                            wait_evicted(pe, first[L + f"win{i}"] + m)

                win_evicted(range(6))
                attention(L + "A", "A",
                          lambda i: [[(AQ[64 * g:64 * g + 64, i // 2, i % 2 * P:(i % 2 + 1) * P], AK[64 * g:64 * g + 64, i // 2, 0:(i % 2 + 1) * P])
                                      for g in range(2)]],
                          lambda i: [(slice(0, P), 0, [(AV[:, k, i // 2 * P:(i // 2 + 1) * P], 0, k * P, P) for k in range(i % 2 + 1)])])
                pe.wait_ge(squares_ready, tally.add("squares_ready") + 1)
                for i in range(2):
                    n = first[L + "A.norm"] + i
                    product(n, [(bank(n), [(ones, SQ[:, 2 * i:2 * i + 2, :])])])
                tally.add("normed", 1)
                pe.wait_ge(normed, tally.n["normed"])
                halves(L + "A.out", 4, OT, [])
                win_evicted(range(6, 11))
                wait_evicted(pe, first[L + "cmp2"])
                wait_evicted(pe, first[L + "cmp2"] + 1)

                def b_scores(i):
                    q = [BQ[64 * g:64 * g + 64, i // 2, i % 2 * P:(i % 2 + 1) * P] for g in range(2)]
                    n = (i % 2 + 1) * P
                    return [[(q[g], kk[64 * g:64 * g + 64, 0:m]) for g in range(2)] for kk, m in ((KCMP, blocks(i % 2)), (BKS, n), (BKW, n))]

                def b_values(i):
                    out = []
                    for g in range(2):
                        nb = blocks(i % 2)
                        terms = [(VCMP[0:nb, g, :], 0, g * P, nb)]
                        for b, vv in ((1, BVS), (2, BVW)):
                            terms += [(vv[:, k, 64 * g:64 * g + 64], b, (g * (i % 2 + 1) + k) * P, P) for k in range(i % 2 + 1)]
                        out.append((slice(64 * g, 64 * g + 64), 0, terms))
                    return out

                attention(L + "B", "B", b_scores, b_values)
                halves(L + "B.out", 4, OT, attention_numbers(first[L + "B"], "B")[3])
                win_evicted(range(11, 15))
                attention(L + "C", "C",
                          lambda i: [[(CQ2[64 * g:64 * g + 64, i // 2, i % 2 * P:(i % 2 + 1) * P], CK2[64 * g:64 * g + 64, 0:(i % 2 + 1) * P])
                                      for g in range(2)]],
                          lambda i: [(slice(64 * g, 64 * g + 64), 0,
                                      [(CV2[:, k, 64 * g:64 * g + 64], 0, (g * (i % 2 + 1) + k) * P, P) for k in range(i % 2 + 1)])
                                     for g in range(2)])
                halves(L + "C.out", 4, OT, attention_numbers(first[L + "C"], "C")[3])
                pe.wait_ge(merged_ready, tally.add("merged_ready", 1) + 1)
                quarters(L + "wout", MRG)
                ffn(L + "ffn2")
                norm_x(first[L + "ple.norm"])
                s = slab_first[L + "ple.p"]
                wait_weights(pe, s)
                pe.wait_ge(layer_in, 16 * (l + 1))
                for m in range(DK):
                    n = first[L + "ple.p"] + m
                    product(n, [(bank(n, 0, T), [(slot(s, 2, D)[:, k, m * P:(m + 1) * P], PIN[:, k, :]) for k in range(2)])])
                pe.wait_ge(normed, tally.n["normed"])
                quarters(L + "ple.gate", U)
            norm_x(first["2.final.norm"])

        @block.scalar
        def _(act):
            tally = Tally()

            def link(ins):
                ins.then_inc(act_step, 1)
                act.wait_ge(act_step, tally.add("act_step") + 1)

            def evict(n, dst, src, func=ACT.Copy):
                wait_product(act, n)
                nc.scalar.activation(dst, src, func).then_inc(evicted[n % BANKS], 1)

            def norm(v=V, r=RSTD):
                act.wait_ge(mean_ready, tally.add("mean_ready") + 1)
                link(nc.scalar.activation(r, v, ACT.Ln))
                nc.scalar.activation(r, r, ACT.Exp, scale=-0.5).then_inc(rstd_ready, 1)

            def norm_x(n):
                wait_product(act, n)
                nc.scalar.activation(RSTD[:], bank(n, 0, T), ACT.Ln, bias=con("eps", 1), scale=1.0 / D).then_inc(evicted[n % BANKS], 1)
                wait_evicted(act, n)
                nc.scalar.activation(RSTD[:], RSTD[:], ACT.Exp, scale=-0.5).then_inc(rstd_ready, 1)

            def ffn(name):
                s0, p0 = slab_first[name + ".in"], first[name + ".in"]
                n_norm = first[name + ".norm"]
                half = tally.add("half_read", DK)

                def high(r, j):
                    wait_weights(act, s0 + j, r)
                    if j >= 2 and j < FK + 2:
                        wait_product(act, p0 + 2 * (j - 2) + 1, r)
                    elif j >= FK + 2 and j % 2 == 0:
                        act.wait_ge(half_read, half + (j - FK) // 2)
                    elif j >= FK + 2:
                        wait_product(act, first[name + ".out"] + (j - FK) // 2 - 1)
                    elif not isinstance(r, int):
                        wait_product(act, p0 + 2 * (j - 2) + 1, r)
                    nc.scalar.activation(WH[:, j % 2, 0:ffn_words(j)], RING[:, (s0 + j) % SLOTS, 0:ffn_words(j)], ACT.Copy)\
                      .then_inc(weights_high, 1)

                def hidden_part(r, j):
                    wait_evicted(act, p0 + 2 * j + 1, r)
                    nc.scalar.activation(HH[:, bass.ds(r * SLOTS + j, 1), :], HF[:, j % 2:j % 2 + 1, :], ACT.Copy)\
                      .then_inc(hidden_high, 1)

                if n_norm:
                    wait_product(act, n_norm - 1)
                high(0, 0)
                norm_x(n_norm)
                full = tally.add("u_full", DK)
                for k in range(DK):
                    act.wait_ge(u_full, full + k + 1)
                    nc.scalar.activation(UH[:, k, :], U[:, k, :], ACT.Copy).then_inc(u_high, 1)

                def pair(r, j):
                    n = p0 + 2 * j
                    high(r, j + 1)
                    wait_product(act, n, r)
                    if not isinstance(r, int) or j >= 2:
                        wait_evicted(act, n - 3, r)
                    nc.scalar.activation(SILU[:, j % 2, :], bank(n, 0, T), ACT.Silu).then_inc(evicted[n % BANKS], 1)
                    if j or not isinstance(r, int):
                        hidden_part(r, j - 1)

                rounds(act, FK, pair)
                high(0, FK + 1)
                hidden_part(0, FK - 1)
                for j in range(FK + 2, FK + 2 * DK):
                    high(0, j)

            def attention(name, kind, scale=1.0):
                units, n_s, n_t, n_b = ATTN[kind]
                s, t, f, o, _ = attention_numbers(first[name], kind)
                base = tally.add("max_ready", units)
                for i in range(units + 1):
                    if i < units:
                        qt = par = i % 2
                        act.wait_ge(max_ready, base + i + 1)
                        for b in range(n_b):
                            cmp = kind == "B" and b == 0
                            nk = blocks(qt) if cmp else T if kind == "mem" else (qt + 1) * P
                            nk += kind == "C"
                            for g in range(2):
                                src = bank(s[i])[:, g * T:(g + 1) * T] if kind == "mem" else S[:, b, par, g, 0:nk]
                                last = nc.scalar.activation(S[:, b, par, g, 0:nk], src, ACT.Exp, bias=MX[:, par, b, g:g + 1],
                                                            scale=scale, accum_out=SUM[:, par, b, g:g + 1])
                        last.then_inc(evicted[s[i] % BANKS] if kind == "mem" else exp_done, 1)
                    if i >= 1:
                        u = i - 1
                        if u >= 2:
                            wait_product(act, o[u - 2])
                        for b in range(n_t):
                            cmp = kind == "B" and b == 0
                            keys = 1 if cmp else NT if kind == "mem" else u % 2 + 1
                            c = (1 if kind == "A" else 2) * keys * P
                            rows = slice(0, blocks(u % 2)) if cmp else slice(0, P)
                            evict(t[u] + b, PT[rows, b, u % 2, 0:c], bank(t[u] + b)[rows, 0:c])
                        for j in range(DK // units):
                            gate = BRANCH[kind] * DK + u * (DK // units) + j
                            evict(f[u] + j, GATE[:, gate, :], bank(f[u] + j, 0, T), ACT.Sigmoid)

            def tables():
                act.wait_ge(angle_ready, 1)
                nc.scalar.activation(SIN[64:96, :], SIN[64:96, :], ACT.Sin)
                nc.scalar.activation(COS[64:96, :], COS[64:96, :], ACT.Sin).then_inc(rope_ready, 1)
                act.wait_ge(angle_ready, 2)
                link(nc.scalar.activation(LB[:, 2, :], LB[:, 1, :], ACT.Exp, scale=-1.0))
                nc.scalar.activation(LB[:, 2, :], LB[:, 2, :], ACT.Ln, bias=1.0).then_inc(rope_ready, 1)
                act.wait_ge(angle_ready, 3)
                nc.scalar.activation(LAM[:, 2:4, :], LAM[:, 0:2, :], ACT.Exp).then_inc(lambda_ready, 1)

            for l, L in enumerate(block1):
                ffn(L + "ffn1")
                norm_x(first[L + "mix.norm"])
                if l == 0:
                    tables()
                HA, HB = HX[:, 0, :], HX[:, 1, :]
                for i, (c, width, count) in enumerate(WIN1):
                    if i == 4:
                        act.wait_ge(hg_vec, tally.add("hg_vec") + 1)
                        link(nc.scalar.activation(HB, HA, ACT.Exp, scale=-1.0))
                        nc.scalar.activation(HB, HB, ACT.Ln, bias=1.0).then_inc(hg_act, 1)
                    if i == 5:
                        act.wait_ge(hg_vec, tally.add("hg_vec") + 1)
                        if l == 0:
                            nc.scalar.activation(HK, HK, ACT.Exp).then_inc(hg_act, 1)
                        else:
                            for h in range(HG_H):
                                k = HK[:, h * T:(h + 1) * T]
                                last = nc.scalar.activation(k, k, ACT.Exp, bias=LB[:, 4, h:h + 1])
                            last.then_inc(hg_act, 1)
                            act.wait_ge(hg_vec, tally.add("hg_vec") + 1)
                            link(nc.scalar.activation(HB, HA, ACT.Exp, scale=-1.0))
                            nc.scalar.activation(HB, HB, ACT.Ln, bias=1.0).then_inc(hg_act, 1)
                    if i >= PAIRS_AFTER:
                        level = i - PAIRS_AFTER
                        act.wait_ge(hg_vec, tally.add("hg_vec") + 1)
                        nc.scalar.activation(HX[:, level % 2, :], HX[:, level % 2, :], ACT.Exp).then_inc(hg_act, 1)
                    for m in range(count):
                        n = first[L + f"win{i}"] + m
                        if c == C_KR:
                            evict(n, KR[64:96, 0, :], bank(n)[64:96, 0:T])
                        elif C_HI <= c < C_HG:
                            evict(n, VH[:, m, c - C_HI:c - C_HI + 256], bank(n, 0, 256))
                        else:
                            for c0, dst, func in ((C_MQ, MQ, ACT.Copy), (C_HG, HGT, ACT.Silu),
                                                  (C_HF, Z.rearrange("p (h t) -> p h t", t=T), ACT.Copy),
                                                  (C_HQ, HQ, ACT.Silu), (C_KV, CKV, ACT.Copy), (C_Q, CQ, ACT.Copy)):
                                if c >= c0:
                                    evict(n, dst[:, (c - c0) // P + m, :], bank(n, 0, T), func)
                                    break
                    if i == LATENTS_AFTER:
                        norm(V[:], RSTD[:])
                        norm(V[:], RSTD[:])
                if l == 0:
                    evict(first["bias"], ROWS[0:BIAS_H, :], bank(first["bias"])[0:BIAS_H, :])
                for h in range(MLA_H):
                    evict(first[L + "uq"] + h, QH[0:QK, h, :], bank(first[L + "uq"] + h)[0:QK, 0:T])
                for h in range(MLA_H):
                    evict(first[L + "uk"] + h, KH[0:NOPE, h, :], bank(first[L + "uk"] + h)[0:NOPE, 0:T])
                for m in range(NT):
                    evict(first[L + "uv"] + m, VM[:, m, :], bank(first[L + "uv"] + m))
                for i in range(2):
                    evict(first[L + "hg.o"] + i, OT[:, 2 * i:2 * i + 2, :], bank(first[L + "hg.o"] + i))
                for m in range(4):
                    evict(first[L + "hg.gate0"] + m, GATE[:, DK + m, :], bank(first[L + "hg.gate0"] + m, 0, T), ACT.Sigmoid)
                norm(TMP[:], TMP[:])
                for m in range(4):
                    evict(first[L + "hg.gate1"] + m, GATE[:, DK + 4 + m, :], bank(first[L + "hg.gate1"] + m, 0, T), ACT.Sigmoid)
                attention(L + "mla", "mla")
                norm(V[:], RSTD[:])
                for i in range(8):
                    n = first[L + "mem.kv"] + i
                    if i < 4:
                        evict(n, MK[:, i, :], bank(n, 0, T))
                    else:
                        c = (i - 4) // 2 * 256
                        evict(n, MV[:, i % 2, c:c + 256], bank(n, 0, 256))
                attention(L + "mem", "mem", P ** -0.5)
                ffn(L + "ffn2")
            norm_x(first["1.final.norm"])

            for l, L in enumerate(block2):
                ffn(L + "ffn1")
                norm_x(first[L + "mix.norm"])
                for i, (kind, c, width, count) in enumerate(WIN2):
                    n = first[L + f"win{i}"]
                    if kind in ("tiles", "pairs"):
                        for c0, dst, func in ((D_CQ, CQ2, ACT.Copy), (D_BQ, BQ, ACT.Copy),
                                              (D_AK, AK, ACT.Copy), (D_AQ, AQ, ACT.Copy)):
                            if c >= c0:
                                tile = (c - c0) // (64 if kind == "pairs" else P)
                                for m in range(2):
                                    evict(n + m, dst[:, tile + m, :], bank(n + m, 0, T), func)
                                break
                    elif kind == "tokens":
                        for m in range(NT):
                            evict(n + m, AV[:, m, c - D_AV:c - D_AV + 256], bank(n + m, 0, 256))
                    elif kind == "gate":
                        evict(n, BG, bank(n, 0, 24 * NT).rearrange("p (m c) -> p m c", m=NT), ACT.Sigmoid)
                    elif kind == "kv":
                        kd, vd = {D_BKS: (BKS, BVS), D_BKW: (BKW, BVW), D_CK: (CK2, CV2)}[c]
                        evict(n, kd, bank(n, 0, T))
                        evict(n + 1, vd, bank(n + 1, 0, NT * P).rearrange("p (m c) -> p m c", m=NT))
                    elif kind == "shift":
                        for m, dst in enumerate((KC2, VC2)):
                            b3 = bank(n + m).rearrange("p (g t) -> p g t", g=2)
                            wait_product(act, n + m)
                            nc.scalar.activation(dst[0:64, :, :], b3[0:64], ACT.Copy)
                            nc.scalar.activation(dst[64:128, :, 0:T - 1], b3[64:128, :, 1:T], ACT.Copy)\
                              .then_inc(evicted[(n + m) % BANKS], 1)
                    if i == CMP_AFTER:
                        for kv in range(2):
                            act.wait_ge(gelu_vec, tally.add("gelu_vec") + 1)
                            nc.scalar.activation(GY, GY, ACT.Exp, scale=-2.0 * (2.0 / np.pi) ** 0.5).then_inc(gelu_act, 1)
                n = first[L + "cmp2"]
                evict(n, KCMP[:, 0:15], bank(n, 0, 15))
                evict(n + 1, VCMP[0:15, :, :], bank(n + 1)[0:15, 0:P].rearrange("p (g d) -> p g d", g=2))
                attention(L + "A", "A")
                norm(TMP[:], TMP[:])
                attention(L + "B", "B")
                attention(L + "C", "C")
                ffn(L + "ffn2")
                norm_x(first[L + "ple.norm"])
                for m in range(DK):
                    evict(first[L + "ple.p"] + m, PLE[:, m, :], bank(first[L + "ple.p"] + m, 0, T))
                for m in range(DK):
                    evict(first[L + "ple.gate"] + m, GATE[:, DK + m, :], bank(first[L + "ple.gate"] + m, 0, T), ACT.Sigmoid)
            norm_x(first["2.final.norm"])

        @block.vector
        def _(dve):
            tally = Tally()
            v_ = nc.vector

            def link(ins):
                ins.then_inc(vec_step, 1)
                dve.wait_ge(vec_step, tally.add("vec_step") + 1)

            def norm_x(gain, dst, done=normed):
                dve.wait_ge(rstd_ready, tally.add("rstd_ready") + 1)
                for k in range(DK):
                    v_.scalar_tensor_tensor(dst[:, k, :], X[:, k, :], gain[:, k:k + 1], RSTD[:], ALU.mult, ALU.mult)\
                      .then_inc(done, 1)

            def add_squares(m):
                if m == 0:
                    link(v_.tensor_tensor(ACC, X[:, 0, :], X[:, 0, :], ALU.mult))
                    return
                link(v_.tensor_tensor(SQX, X[:, m, :], X[:, m, :], ALU.mult))
                added = v_.tensor_tensor(ACC, ACC, SQX, ALU.add)
                if m < DK - 1:
                    link(added)
                else:
                    added.then_inc(squares_ready, 1)

            def add_to_x(name, factor, m):
                n = first[name] + m
                wait_product(dve, n)
                v_.scalar_tensor_tensor(X[:, m, :], bank(n, 0, T), factor, X[:, m, :], ALU.mult, ALU.add)\
                  .then_inc(evicted[n % BANKS], 1)
                wait_evicted(dve, n)
                add_squares(m)

            def ffn(name, gain):
                s0, p0 = slab_first[name + ".in"], first[name + ".in"]
                u = tally.add("u_high", DK)
                high = tally.add("weights_high", FK + 2 * DK)
                hidden = tally.add("hidden", FK)
                norm_x(gain, U, done=u_full)

                def low(r, j):
                    n = ffn_words(j)
                    dve.wait_ge(weights_high, r * SLOTS + high + j + 1)
                    v_.tensor_tensor(WL[:, j % 2, 0:n], RING[:, (s0 + j) % SLOTS, 0:n], WH[:, j % 2, 0:n].bitcast(FP), ALU.subtract)\
                      .then_inc(weights_low, 1)

                def hidden_part(r, j):
                    dve.wait_ge(hidden_high, r * SLOTS + hidden + j + 1)
                    v_.tensor_tensor(HL[:, bass.ds(r * SLOTS + j, 1), :], HF[:, j % 2:j % 2 + 1, :],
                                     HH[:, bass.ds(r * SLOTS + j, 1), :].bitcast(FP), ALU.subtract).then_inc(hidden_low, 1)

                low(0, 0)
                for k in range(DK):
                    dve.wait_ge(u_high, u + k + 1)
                    v_.tensor_tensor(UL[:, k, :], U[:, k, :], UH[:, k, :].bitcast(FP), ALU.subtract).then_inc(u_low, 1)

                def pair(r, j):
                    n = p0 + 2 * j
                    low(r, j + 1)
                    wait_evicted(dve, n, r)
                    wait_product(dve, n + 1, r)
                    if not isinstance(r, int) or j >= 2:
                        dve.wait_ge(hidden_low, r * SLOTS + hidden + j - 1)
                    v_.tensor_tensor(HF[:, j % 2, :], SILU[:, j % 2, :], bank(n + 1, 0, T), ALU.mult)\
                      .then_inc(evicted[(n + 1) % BANKS], 1)
                    if j or not isinstance(r, int):
                        hidden_part(r, j - 1)

                rounds(dve, FK, pair)
                low(0, FK + 1)
                hidden_part(0, FK - 1)
                for m in range(DK):
                    if m < DK - 1:
                        low(0, FK + 2 * m + 2)
                    add_to_x(name + ".out", 0.5, m)
                    if m < DK - 1:
                        low(0, FK + 2 * m + 3)

            def merge(name, branch, start=False, end=False):
                for m in range(DK):
                    n = first[name] + m
                    g = GATE[:, branch * DK + m, :]
                    wait_product(dve, n)
                    if start:
                        v_.tensor_tensor(MRG[:, m, :], bank(n, 0, T), g, ALU.mult).then_inc(evicted[n % BANKS], 1)
                    else:
                        v_.tensor_tensor(TMP[:, m % 2, 0:T], bank(n, 0, T), g, ALU.mult).then_inc(evicted[n % BANKS], 1)
                        wait_evicted(dve, n)
                        link(v_.tensor_tensor(MRG[:, m, :], MRG[:, m, :], TMP[:, m % 2, 0:T], ALU.add))
                if end:
                    v_.tensor_copy(MRG[:, DK - 1, T - 1:T], MRG[:, DK - 1, T - 1:T]).then_inc(merged_ready, 1)
                else:
                    for m in range(DK):
                        wait_evicted(dve, first[name] + m)

            def attention(name, kind, scale, window=None, lam=None, sinks=None):
                units, n_s, n_t, n_b = ATTN[kind]
                s, t, f, o, _ = attention_numbers(first[name], kind)
                exps = tally.add("exp_done", 0 if kind == "mem" else units)

                def scores(i):
                    qt = par = i % 2
                    for b in range(n_b):
                        n = s[i] + b
                        cmp = kind == "B" and b == 0
                        nk = blocks(qt) if cmp else T if kind == "mem" else (qt + 1) * P
                        if kind == "mem":
                            wait_product(dve, n)
                            sc = bank(n).rearrange("p (g t) -> p g t", g=2)[:, :, 0:nk]
                            link(v_.reduce_max(MX[:, par, b, :], sc, AX.X))
                            continue
                        if i >= 2:
                            wait_product(dve, t[i - 2] + b)
                        if n_s == n_b:
                            wait_product(dve, n)
                            sc = bank(n).rearrange("p (g t) -> p g t", g=2)[:, :, 0:nk]
                            v_.scalar_tensor_tensor(S[:, b, par, :, 0:nk], sc, scale, window(i, b), ALU.mult, ALU.add)\
                              .then_inc(evicted[n % BANKS], 1)
                        else:
                            for g in range(2):
                                n = s[i] + 2 * b + g
                                wait_product(dve, n)
                                v_.scalar_tensor_tensor(S[:, b, par, g, 0:nk], bank(n, 0, nk), scale, window(i, b)[:, g, :],
                                                        ALU.mult, ALU.add).then_inc(evicted[n % BANKS], 1)
                            wait_evicted(dve, n - 1)
                        if kind == "C":
                            link(v_.tensor_copy(S[:, b, par, :, nk:nk + 1], sinks[:, i // 2 * 2:i // 2 * 2 + 2].unsqueeze(2)))
                            nk += 1
                        wait_evicted(dve, n)
                        link(v_.reduce_max(MX[:, par, b, :], S[:, b, par, :, 0:nk], AX.X))
                    v_.tensor_scalar(MX[:, par, 0:n_b, :], MX[:, par, 0:n_b, :], -scale if kind == "mem" else -1.0, None, ALU.mult)\
                      .then_inc(max_ready, 1)

                def scale_probs(i):
                    qt = par = i % 2
                    if kind == "mem":
                        wait_evicted(dve, s[i])
                    else:
                        dve.wait_ge(exp_done, exps + i + 1)
                    link(v_.reciprocal(SUM[:, par, 0:n_b, :], SUM[:, par, 0:n_b, :]))
                    if kind == "A":
                        link(v_.tensor_scalar(SUM[:, par, 0, 1:2], SUM[:, par, 0, 1:2], lam, None, ALU.mult))
                        p0, p1 = S[:, 0, par, 0, 0:(qt + 1) * P], S[:, 0, par, 1, 0:(qt + 1) * P]
                        link(v_.tensor_scalar(p0, p0, SUM[:, par, 0, 0:1], None, ALU.mult))
                        v_.scalar_tensor_tensor(p0, p1, SUM[:, par, 0, 1:2], p0, ALU.mult, ALU.add).then_inc(probs_ready, 1)
                        return
                    if kind == "B":
                        gates = BG[:, qt, :].rearrange("p (g j b) -> p j b g", g=2, j=4)[:, i // 2]
                        link(v_.tensor_tensor(SUM[:, par, :, :], SUM[:, par, :, :], gates, ALU.mult))
                        if qt == 0:
                            link(v_.tensor_scalar(SUM[:, par, 0, :], SUM[:, par, 0, :], con("sees", 1), None, ALU.mult))
                    for b in range(n_b):
                        nk = blocks(qt) if kind == "B" and b == 0 else T if kind == "mem" else (qt + 1) * P
                        for g in range(2):
                            p = S[:, b, par, g, 0:nk]
                            last = v_.tensor_scalar(p, p, SUM[:, par, b, g:g + 1], None, ALU.mult)
                    last.then_inc(probs_ready, 1)

                def outputs(i):
                    wait_product(dve, o[i])
                    j, q = i // 2, slice(i % 2 * P, i % 2 * P + P)
                    if kind == "mem":
                        dst, src = OT[:, 2 * j:2 * j + 2, q], bank(o[i], 0, 2 * P).rearrange("p (g t) -> p g t", g=2)
                    else:
                        dst, src = OT[:, j, q], bank(o[i], 0, P)
                    v_.tensor_copy(dst, src).then_inc(evicted[o[i] % BANKS], 1)

                scores(0)
                for i in range(units):
                    if i + 1 < units:
                        scores(i + 1)
                    scale_probs(i)
                    if i >= 1:
                        outputs(i - 1)
                outputs(units - 1)
                return o

            def group_norm(name, count):
                v_.tensor_tensor(SQ[:, 0:4, :], OT, OT, ALU.mult).then_inc(squares_ready, 1)
                for i in range(2):
                    n = first[name] + i
                    wait_product(dve, n)
                    v_.tensor_scalar(TMP[:, i, :], bank(n), 1.0 / count, EPS, ALU.mult, ALU.add)\
                      .then_inc(evicted[n % BANKS], 1)
                    wait_evicted(dve, n)
                v_.tensor_copy(TMP[:, 0, 0:1], TMP[:, 0, 0:1]).then_inc(mean_ready, 1)
                dve.wait_ge(rstd_ready, tally.add("rstd_ready") + 1)

            def tables():
                link(v_.tensor_copy(V[64:96, :], COS[64:96, :].bitcast(I32)))
                link(v_.tensor_scalar(V[64:96, :], V[64:96, :], con("freq", 1, slice(64, 96)), None, ALU.mult))
                for table, turn in ((SIN, 0.0), (COS, 0.25)):
                    a, n, r = V[64:96, :], TMP[64:96, 0, T:2 * T], table[64:96, :]
                    link(v_.tensor_scalar(n, a, 1.0 / (2.0 * np.pi), turn, ALU.mult, ALU.add))
                    link(v_.tensor_scalar(n, n, 12582912.0, None, ALU.add))
                    link(v_.tensor_scalar(n, n, -12582912.0, None, ALU.add))
                    link(v_.scalar_tensor_tensor(r, n, -TURN[0], a, ALU.mult, ALU.add))
                    link(v_.scalar_tensor_tensor(r, n, -TURN[1], r, ALU.mult, ALU.add))
                    link(v_.scalar_tensor_tensor(r, n, -TURN[2], r, ALU.mult, ALU.add))
                    link(v_.tensor_scalar(r, r, turn * 2.0 * np.pi, None, ALU.add))
                    link(v_.tensor_scalar(r, r, 3.1415925, -3.1415925, ALU.min, ALU.max))
                v_.memset(RESET[:], 1.0).then_inc(angle_ready, 1)
                link(v_.tensor_tensor(LB[:, 0, :], vec("lb1", HG_H), vec("lb0", HG_H), ALU.subtract))
                v_.scalar_tensor_tensor(LB[:, 1, :], LB[:, 0, :], -1.0, LB[:, 0, :], ALU.mult, ALU.max).then_inc(angle_ready, 1)
                dve.wait_ge(rope_ready, 2)
                link(v_.scalar_tensor_tensor(LB[:, 3, :], LB[:, 0, :], 0.0, LB[:, 2, :], ALU.min, ALU.subtract))
                link(v_.tensor_tensor(LB[:, 4, :], LB[:, 3, :], LB[:, 0, :], ALU.subtract))
                link(v_.tensor_tensor(LB[:, 5, :], LB[:, 4, :], LB[:, 3, :], ALU.subtract))
                for l in range(DEPTH):
                    pairs = vec(f"lambda{l}", 256).rearrange("p (a b d) -> p a b d", a=2, b=2)
                    prod = TMP[:, l, 0:P].rearrange("p (a d) -> p a d", a=2)
                    link(v_.tensor_tensor(prod, pairs[:, :, 0, :], pairs[:, :, 1, :], ALU.mult))
                    link(v_.reduce_sum(LAM[:, 0:2, l], prod, AX.X))
                v_.memset(RESET[:].rearrange("p (c t) -> p c t", t=CHUNK)[:, :, 0:1], 0.0).then_inc(angle_ready, 1)
                dve.wait_ge(lambda_ready, 1)
                link(v_.tensor_tensor(LAM[:, 4, :], LAM[:, 3, :], LAM[:, 2, :], ALU.subtract))
                for l in range(DEPTH):
                    link(v_.tensor_scalar(LAM[:, 5, l:l + 1], LAM[:, 4, l:l + 1], -LAM_INIT[l], None, ALU.add))
                v_.tensor_copy(TAB[0:BUCKETS, :], vec("rel_bias", BIAS_H, slice(0, BUCKETS)))
                v_.tensor_copy(TAB[BUCKETS:BUCKETS + 2, :], con("mask_rows", BIAS_H, slice(BUCKETS, BUCKETS + 2))).then_inc(setup_done, 1)

            dve.wait_ge(inputs_in, 64)
            for m in range(DK):
                add_squares(m)
            heads = "p (h t) -> p h t"
            for l, L in enumerate(block1):
                ffn(L + "ffn1", vec(f"ffn1_norm{l}", DK))
                norm_x(vec(f"mix_norm{l}", DK), U)
                if l == 0:
                    tables()
                HA, HB = HX[:, 0, :], HX[:, 1, :]
                for i in range(4):
                    for m in range(2):
                        wait_evicted(dve, first[L + f"win{i}"] + m)
                v_.scalar_tensor_tensor(HA, Z, -1.0, Z, ALU.mult, ALU.max).then_inc(hg_vec, 1)
                dve.wait_ge(hg_act, tally.add("hg_act") + 1)
                link(v_.scalar_tensor_tensor(GS, Z, 0.0, HB, ALU.min, ALU.subtract))
                v_.tensor_tensor(HK, GS, Z, ALU.subtract).then_inc(hg_vec, 1)
                dve.wait_ge(hg_act, tally.add("hg_act") + 1)
                g = GS
                if l > 0:
                    for h in range(HG_H):
                        c = slice(h * T, (h + 1) * T)
                        link(v_.tensor_scalar(Z[:, c], GS[:, c], LB[:, 5, h:h + 1], None, ALU.add))
                    v_.scalar_tensor_tensor(HA, Z, -1.0, Z, ALU.mult, ALU.max).then_inc(hg_vec, 1)
                    dve.wait_ge(hg_act, tally.add("hg_act") + 1)
                    link(v_.scalar_tensor_tensor(Z, Z, 0.0, HB, ALU.max, ALU.add))
                    for h in range(HG_H):
                        c = slice(h * T, (h + 1) * T)
                        link(v_.tensor_scalar(Z[:, c], Z[:, c], LB[:, 3, h:h + 1], None, ALU.add))
                    src, GC = Z, GS
                else:
                    src, GC = GS, Z
                v_.tensor_tensor_scan(GC, RESET[:], src, 0.0, ALU.mult, ALU.add).then_inc(pair_ready, 1)
                dve.wait_ge(pair_ready, l * (LEVELS + 1) + 1)

                def exponents(level):
                    x = HX[:, level % 2, :]
                    if level < 6:
                        n = 1 << level
                        gv = GC.rearrange("p (b two n) -> p b two n", two=2, n=n)
                        xv = x.rearrange("p (b two n) -> p b two n", two=2, n=n)
                        pivot = gv[:, :, 0, n - 1:n].broadcast_to([P, HG_H * T // (2 * n), n])
                        v_.tensor_tensor(xv[:, :, 1, :], gv[:, :, 1, :], pivot, ALU.subtract)
                        v_.tensor_tensor(xv[:, :, 0, :], pivot, gv[:, :, 0, :], ALU.subtract).then_inc(hg_vec, 1)
                        return
                    gv = GC.rearrange("p (h c n) -> p h c n", h=HG_H, n=CHUNK)
                    xv = x.rearrange("p (h c n) -> p h c n", h=HG_H, n=CHUNK)

                    def end(c):
                        return gv[:, :, c, CHUNK - 1:CHUNK].broadcast_to([P, HG_H, CHUNK])

                    if level == 6:
                        v_.tensor_copy(xv[:, :, 1, :], gv[:, :, 1, :])
                        v_.tensor_copy(xv[:, :, 3, :], gv[:, :, 3, :])
                        v_.tensor_tensor(xv[:, :, 0, :], end(0), gv[:, :, 0, :], ALU.subtract)
                        v_.tensor_tensor(xv[:, :, 2, :], end(2), gv[:, :, 2, :], ALU.subtract).then_inc(hg_vec, 1)
                    else:
                        link(v_.tensor_tensor(xv[:, :, 0, :], end(0), gv[:, :, 0, :], ALU.subtract))
                        v_.tensor_copy(xv[:, :, 2, :], gv[:, :, 2, :])
                        v_.tensor_tensor(xv[:, :, 3, :], gv[:, :, 3, :], end(2), ALU.add)
                        v_.tensor_tensor(xv[:, :, 1, :], end(1), gv[:, :, 1, :], ALU.subtract)
                        v_.tensor_tensor(xv[:, :, 0, :], xv[:, :, 0, :], end(1), ALU.add).then_inc(hg_vec, 1)

                def factors(level):
                    dve.wait_ge(hg_act, tally.add("hg_act") + 1)
                    n = 1 << level
                    xv = HX[:, level % 2, :].rearrange("p (b two n) -> p b two n", two=2, n=n)
                    kv = HK.rearrange("p (b two n) -> p b two n", two=2, n=n)
                    qv = HQ.rearrange("p h t -> p (h t)").rearrange("p (b two n) -> p b two n", two=2, n=n)
                    v_.tensor_tensor(xv[:, :, 0, :], xv[:, :, 0, :], kv[:, :, 0, :], ALU.mult)
                    v_.tensor_tensor(xv[:, :, 1, :], xv[:, :, 1, :], qv[:, :, 1, :], ALU.mult).then_inc(pair_ready, 1)

                def masked(level):
                    for tt in ((0, 1) if level < LEVELS else (0,)):
                        n = first[L + f"pairs{level}"] + tt
                        wait_product(dve, n)
                        a4 = bank(n).rearrange(heads, t=P)
                        dst = AT[:, :, 1, :] if level == LEVELS else AT[:, :, 2 * tt, :]
                        if level == LEVELS:
                            v_.tensor_copy(dst, a4).then_inc(evicted[n % BANKS], 1)
                            continue
                        mask = con(f"pair{level}", P).unsqueeze(1).broadcast_to([P, HG_H, P])
                        tmp = TMP[:, tt, :].rearrange(heads, t=P)
                        v_.tensor_tensor(dst if level == 0 else tmp, a4, mask, ALU.mult).then_inc(evicted[n % BANKS], 1)
                        wait_evicted(dve, n)
                        if level:
                            link(v_.tensor_tensor(dst, dst, tmp, ALU.add))

                def mean_square(n, count):
                    wait_product(dve, n)
                    v_.tensor_scalar(V[:], bank(n, 0, T), 1.0 / count, EPS, ALU.mult, ALU.add).then_inc(evicted[n % BANKS], 1)
                    wait_evicted(dve, n)
                    v_.tensor_copy(V[:, 0:1], V[:, 0:1]).then_inc(mean_ready, 1)

                def scale_tiles(a, kt, gain):
                    dve.wait_ge(rstd_ready, tally.add("rstd_ready") + 1)
                    for k in range(kt):
                        v_.scalar_tensor_tensor(a[:, k, :], a[:, k, :], gain[:, k:k + 1], RSTD[:], ALU.mult, ALU.mult)\
                          .then_inc(normed, 1)

                for level in range(LEVELS + 1):
                    if level < LEVELS:
                        if level >= 2:
                            wait_product(dve, first[L + f"pairs{level - 1}"] + 1)
                        exponents(level)
                    if level == LATENTS_AFTER - PAIRS_AFTER:
                        for i in (4, 5, 6):
                            for m in range(WIN1[i][2]):
                                wait_evicted(dve, first[L + f"win{i}"] + m)
                        v_.tensor_tensor(SQ[:, 0:3, :], CQ, CQ, ALU.mult).then_inc(squares_ready, 1)
                        v_.tensor_tensor(SQ[:, 3:5, :], CKV, CKV, ALU.mult).then_inc(squares_ready, 1)
                        mean_square(first[L + "latent.norm"], 3 * P)
                        scale_tiles(CQ, 3, vec(f"q_lat_norm{l}", 3))
                        mean_square(first[L + "latent.norm"] + 1, 2 * P)
                        scale_tiles(CKV, 2, vec(f"kv_lat_norm{l}", 2))
                    masked(level)
                    if level < LEVELS:
                        factors(level)
                wait_evicted(dve, first[L + f"pairs{LEVELS}"])
                v_.tensor_copy(AT[:, 0, 0, 0:1], AT[:, 0, 0, 0:1]).then_inc(pairs_summed, 1)
                cos2 = COS[64:96, :].unsqueeze(1).broadcast_to([ROPE, 2, T])
                sin2 = SIN[64:96, :].unsqueeze(1).broadcast_to([ROPE, 2, T])
                for m in range(4):
                    n = first[L + "swap"] + m
                    q = QH[64:96, 2 * m:2 * m + 2, :]
                    turned = TMP[64:96, m % 2, :].rearrange("p (g t) -> p g t", g=2)
                    wait_product(dve, n)
                    v_.tensor_tensor(turned, bank(n)[64:96, :].rearrange("p (g t) -> p g t", g=2), sin2, ALU.mult)\
                      .then_inc(evicted[n % BANKS], 1)
                    wait_evicted(dve, n)
                    link(v_.tensor_tensor(q, q, cos2, ALU.mult))
                    link(v_.tensor_tensor(q, q, turned, ALU.add))
                n = first[L + "swap"] + 4
                wait_product(dve, n)
                v_.tensor_tensor(TMP[64:96, 0, 0:T], bank(n)[64:96, 0:T], SIN[64:96, :], ALU.mult).then_inc(evicted[n % BANKS], 1)
                link(v_.tensor_tensor(KR[64:96, 1, :], KR[64:96, 0, :], COS[64:96, :], ALU.mult))
                wait_evicted(dve, n)
                link(v_.tensor_tensor(KR[64:96, 1, :], KR[64:96, 1, :], TMP[64:96, 0, 0:T], ALU.add))
                v_.tensor_copy(KH[64:96, :, :], KR[64:96, 1, :].unsqueeze(1).broadcast_to([ROPE, MLA_H, T])).then_inc(roped, 1)
                wait_evicted(dve, first[L + "hg.o"])
                wait_evicted(dve, first[L + "hg.o"] + 1)
                group_norm(L + "hg.norm", P)
                link(v_.scalar_tensor_tensor(OT, OT, vec(f"hg_out_norm{l}", 1), TMP[:].rearrange("p a (b t) -> p (a b) t", t=T), ALU.mult, ALU.mult))
                for i in (10, 11):
                    for m in range(2):
                        wait_evicted(dve, first[L + f"win{i}"] + m)
                v_.tensor_tensor(OT, OT, HGT, ALU.mult).then_inc(normed, 1)
                merge(L + "hg.out", 1, start=True)
                dve.wait_ge(mem_in, 16 * (l + 1))
                v_.tensor_tensor(SQ[:, :, :], MEM, MEM, ALU.mult).then_inc(squares_ready, 1)
                causal = con("causal", 2 * P)

                def own(i, b):
                    return causal[:, (1 - i % 2) * P:2 * P].unsqueeze(1).broadcast_to([P, 2, (i % 2 + 1) * P])

                attention(L + "mla", "mla", QK ** -0.5, own)
                mean_square(first[L + "mem.norm"], D)
                scale_tiles(MEM, DK, vec(f"mem_norm{l}", DK))
                merge(L + "mla.out", 0)
                attention(L + "mem", "mem", P ** -0.5)
                merge(L + "mem.out", 2, end=True)
                for m in range(DK):
                    add_to_x(L + "wout", 1.0, m)
                ffn(L + "ffn2", vec(f"ffn2_norm{l}", DK))
            norm_x(vec("final1", DK), X)
            dve.wait_ge(normed, NORMED_1)
            for m in range(DK):
                add_squares(m)

            for l, L in enumerate(block2):
                ffn(L + "ffn1", vec(f"norm_g{l}0", DK))
                norm_x(vec(f"norm_g{l}1", DK), U)
                for kv in range(2):
                    wait_evicted(dve, first[L + "win8"] + kv)
                    src = (KC2, VC2)[kv]
                    for half in range(2):
                        dst = (BLK, BLK2)[kv][:, 8 * half:8 * half + 8, :].rearrange("p l (g n) -> p l g n", g=2)
                        tok = src[:, :, 16 * half:16 * half + 240].rearrange("p g (n l two) -> p l g n two", l=8, two=2)[:, :, :, :, 0]
                        pos = vec(f"pos{l}{kv}", 16)[:, 8 * half:8 * half + 8].unsqueeze(2).unsqueeze(3).broadcast_to([P, 8, 2, 15])
                        last = v_.tensor_tensor(dst, tok, pos, ALU.add)
                    last.then_inc(blocks_ready, 1)
                for kv in range(2):
                    n = first[L + "cmp"] + kv
                    if 2 * l + kv:
                        dve.wait_ge(hidden_ready, 2 * l + kv)
                    wait_product(dve, n)
                    v_.tensor_copy(GX, bank(n, 0, 60).rearrange("p (a b) -> p a b", a=2)).then_inc(evicted[n % BANKS], 1)
                    wait_evicted(dve, n)
                    link(v_.tensor_tensor(GY, GX, GX, ALU.mult))
                    link(v_.tensor_scalar(GY, GY, 0.044715, 1.0, ALU.mult, ALU.add))
                    v_.tensor_tensor(GY, GY, GX, ALU.mult).then_inc(gelu_vec, 1)
                    dve.wait_ge(gelu_act, tally.add("gelu_act") + 1)
                    link(v_.tensor_scalar(GY, GY, 1.0, None, ALU.add))
                    link(v_.reciprocal(GY, GY))
                    v_.tensor_tensor((HID, HID2)[kv], GX, GY, ALU.mult).then_inc(hidden_ready, 1)
                if l == 0:
                    dve.wait_ge(windows_in, 16)

                def pair_window(h0):
                    def get(i, b):
                        if h0 == 4 and b == 0:
                            h = h0 + i // 2
                            return WIN[:, h:h + 5:4, (CMP_LEN - 1 + P * (1 - i % 2)):2 * P:CMP_STRIDE]
                        h = h0 + i // 2
                        return WIN[:, h:h + 5:4, (1 - i % 2) * P:2 * P]
                    return get

                def head_window(i, b):
                    return WIN[:, i // 2, (1 - i % 2) * P:2 * P].unsqueeze(1).broadcast_to([P, 2, (i % 2 + 1) * P])

                o = attention(L + "A", "A", 64 ** -0.5, head_window, lam=LAM[:, 5, l:l + 1])
                for i in range(6, 8):
                    wait_evicted(dve, o[i])
                group_norm(L + "A.norm", P)
                link(v_.tensor_scalar(OT, OT, vec(f"subln{l}", 1), 1.0 - LAM_INIT[l], ALU.mult, ALU.mult))
                v_.tensor_tensor(OT, OT, TMP[:].rearrange("p a (b t) -> p (a b) t", t=T), ALU.mult).then_inc(normed, 1)
                merge(L + "A.out", 0, start=True)
                wait_evicted(dve, first[L + "win11"])
                attention(L + "B", "B", 64 ** -0.5, pair_window(4))
                merge(L + "B.out", 1)
                attention(L + "C", "C", 64 ** -0.5, pair_window(12), sinks=vec(f"sinks{l}", 8))
                merge(L + "C.out", 2, end=True)
                for m in range(DK):
                    add_to_x(L + "wout", 1.0, m)
                ffn(L + "ffn2", vec(f"norm_g{l}2", DK))
                norm_x(vec(f"norm_g{l}3", DK), U)
                for m in range(DK):
                    wait_evicted(dve, first[L + "ple.gate"] + m)
                    link(v_.tensor_tensor(GATE[:, DK + m, :], GATE[:, DK + m, :], PLE[:, m, :], ALU.mult))
                    link(v_.tensor_tensor(X[:, m, :], X[:, m, :], GATE[:, DK + m, :], ALU.add))
                    add_squares(m)
            norm_x(vec("final2", DK), U, done=result_ready)


_WEIGHTS = ["w_ffn1_in", "w_ffn1_out", "w_in", "w_uq", "w_uk", "w_uv", "w_o_mla", "w_o_hg", "w_mem_kv", "w_o_mem",
            "w_out", "w_ffn2_in", "w_ffn2_out", "ffn1_wi_2", "ffn1_wo_2", "w_in_2", "nsa_cmp_w1_2", "nsa_cmp_w2_2",
            "w_branch_2", "w_out_2", "ffn2_wi_2", "ffn2_wo_2", "w_ple_2", "w_ple_gate_2"]


def kernel(**inputs):
    import concourse.bacc as _bacc
    from concourse.bass_utils import run_bass_kernel_spmd as _run

    arrays = {name: np.ascontiguousarray(inputs[name]) for name in _WEIGHTS}
    arrays["cst"] = constants()[0]
    arrays["vec"] = pack_vectors(inputs)
    arrays["xT"] = np.ascontiguousarray(np.asarray(inputs["x"])[0].T)
    arrays["memT"] = np.ascontiguousarray(np.asarray(inputs["mem"])[0].T)
    arrays["pT"] = np.ascontiguousarray(np.asarray(inputs["p_2"])[:, 0].transpose(0, 2, 1))
    arrays["pos"] = np.ascontiguousarray(np.broadcast_to(np.asarray(inputs["positions"]), (ROPE, T)))

    nc = _bacc.Bacc("TRN2", target_bir_lowering=False, num_devices=1)
    w = {name: nc.dram_tensor(f"in_{name}", a.shape, mybir.dt.from_np(a.dtype), kind="ExternalInput").ap()
         for name, a in arrays.items()}
    out = nc.dram_tensor("out_xT", [D, T], FP, kind="ExternalOutput").ap()
    scratch_rows = nc.dram_tensor("bias_rows", [P, BIAS_H, 2 * T], FP, kind="Internal").ap()
    build(nc, w, VECS, out, scratch_rows)
    r = _run(nc, [{f"in_{name}": a for name, a in arrays.items()}], core_ids=[0])
    return np.ascontiguousarray(r.results[0]["out_xT"].T).reshape(1, T, D)
```

```python
import numpy as np
import concourse.bass as bass
from concourse import mybir
from concourse.alu_op_type import AluOpType as ALU
from contextlib import ExitStack

REGION_WORDS = 26420
FP = mybir.dt.float32
FR = mybir.dt.float32r
I32 = mybir.dt.int32
ACT = mybir.ActivationFunctionType
AX = mybir.AxisListType

P = 128
T = 256
NT = T // P
D = 1024
DK = D // P
FF = 2816
FK = FF // P
DEPTH = 2
EPS = 1e-6
NEG = -1e30

MLA_H, NOPE, ROPE = 8, 64, 32
QK = NOPE + ROPE
Q_LORA, KV_LORA = 384, 256
HG_H, CHUNK = 4, 64
MEM_H = 4
LEVELS = 8
A_H = 4
N_CMP, CMP_STRIDE, CMP_LEN = 15, 16, 32
BUCKETS, BIAS_H = 32, 20

LAM_INIT = [0.8 - 0.6 * float(np.exp(-0.3 * l)) for l in range(DEPTH)]
TURN = (6.28125, 0.001934051513671875, 2.0 * float(np.pi) - 6.28125 - 0.001934051513671875)
NORMED_1 = DEPTH * (DK + 3 + 2 + 1) + DK

BANKS = 8
SLOTS = 2
UNROLL = 4
SLOT = 2048

C_Q, C_KV, C_KR, C_HQ, C_HF, C_HI, C_HG, C_MQ, C_GATE = 0, 384, 640, 672, 1184, 1696, 2208, 2720, 3232
(D_AQ, D_AK, D_AV, D_BQ, D_BKC, D_BVC, D_BKS, D_BVS, D_BKW, D_BVW, D_BG, D_CQ, D_CK, D_CV,
 D_GATE) = (0, 512, 1024, 1536, 2048, 2176, 2304, 2432, 2560, 2688, 2816, 2840, 3352, 3480, 3608)


def blocks(qt):
    return min(N_CMP, ((qt + 1) * P - CMP_LEN) // CMP_STRIDE + 1)


class Tally:

    def __init__(self):
        self.n = {}

    def add(self, name, k=1):
        before = self.n.get(name, 0)
        self.n[name] = before + k
        return before


def constants():
    parts, at, n = [], {}, 0

    def put(name, a):
        nonlocal n
        full = np.zeros((P, a.shape[1]), np.float32)
        full[:a.shape[0]] = a
        parts.append(full)
        at[name] = n
        n += a.shape[1]

    put("ident", np.eye(P, dtype=np.float32))
    put("ones", np.ones((P, P), np.float32))
    s, t = np.arange(P)[:, None], np.arange(P)[None, :]
    put("pair0", (s == t).astype(np.float32))
    for l in range(LEVELS - 1):
        put(f"pair{l + 1}", ((s >> (l + 1) == t >> (l + 1)) & (s >> l & 1 == 0) & (t >> l & 1 == 1)).astype(np.float32))
    j = np.arange(2 * P)[None, :]
    put("causal", np.where(s - j + P >= 0, 0.0, NEG).astype(np.float32))
    swap = np.zeros((P, ROPE), np.float32)
    for i in range(ROPE // 2):
        swap[64 + ROPE // 2 + i, i] = -1.0
        swap[64 + i, ROPE // 2 + i] = 1.0
    put("swap", swap)
    freq = np.zeros((P, 1), np.float32)
    inv = (np.float32(10000.0) ** (-np.arange(0, ROPE, 2, dtype=np.float32) / np.float32(ROPE))).astype(np.float32)
    freq[64:96, 0] = np.concatenate([inv, inv])
    put("freq", freq)
    i = np.arange(2 * T)
    d = 255 - i
    m = np.maximum(d, 0)
    half = BUCKETS // 2
    large = half + (np.log(np.maximum(m, 1).astype(np.float32) / np.float32(half)) / np.float32(np.log(P / half))
                    * np.float32(BUCKETS - half)).astype(np.int32)
    bucket = np.where(m < half, m, np.minimum(large, BUCKETS - 1))
    hot = np.zeros((BUCKETS + 2, 2 * T), np.float32)
    hot[bucket, i] = 1.0
    hot[BUCKETS] = np.where(d < 0, NEG, 0.0)
    hot[BUCKETS + 1] = np.where((d >= P), NEG, 0.0)
    put("hot", hot)
    rows = np.zeros((2, BIAS_H), np.float32)
    rows[0] = 1.0
    rows[1, 12:] = 1.0
    mask_rows = np.zeros((P, BIAS_H), np.float32)
    mask_rows[BUCKETS:BUCKETS + 2] = rows
    put("mask_rows", mask_rows)
    put("eps", np.full((P, 1), EPS, np.float32))
    put("sees", (np.arange(P) >= CMP_LEN - 1).astype(np.float32)[:, None])
    return np.concatenate(parts, axis=1), at


def constant_places():
    return constants()[1]


VECS = {}


def pack_vectors(v):
    parts, n = [], 0

    def put(name, a):
        nonlocal n
        a = np.asarray(a, np.float32)
        full = np.zeros((P, a.shape[1]), np.float32)
        full[:a.shape[0]] = a
        parts.append(full)
        VECS[name] = n
        n += a.shape[1]

    def cols(a):
        return np.asarray(a).reshape(-1, P).T

    for l in range(DEPTH):
        for name in ("ffn1_norm", "mix_norm", "q_lat_norm", "kv_lat_norm", "hg_out_norm", "mem_norm", "ffn2_norm"):
            put(f"{name}{l}", cols(v[name][l]))
        for k in range(4):
            put(f"norm_g{l}{k}", cols(v["norm_g_2"][l, k]))
        put(f"subln{l}", cols(v["diff_subln_2"][l]))
        put(f"lambda{l}", np.broadcast_to(np.asarray(v["diff_lambda_2"][l]).reshape(1, 256), (P, 256)))
        put(f"sinks{l}", np.broadcast_to(np.asarray(v["swa_sinks_2"][l]).reshape(1, 2, 4).transpose(0, 2, 1).reshape(1, 8), (P, 8)))
        for kv in range(2):
            put(f"pos{l}{kv}", np.asarray(v["nsa_cmp_pos_2"][l, kv]).reshape(16, P).T)
        put(f"lb{l}", cols(v["hg_lower_bounds"][l]))
    put("rel_bias", np.asarray(v["rel_bias_2"]))
    put("final1", cols(v["final_norm"]))
    put("final2", cols(v["final_norm_2"]))
    return np.concatenate(parts, axis=1)


class Plan:

    def __init__(self):
        self.first = {}
        self.total = 0
        self.slab_first = {}
        self.slab_last = []
        self.slab_in = []
        self.split = []
        self.splits = []
        self.words = []

    def products(self, name, n):
        self.first[name] = self.total
        self.total += n

    def slab(self, last, dmas=1, split=False, words=SLOT):
        s = len(self.slab_last)
        before = self.slab_in[-SLOTS] if s >= SLOTS else 0
        self.slab_in.append(before + 16 * dmas)
        self.slab_last.append(last)
        self.split.append(len(self.splits) if split else None)
        self.words.append(words)
        if split:
            self.splits.append(s)

    def slabs(self, name, per_slab, dmas=1, split=False, words=SLOT):
        if name not in self.first:
            self.products(name, 0)
            self.slab_first[name] = len(self.slab_last)
        for n in per_slab:
            self.total += n
            self.slab(self.total - 1 if n else self.total, dmas, split, words)


WIN1 = ([(c + 256 * i, 256, 2) for c in (C_HQ, C_HF) for i in range(2)]
        + [(C_Q, 256, 2), (C_Q + 256, 128, 1), (C_KV, 256, 2), (C_KR, 32, 1)]
        + [(c + 256 * i, 256, 2) for c in (C_HI, C_HG, C_MQ) for i in range(2)])
PAIRS_AFTER = len(WIN1) - LEVELS
LATENTS_AFTER = 9
WIN2 = [("shift", D_BKC, 256, 1), ("shift", D_BVC, 256, 1),
        ("tiles", D_AQ, 256, 2), ("tiles", D_AQ + 256, 256, 2), ("tiles", D_AK, 256, 2), ("tiles", D_AK + 256, 256, 2),
        ("tokens", D_AV, 256, 2), ("tokens", D_AV + 256, 256, 2), ("pairs", D_BQ, 256, 2), ("gate", D_BG, 24, 1),
        ("pairs", D_BQ + 128, 256, 2), ("kv", D_CK, 256, 2), ("keys", D_BKS, 256, 2), ("values", D_BVS, 256, 2),
        ("pairs", D_CQ, 256, 2), ("pairs", D_CQ + 128, 256, 2)]
CMP_AFTER = {4: 0, 5: 1, 6: 2, 7: 3}
CMP2_AFTER = 12
GELU_AFTER = (8, 10)
ATTN = {"mla": (8, 1, 1, 1), "mem": (4, 1, 1, 1), "A": (8, 2, 1, 1), "B": (8, 6, 3, 3), "C": (8, 2, 1, 1)}


def attention_numbers(first, kind):
    units, n_s, n_t, _ = ATTN[kind]
    n_f = DK // units
    s, t, f, o, n = [0] * units, [0] * units, [0] * units, [0] * units, first
    for i in range(-2, units):
        if i >= 0:
            t[i] = n
            n += n_t
        if i + 2 < units:
            s[i + 2] = n
            n += n_s
        if i >= 0:
            f[i] = n
            n += n_f
            o[i] = n
            n += 1
    return s, t, f, o, n - first


def make_plan():
    pl = Plan()

    def ffn(name):
        pl.products(name + ".norm", 1)
        pl.slabs(name + ".in", [2] * FK, dmas=2, split=True)
        pl.slabs(name + ".out", [0, 1] * DK, split=True, words=FK // 2 * P)

    def attention(name, kind):
        _, _, f, _, n = attention_numbers(pl.total, kind)
        pl.slab_first[name] = len(pl.slab_last)
        for m in range(1, DK, 2):
            pl.slab(f[m * ATTN[kind][0] // DK] + m % (DK // ATTN[kind][0]))
        pl.products(name, n)

    for l in range(DEPTH):
        L = f"1.{l}."
        ffn(L + "ffn1")
        pl.products(L + "mix.norm", 1)
        for i, (c, width, n) in enumerate(WIN1):
            pl.slabs(L + f"win{i}", [n], split=c != C_KR, words=DK * width)
            if i == LATENTS_AFTER:
                pl.products(L + "latent.norm", 2)
            if i >= PAIRS_AFTER:
                pl.products(L + f"pairs{i - PAIRS_AFTER}", 2)
        if l == 0:
            pl.products("bias", 1)
        pl.slabs(L + "uq", [4, 4])
        pl.products(L + f"pairs{LEVELS}", 1)
        pl.slabs(L + "uk", [8])
        pl.slabs(L + "uv", [2])
        pl.products(L + "swap", 5)
        pl.products(L + "hg.o", 2)
        pl.slabs(L + "hg.gate0", [2] * 2, split=True)
        pl.products(L + "hg.norm", 2)
        pl.slabs(L + "hg.gate1", [2] * 2, split=True)
        pl.slabs(L + "hg.out", [4, 4])
        attention(L + "mla", "mla")
        pl.products(L + "mem.norm", 1)
        pl.slabs(L + "mla.out", [4, 4])
        pl.slabs(L + "mem.kv", [2] * 4)
        attention(L + "mem", "mem")
        pl.slabs(L + "mem.out", [4, 4])
        pl.slabs(L + "wout", [2] * 4)
        ffn(L + "ffn2")
    pl.products("1.final.norm", 1)
    for l in range(DEPTH):
        L = f"2.{l}."
        ffn(L + "ffn1")
        pl.products(L + "mix.norm", 1)
        for i, (kind, _, width, n) in enumerate(WIN2):
            pl.slabs(L + f"win{i}", [n], dmas={"pairs": 4, "shift": 4, "keys": 2, "values": 2}.get(kind, 1),
                     split=kind not in ("gate", "kv"), words=DK * width)
            if i in CMP_AFTER:
                pl.slabs(L + f"cmp{CMP_AFTER[i]}", [1])
            if i == CMP2_AFTER:
                pl.slabs(L + "cmp.out", [2], dmas=2)
        attention(L + "A", "A")
        pl.products(L + "A.norm", 2)
        pl.slabs(L + "A.out", [4, 4])
        attention(L + "B", "B")
        pl.slabs(L + "B.out", [4, 4], dmas=2)
        attention(L + "C", "C")
        pl.slabs(L + "C.out", [4, 4], dmas=2)
        pl.slabs(L + "wout", [2] * 4)
        ffn(L + "ffn2")
        pl.products(L + "ple.norm", 1)
        pl.slabs(L + "ple.p", [8])
        pl.slabs(L + "ple.gate", [2] * 4, split=True)
    pl.products("2.final.norm", 1)
    return pl


def build(nc, w, vec_places, out, scratch_rows):
    pl = make_plan()
    first, slab_first = pl.first, pl.slab_first
    cst = constant_places()
    n_cst, n_vec = w["cst"].shape[1], w["vec"].shape[1]
    block1 = [f"1.{l}." for l in range(DEPTH)]
    block2 = [f"2.{l}." for l in range(DEPTH)]

    ctx = ExitStack()
    with ctx:
        def sb(name, shape, dt=FP):
            return ctx.enter_context(nc.sbuf_tensor(name, shape, dt))

        def sem(name):
            return ctx.enter_context(nc.semaphore(name))

        cst_sb = sb("cst_sb", [P, n_cst])
        vec_sb = sb("vec_sb", [P, n_vec])
        X = sb("X", [P, DK, T])
        U = sb("U", [P, DK, T])
        UH, UL = sb("UH", [P, DK, T], FR), sb("UL", [P, DK, T], FR)
        RING = sb("RING", [P, SLOTS, SLOT])
        WH, WL = sb("WH", [P, SLOTS, SLOT], FR), sb("WL", [P, SLOTS, SLOT], FR)
        V = sb("V", [P, T])
        RSTD = sb("RSTD", [P, T])
        COS = sb("COS", [P, T])
        SIN = sb("SIN", [P, T])
        SILU = sb("SILU", [P, 2, T])
        TMP = sb("TMP", [P, 2, 512])
        LB = sb("LB", [P, 6, HG_H])
        LAM = sb("LAM", [P, 6, DEPTH])
        TAB = sb("TAB", [P, BIAS_H])
        MX = sb("MX", [P, 2, 3, 2])
        SUM = sb("SUM", [P, 2, 3, 2])
        region_base = (nc.sbuf_base + 31) // 32 * 32
        REGION = sb("REGION", [P, REGION_WORDS])
        used = [0]

        def region(*shape):
            n = int(np.prod(shape))
            a = REGION[:, used[0]:used[0] + n]
            used[0] += n
            assert used[0] <= REGION_WORDS, used[0]
            if len(shape) == 2:
                return a.rearrange("p (a b) -> p a b", b=shape[1])
            if len(shape) == 3:
                return a.rearrange("p (a b c) -> p a b c", b=shape[1], c=shape[2])
            if len(shape) == 4:
                return a.rearrange("p (a b c d) -> p a b c d", b=shape[1], c=shape[2], d=shape[3])
            return a

        def overlay(name, shape, at):
            return nc.alloc_sbuf_tensor_at(name, shape, FR, offset=region_base + 4 * at)

        HH, HL = overlay("HH", [P, FK, T], 0), overlay("HL", [P, FK, T], FK * T)
        HF = U[:, 0:2, :]
        ACC, SQX = U[:, DK - 1, :], U[:, DK - 2, :]
        used[0] = 0
        GATE = region(DK, T)
        MRG = region(DK, T)
        OT = region(4, T)
        PT = region(3, 2, 512)
        S = region(3, 2, 2, 260)
        both = used[0]
        used[0] = both - 3 * 2 * 2 * 260 - 2 * 2 * 512
        MK, MV = region(4, T), region(NT, 512)
        used[0] = both - 2 * 2 * 2 * 260
        Z, HK = region(HG_H * T), region(HG_H * T)
        used[0] = both
        CQ, CKV = region(3, T), region(2, T)
        QH, KH = region(MLA_H, T), region(MLA_H, T)
        latent_at = used[0]
        VM = region(NT, 512)
        MQ = region(4, T)
        LATENT_SQ = REGION[:, latent_at:latent_at + 5 * T].rearrange("p (k t) -> p k t", t=T)
        memory_at = used[0]
        HQ, HGT, VH = region(HG_H, T), region(HG_H, T), region(NT, 512)
        MEM_SQ = REGION[:, memory_at:memory_at + DK * T].rearrange("p (k t) -> p k t", t=T)
        GS = region(HG_H * T)
        HG_SQ = GS.rearrange("p (k t) -> p k t", t=T)
        HX = region(2, HG_H * T)
        MEM = HX.rearrange("p a (b t) -> p (a b) t", t=T)
        AT = region(HG_H, 3, P)
        RESET = REGION[:, used[0] - HG_H * 3 * P:used[0] - HG_H * 3 * P + HG_H * T]
        KR = SILU
        used[0] = both
        AQ, AK, AV = region(4, T), region(4, T), region(NT, 512)
        BQ, CQ2 = region(4, T), region(4, T)
        KC2, VC2 = region(2, T), region(2, T)
        BKS, BKW, CK2 = region(T), region(T), region(T)
        BV, CV2 = region(NT, 2 * P), region(NT, P)
        BVS, BVW = BV[:, :, 0:P], BV[:, :, P:2 * P]
        BG = region(NT, 24)
        BLK = region(16, 30)
        GY, HID, HID2 = region(2, 30), region(2, 30), region(2, 30)
        BLK2 = region(16, 30)
        KCMP, VCMP = region(16), region(2, 64)
        WIN = region(BIAS_H, T)
        PLE = MRG
        PIN = region(2, T)

        ps = ctx.enter_context(nc.psum_tensor("ps", [P, BANKS, 512], FP))
        ROWS = sb("ROWS", [P, 512])

        product_done = sem("product_done")
        evicted = [sem(f"evicted{b}") for b in range(BANKS)]
        weights_in = [sem(f"weights_in{i}") for i in range(SLOTS)]
        inputs_in = sem("inputs_in")
        x_in = sem("x_in")
        mem_in = sem("mem_in")
        layer_in = sem("layer_in")
        windows_in = sem("windows_in")
        scratch_out = sem("scratch_out")
        result_out = sem("result_out")
        setup_done = sem("setup_done")
        angle_ready = sem("angle_ready")
        rope_ready = sem("rope_ready")
        lambda_ready = sem("lambda_ready")
        squares_ready = sem("squares_ready")
        weights_high = sem("weights_high")
        weights_low = sem("weights_low")
        u_full = sem("u_full")
        u_high = sem("u_high")
        u_low = sem("u_low")
        hidden_high = sem("hidden_high")
        hidden_low = sem("hidden_low")
        half_read = sem("half_read")
        mean_ready = sem("mean_ready")
        rstd_ready = sem("rstd_ready")
        normed = sem("normed")
        hidden_ready = sem("hidden_ready")
        max_ready = sem("max_ready")
        exp_done = sem("exp_done")
        probs_ready = sem("probs_ready")
        merged_ready = sem("merged_ready")
        roped = sem("roped")
        hg_vec = sem("hg_vec")
        hg_act = sem("hg_act")
        pair_ready = sem("pair_ready")
        pairs_summed = sem("pairs_summed")
        result_ready = sem("result_ready")
        blocks_ready = sem("blocks_ready")
        gelu_vec = sem("gelu_vec")
        gelu_act = sem("gelu_act")
        vec_step = sem("vec_step")
        act_step = sem("act_step")

        block = ctx.enter_context(nc.Block())

        def con(name, n, rows=slice(0, P)):
            return cst_sb[rows, cst[name]:cst[name] + n]

        def vec(name, n, rows=slice(0, P)):
            return vec_sb[rows, vec_places[name]:vec_places[name] + n]

        def bank(n, *cols):
            return ps[:, n % BANKS, :] if not cols else ps[:, n % BANKS, cols[0]:cols[1]]

        def wait_product(eng, n, r=0):
            eng.wait_ge(product_done, r * BANKS + n + 1)

        def wait_evicted(eng, n, r=0):
            eng.wait_ge(evicted[n % BANKS], r + n // BANKS + 1)

        def wait_room(eng, n, r=0):
            if n >= BANKS or not isinstance(r, int):
                eng.wait_ge(evicted[n % BANKS], r + n // BANKS)

        def wait_weights(eng, s, r=0):
            eng.wait_ge(weights_in[s % SLOTS], r * (UNROLL // SLOTS * 32) + pl.slab_in[s])

        def slot(s, kt, width):
            return RING[:, s % SLOTS, 0:kt * width].rearrange("p (k n) -> p k n", n=width)

        def wait_split(eng, s, r=0):
            eng.wait_ge(weights_low, r * UNROLL + pl.split[s] + 1)

        def part(t, s, n=None):
            return t[:, pl.split[s] % SLOTS, 0:pl.words[s] if n is None else n]

        def parts(s, kt, width):
            return tuple(part(t, s, kt * width).rearrange("p (k n) -> p k n", n=width) for t in (WH, WL))

        def rounds(eng, n, body):
            for j in range(UNROLL):
                body(0, j)
            with eng.Fori(1, n // UNROLL) as r:
                for j in range(UNROLL):
                    body(r, j)
            for j in range(n // UNROLL * UNROLL, n):
                body(0, j)

        class Feed:

            def __init__(self, emit):
                self.q, self.emit = 0, emit

            def to(self, s):
                while self.q < len(pl.splits) and pl.splits[self.q] <= s:
                    self.emit(pl.splits[self.q])
                    self.q += 1

        def wide(a, shape):
            return a.broadcast_to(shape)

        @block.sync
        def _(sp):
            sp.dma_start(COS[64:96, :].bitcast(I32), w["pos"]).then_inc(inputs_in, 16)
            sp.dma_start(cst_sb[:], w["cst"]).then_inc(inputs_in, 16)
            sp.dma_start(vec_sb[:], w["vec"]).then_inc(inputs_in, 16)
            sp.dma_start(X[:], w["xT"].rearrange("(k p) t -> p k t", p=P)).then_inc(x_in, 16)

            def room(s):
                if s >= SLOTS:
                    if pl.split[s - SLOTS] is None:
                        wait_product(sp, pl.slab_last[s - SLOTS])
                    else:
                        wait_split(sp, s - SLOTS)

            def load(s, *pairs):
                room(s)
                for dst, src in pairs:
                    sp.dma_start(dst, src).then_inc(weights_in[s % SLOTS], 16)

            def rows(a):
                return a.rearrange("(k p) n -> p k n", p=P)

            def ffn(name, wi, wo):
                s0 = slab_first[name + ".in"]

                def pair(r, j):
                    s = s0 + j
                    if isinstance(r, int):
                        room(s)
                    else:
                        sp.wait_ge(weights_low, r * UNROLL + pl.split[s] - SLOTS + 1)
                    dst = slot(s, DK, 256)
                    for side in range(2):
                        sp.dma_start(dst[:, :, side * P:(side + 1) * P],
                                     rows(wi[:, bass.ds(r * (UNROLL * P) + (j * P + side * FF), P)]))\
                          .then_inc(weights_in[s % SLOTS], 16)

                rounds(sp, FK, pair)
                for i in range(2 * DK):
                    m, half = i // 2, i % 2
                    k0 = half * (FK // 2)
                    load(slab_first[name + ".out"] + i,
                         (slot(slab_first[name + ".out"] + i, FK // 2, P),
                          rows(wo[k0 * P:(k0 + FK // 2) * P, m * P:(m + 1) * P])))

            def halves(name, a, kt):
                n = a.shape[1] // 2
                for i in range(2):
                    s = slab_first[name] + i
                    load(s, (slot(s, kt, n), rows(a[:, i * n:(i + 1) * n])))

            def quarters(name, a, count=4):
                for i in range(count):
                    s = slab_first[name] + i
                    load(s, (slot(s, DK, 256), rows(a[:, i * 256:(i + 1) * 256])))

            for l, L in enumerate(block1):
                ffn(L + "ffn1", w["w_ffn1_in"][l], w["w_ffn1_out"][l])
                for i, (c, n, _) in enumerate(WIN1):
                    s = slab_first[L + f"win{i}"]
                    load(s, (slot(s, DK, n), rows(w["w_in"][l][:, c:c + n])))
                halves(L + "uq", w["w_uq"][l], 3)
                s = slab_first[L + "uk"]
                load(s, (slot(s, 2, 512), rows(w["w_uk"][l])))
                s = slab_first[L + "uv"]
                load(s, (slot(s, 2, 512), rows(w["w_uv"][l])))
                gate = [w["w_in"][l][:, C_GATE + b * D:C_GATE + (b + 1) * D] for b in range(3)]
                quarters(L + "hg.gate0", gate[1][:, 0:D // 2], 2)
                quarters(L + "hg.gate1", gate[1][:, D // 2:D], 2)
                halves(L + "hg.out", w["w_o_hg"][l], 4)
                quarters(L + "mla", gate[0])
                halves(L + "mla.out", w["w_o_mla"][l], 4)
                quarters(L + "mem.kv", w["w_mem_kv"][l])
                quarters(L + "mem", gate[2])
                halves(L + "mem.out", w["w_o_mem"][l], 4)
                quarters(L + "wout", w["w_out"][l])
                ffn(L + "ffn2", w["w_ffn2_in"][l], w["w_ffn2_out"][l])
            for l, L in enumerate(block2):
                ffn(L + "ffn1", w["ffn1_wi_2"][l], w["ffn1_wo_2"][l])
                wi = w["w_in_2"][l]
                for i, (kind, c, n, _) in enumerate(WIN2):
                    s = slab_first[L + f"win{i}"]
                    dst = slot(s, DK, n)
                    if kind in ("pairs", "shift"):
                        d5 = dst.rearrange("p k (j g d) -> p k j g d", j=2, g=2)
                        load(s, *[(d5[:, :, j, g, :], rows(wi[:, c + at:c + at + 64]))
                                  for j in range(2) for g in range(2)
                                  for at in (64 * j + (256 * g if kind == "pairs" else 0),)])
                    elif kind in ("keys", "values"):
                        load(s, *[(dst[:, :, g * P:(g + 1) * P], rows(wi[:, c + (D_BKW - D_BKS) * g:c + (D_BKW - D_BKS) * g + P]))
                                  for g in range(2)])
                    else:
                        load(s, (dst, rows(wi[:, c:c + n])))
                    if i in CMP_AFTER:
                        j = CMP_AFTER[i]
                        s = slab_first[L + f"cmp{j}"]
                        load(s, (slot(s, DK, 256), rows(w["nsa_cmp_w1_2"][l, j // 2][j % 2 * D:(j % 2 + 1) * D, :])))
                    if i == CMP2_AFTER:
                        s = slab_first[L + "cmp.out"]
                        w2 = slot(s, 4, 64)
                        load(s, *[(w2[:, 2 * kv:2 * kv + 2, :], rows(w["nsa_cmp_w2_2"][l, kv])) for kv in range(2)])
                gate = [wi[:, D_GATE + b * D:D_GATE + (b + 1) * D] for b in range(3)]
                quarters(L + "A", gate[0])
                halves(L + "A.out", w["w_branch_2"][l, 0], 4)
                for b, name in ((1, "B"), (2, "C")):
                    quarters(L + name, gate[b])
                    for i in range(2):
                        s = slab_first[L + name + ".out"] + i
                        dst = slot(s, 4, 512)
                        src = w["w_branch_2"][l, b][:, i * 512:(i + 1) * 512].rearrange("(g j d) n -> g d j n", g=2, j=4)
                        load(s, *[(dst[64 * g:64 * g + 64], src[g]) for g in range(2)])
                quarters(L + "wout", w["w_out_2"][l])
                ffn(L + "ffn2", w["ffn2_wi_2"][l], w["ffn2_wo_2"][l])
                s = slab_first[L + "ple.p"]
                load(s, (slot(s, 2, D), rows(w["w_ple_2"][l])))
                quarters(L + "ple.gate", w["w_ple_gate_2"][l])
            sp.wait_ge(result_ready, DK)
            sp.dma_start(out.rearrange("(k p) t -> p k t", p=P), U[:]).then_inc(result_out, 16)
            sp.wait_ge(result_out, 16)

        @block.gpsimd
        def _(pool):
            for l, L in enumerate(block1):
                wait_product(pool, first[L + f"pairs{LEVELS}"])
                pool.dma_start(HX, w["memT"].rearrange("(k p) t -> p k t", p=P)).then_inc(mem_in, 16)
                if l == 0:
                    wait_product(pool, first[L + "mla"])
                    wait_evicted(pool, first["bias"])
                    pool.dma_start(scratch_rows.rearrange("r h i -> h r i"),
                                   ROWS[0:BIAS_H, :].unsqueeze(1).broadcast_to([BIAS_H, P, 2 * T])).then_inc(scratch_out, 16)
            pool.wait_ge(scratch_out, 16)
            wait_product(pool, first["1.final.norm"])
            wins = bass.AP(tensor=scratch_rows.tensor, offset=P - 1, ap=[[BIAS_H * 2 * T - 1, P], [2 * T, BIAS_H], [1, T]])
            for l, L in enumerate(block2):
                wait_product(pool, first[L + "mix.norm"])
                if l == 0:
                    pool.dma_start(WIN, wins).then_inc(windows_in, 16)
                wait_product(pool, first[L + "ple.norm"])
                pool.dma_start(PIN, w["pT"][l].rearrange("(k p) t -> p k t", p=P)).then_inc(layer_in, 16)

        @block.tensor
        def _(pe):
            tally = Tally()
            ones = con("ones", P)
            ident = con("ident", P)
            UP = (UH, UL)

            def product(n, groups, after=None):
                wait_room(pe, n)
                for o, terms in groups:
                    for i, (a, b) in enumerate(terms):
                        last = nc.tensor.matmul(o, a, b, start=i == 0, stop=i == len(terms) - 1)
                last.then_inc(product_done, 1)

            def feature(wp, ap, kt, cols):
                (wh, wl), (ah, al) = wp, ap
                return [t for k in range(kt) for t in ((wh[:, k, cols], ah[:, k, :]), (wh[:, k, cols], al[:, k, :]),
                                                       (wl[:, k, cols], ah[:, k, :]))]

            def token(wp, ap, kt, cols, tt):
                (wh, wl), (ah, al) = wp, ap
                q = slice(tt * P, (tt + 1) * P)
                return [t for k in range(kt) for t in ((ah[:, k, q], wh[:, k, cols]), (ah[:, k, q], wl[:, k, cols]),
                                                       (al[:, k, q], wh[:, k, cols]))]

            def product_first(n, s, groups):
                wait_room(pe, n)
                u = tally.add("u", DK)
                pe.wait_ge(weights_high, pl.split[s] + 1)
                for j, (o, (wh, wl), cols) in enumerate(groups):
                    for i, (a, b) in enumerate(((wh, UH), (wl, UH), (wh, UL))):
                        if j == 0 and i == 1:
                            wait_split(pe, s)
                        for k in range(DK):
                            if j == 0 and i != 1:
                                pe.wait_ge(u_high if i == 0 else u_low, u + k + 1)
                            last = nc.tensor.matmul(o, a[:, k, cols], b[:, k, :], start=i == 0 and k == 0, stop=i == 2 and k == DK - 1)
                last.then_inc(product_done, 1)

            def u_parts():
                pe.wait_ge(u_low, tally.add("u", DK) + DK)

            def norm(n, squares, kt):
                pe.wait_ge(squares_ready, tally.add("squares_ready") + 1)
                tally.add("normed", kt)
                product(n, [(bank(n, 0, T), [(ones, squares[:, k, :]) for k in range(kt)])])

            def norm_x(n, tiles=DK):
                pe.wait_ge(squares_ready, tally.add("squares_ready") + 1)
                tally.add("normed", tiles)
                product(n, [(bank(n, 0, T), [(ones, ACC)])])

            def ffn(name):
                norm_x(first[name + ".norm"], 0)
                s0, p0 = slab_first[name + ".in"], first[name + ".in"]
                u = tally.add("u", DK)
                hidden = tally.add("hidden", FK)

                def pair(r, j):
                    wh, wl = parts(s0 + j, DK, 256)
                    peeled = isinstance(r, int) and j == 0
                    if peeled:
                        pe.wait_ge(weights_high, pl.split[s0] + 1)
                    else:
                        wait_split(pe, s0 + j, r)
                    for side in range(2):
                        n = p0 + 2 * j + side
                        wait_room(pe, n, r)
                        terms = [(a, b) for a, b in ((wh, UH), (wl, UH), (wh, UL))]
                        for i, (a, b) in enumerate(terms):
                            if peeled and side == 0 and i == 1:
                                wait_split(pe, s0)
                            for k in range(DK):
                                if peeled and side == 0 and i != 1:
                                    pe.wait_ge(u_high if i == 0 else u_low, u + k + 1)
                                last = nc.tensor.matmul(bank(n, 0, T), a[:, k, side * P:(side + 1) * P], b[:, k, :],
                                                        start=i == 0 and k == 0, stop=i == 2 and k == DK - 1)
                        last.then_inc(product_done, 1)

                rounds(pe, FK, pair)
                for m in range(DK):
                    n = first[name + ".out"] + m
                    wait_room(pe, n)
                    for half in range(2):
                        j = FK + 2 * m + half
                        wh, wl = parts(s0 + j, FK // 2, P)
                        wait_split(pe, s0 + j)
                        for k in range(FK // 2):
                            kk = half * (FK // 2) + k
                            if m == 0:
                                pe.wait_ge(hidden_low, hidden + kk + 1)
                            for a, b in ((wh, HH), (wl, HH), (wh, HL)):
                                last = nc.tensor.matmul(bank(n, 0, T), a[:, k, :], b[:, kk, :],
                                                        start=kk == 0 and a is wh and b is HH, stop=kk == FK - 1 and b is HL)
                        last.then_inc(half_read if half == 0 else product_done, 1)

            def halves(name, kt, act, waits):
                for n in waits:
                    wait_evicted(pe, n)
                for i in range(2):
                    s = slab_first[name] + i
                    wait_weights(pe, s)
                    for m in range(4):
                        n = first[name] + 4 * i + m
                        product(n, [(bank(n, 0, T),
                                     [(slot(s, kt, 512)[:, k, m * P:(m + 1) * P], act[:, k, :]) for k in range(kt)])])

            def quarters(name, act, count=4):
                for i in range(count):
                    s = slab_first[name] + i
                    (wait_split if act is UP else wait_weights)(pe, s)
                    for m in range(2):
                        n = first[name] + 2 * i + m
                        cols = slice(m * P, (m + 1) * P)
                        product(n, [(bank(n, 0, T), feature(parts(s, DK, 256), act, DK, cols) if act is UP else
                                     [(slot(s, DK, 256)[:, k, cols], act[:, k, :]) for k in range(DK)])])

            def tokens(n, parts, act, kt):
                product(n, [(o, [(act[:, k, tt * P:(tt + 1) * P], wk(k)) for k in range(kt)]) for o, wk, tt in parts])

            def attention(name, kind, scores, values):
                units, n_s, n_t, n_b = ATTN[kind]
                s, t, f, o, _ = attention_numbers(first[name], kind)
                base = tally.add("probs_ready", units)
                for i in range(-2, units):
                    if i >= 0:
                        pe.wait_ge(probs_ready, base + i + 1)
                        qt, par = i % 2, i % 2
                        for b in range(n_t):
                            groups = 1 if kind == "A" else 2
                            cmp = kind == "B" and b == 0
                            keys = [(0, blocks(qt))] if cmp else [(k * P, P) for k in range(NT if kind == "mem" else qt + 1)]
                            gr = []
                            for g in range(groups):
                                for k, (k0, kn) in enumerate(keys):
                                    c = (g * len(keys) + k) * P
                                    gr.append((S[:, b, par, g, k0:k0 + kn], bank(t[i] + b)[0:kn, c:c + P]))
                            wait_room(pe, t[i] + b)
                            for src, dst in gr:
                                last = nc.tensor.transpose(dst, src, ident)
                            last.then_inc(product_done, 1)
                    if i + 2 < units:
                        for b, groups in enumerate(scores(i + 2)):
                            if n_s == n_b:
                                n = s[i + 2] + b
                                product(n, [(bank(n)[:, g * T:g * T + k.shape[-1]], [(q, k)]) for g, (q, k) in enumerate(groups)])
                            else:
                                for g, (q, k) in enumerate(groups):
                                    n = s[i + 2] + 2 * b + g
                                    product(n, [(bank(n, 0, k.shape[-1]), [(q, k)])])
                    if i >= 0:
                        for j in range(DK // units):
                            m = i * (DK // units) + j
                            sl = slab_first[name] + m // 2
                            wait_weights(pe, sl)
                            product(f[i] + j, [(bank(f[i] + j, 0, T),
                                                [(slot(sl, DK, 256)[:, k, m % 2 * P:(m % 2 + 1) * P], U[:, k, :]) for k in range(DK)])])
                        for b in range(n_t):
                            wait_evicted(pe, t[i] + b)
                        wait_room(pe, o[i])
                        for rows, c, terms in values(i):
                            for j, (v, b, c0, kn) in enumerate(terms):
                                last = nc.tensor.matmul(bank(o[i])[rows, c:c + P], v, PT[0:kn, b, par, c0:c0 + P],
                                                        start=j == 0, stop=j == len(terms) - 1)
                        last.then_inc(product_done, 1)

            pe.wait_ge(inputs_in, 48)
            for l, L in enumerate(block1):
                ffn(L + "ffn1")
                norm_x(first[L + "mix.norm"], 0)
                def pairs(level):
                    pe.wait_ge(pair_ready, l * (LEVELS + 1) + level + 1)
                    if level == 0:
                        left, right = HK.rearrange("p (h t) -> p h t", t=T), HQ
                    else:
                        left = right = HX[:, (level - 1) % 2, :].rearrange("p (h t) -> p h t", t=T)
                    for tt in ((0, 1) if level < LEVELS else (0,)):
                        n = first[L + f"pairs{level}"] + tt
                        q = slice(tt * P, tt * P + P) if level < LEVELS else slice(P, 2 * P)
                        product(n, [(bank(n, h * P, h * P + P), [(left[:, h, tt * P:tt * P + P], right[:, h, q])])
                                    for h in range(HG_H)])

                for i, (c, width, count) in enumerate(WIN1):
                    n, s = first[L + f"win{i}"], slab_first[L + f"win{i}"]
                    if c == C_KR:
                        wait_weights(pe, s)
                        product(n, [(bank(n)[64:96, 0:T], [(slot(s, DK, width)[:, k, :], U[:, k, :]) for k in range(DK)])])
                    else:
                        if i:
                            wait_split(pe, s)
                        wp = parts(s, DK, width)
                    for m in range(count if c != C_KR else 0):
                        if i == m == 0:
                            product_first(n, s, [(bank(n, 0, T), wp, slice(0, P))])
                        elif C_HI <= c < C_HG:
                            product(n + m, [(bank(n + m, 0, 256), token(wp, UP, DK, slice(0, 256), m))])
                        else:
                            product(n + m, [(bank(n + m, 0, T), feature(wp, UP, DK, slice(m * P, (m + 1) * P)))])
                    if i == LATENTS_AFTER:
                        norm(first[L + "latent.norm"], LATENT_SQ, 3)
                        norm(first[L + "latent.norm"] + 1, LATENT_SQ[:, 3:5, :], 2)
                    if i >= PAIRS_AFTER:
                        pairs(i - PAIRS_AFTER)
                if l == 0:
                    pe.wait_ge(setup_done, 1)
                    n = first["bias"]
                    hot = con("hot", 2 * T, slice(0, BUCKETS + 2))
                    product(n, [(bank(n)[0:BIAS_H, :], [(TAB[0:BUCKETS + 2, :], hot)])])
                pe.wait_ge(normed, tally.n["normed"] - 2)
                for i in range(2):
                    s = slab_first[L + "uq"] + i
                    wait_weights(pe, s)
                    for m in range(4):
                        n = first[L + "uq"] + 4 * i + m
                        product(n, [(bank(n)[0:QK, 0:T], [(slot(s, 3, 384)[:, k, m * QK:(m + 1) * QK], CQ[:, k, :]) for k in range(3)])])
                pairs(LEVELS)
                pe.wait_ge(normed, tally.n["normed"])
                s = slab_first[L + "uk"]
                wait_weights(pe, s)
                for m in range(MLA_H):
                    n = first[L + "uk"] + m
                    product(n, [(bank(n)[0:NOPE, 0:T], [(slot(s, 2, 512)[:, k, m * NOPE:(m + 1) * NOPE], CKV[:, k, :]) for k in range(2)])])
                s = slab_first[L + "uv"]
                wait_weights(pe, s)
                for m in range(NT):
                    tokens(first[L + "uv"] + m, [(bank(first[L + "uv"] + m), lambda k: slot(s, 2, 512)[:, k, :], m)], CKV, 2)
                swap = con("swap", ROPE, slice(64, 96))
                for h in range(MLA_H):
                    wait_evicted(pe, first[L + "uq"] + h)
                for m in range(4):
                    n = first[L + "swap"] + m
                    product(n, [(bank(n)[64:96, :], [(swap, QH[64:96, 2 * m:2 * m + 2, :])])])
                n = first[L + "swap"] + 4
                product(n, [(bank(n)[64:96, 0:T], [(swap, KR[64:96, 0, :])])])
                pe.wait_ge(pairs_summed, l + 1)
                for i in range(2):
                    n = first[L + "hg.o"] + i
                    wait_room(pe, n)
                    for g in range(2):
                        h = 2 * i + g
                        nc.tensor.matmul(bank(n, g * T, g * T + T), VH[:, 0, h * P:h * P + P], AT[:, h, 0:2, :], start=True, stop=False)
                        last = nc.tensor.matmul(bank(n, g * T + P, g * T + T), VH[:, 1, h * P:h * P + P], AT[:, h, 2, :], start=False, stop=True)
                    last.then_inc(product_done, 1)
                quarters(L + "hg.gate0", UP, 2)
                pe.wait_ge(squares_ready, tally.add("squares_ready") + 1)
                for i in range(2):
                    n = first[L + "hg.norm"] + i
                    product(n, [(bank(n), [(ones, HG_SQ[:, 2 * i:2 * i + 2, :])])])
                quarters(L + "hg.gate1", UP, 2)
                tally.add("normed", 1)
                pe.wait_ge(normed, tally.n["normed"])
                halves(L + "hg.out", 4, OT, [])
                pe.wait_ge(roped, l + 1)
                for m in range(MLA_H):
                    wait_evicted(pe, first[L + "uk"] + m)
                for m in range(NT):
                    wait_evicted(pe, first[L + "uv"] + m)
                attention(L + "mla", "mla",
                          lambda i: [[(QH[0:QK, h, i % 2 * P:(i % 2 + 1) * P], KH[0:QK, h, 0:(i % 2 + 1) * P])
                                      for h in (i // 2 * 2, i // 2 * 2 + 1)]],
                          lambda i: [(slice(64 * g, 64 * g + 64), 0,
                                      [(VM[:, k, (i // 2 * 2 + g) * 64:(i // 2 * 2 + g + 1) * 64], 0, (g * (i % 2 + 1) + k) * P, P)
                                       for k in range(i % 2 + 1)]) for g in range(2)])
                norm(first[L + "mem.norm"], MEM_SQ, DK)
                halves(L + "mla.out", 4, OT, attention_numbers(first[L + "mla"], "mla")[3])
                pe.wait_ge(normed, tally.n["normed"])
                for i in range(4):
                    s = slab_first[L + "mem.kv"] + i
                    wait_weights(pe, s)
                    wv = slot(s, DK, 256)
                    for m in range(2):
                        n = first[L + "mem.kv"] + 2 * i + m
                        if i < 2:
                            product(n, [(bank(n, 0, T), [(wv[:, k, m * P:(m + 1) * P], MEM[:, k, :]) for k in range(DK)])])
                        else:
                            tokens(n, [(bank(n, 0, 256), lambda k: wv[:, k, :], m)], MEM, DK)
                for m in range(8):
                    wait_evicted(pe, first[L + "mem.kv"] + m)
                attention(L + "mem", "mem",
                          lambda i: [[(MQ[:, h, i % 2 * P:(i % 2 + 1) * P], MK[:, h, :]) for h in (i // 2 * 2, i // 2 * 2 + 1)]],
                          lambda i: [(slice(0, P), g * P,
                                      [(MV[:, k, (i // 2 * 2 + g) * P:(i // 2 * 2 + g + 1) * P], 0, (g * 2 + k) * P, P) for k in range(2)])
                                     for g in range(2)])
                halves(L + "mem.out", 4, OT, attention_numbers(first[L + "mem"], "mem")[3])
                pe.wait_ge(merged_ready, tally.add("merged_ready", 1) + 1)
                quarters(L + "wout", MRG)
                ffn(L + "ffn2")
            norm_x(first["1.final.norm"])

            for l, L in enumerate(block2):
                ffn(L + "ffn1")
                norm_x(first[L + "mix.norm"], 0)
                for i, (kind, c, width, count) in enumerate(WIN2):
                    n, s = first[L + f"win{i}"], slab_first[L + f"win{i}"]
                    if pl.split[s] is None:
                        wait_weights(pe, s)
                        wv = slot(s, DK, width)
                    else:
                        if i:
                            wait_split(pe, s)
                        wp = parts(s, DK, width)
                    if i == 0:
                        product_first(n, s, [(bank(n, g * T, (g + 1) * T), wp, slice(g * P, (g + 1) * P)) for g in range(2)])
                    elif kind in ("tiles", "pairs", "keys"):
                        for m in range(2):
                            product(n + m, [(bank(n + m, 0, T), feature(wp, UP, DK, slice(m * P, (m + 1) * P)))])
                    elif kind in ("tokens", "values"):
                        for m in range(NT):
                            product(n + m, [(bank(n + m, 0, 256), token(wp, UP, DK, slice(0, 256), m))])
                    elif kind == "gate":
                        tokens(n, [(bank(n, 24 * m, 24 * m + 24), lambda k: wv[:, k, :], m) for m in range(NT)], U, DK)
                    elif kind == "kv":
                        product(n, [(bank(n, 0, T), [(wv[:, k, 0:P], U[:, k, :]) for k in range(DK)])])
                        tokens(n + 1, [(bank(n + 1, P * m, P * m + P), lambda k: wv[:, k, P:2 * P], m) for m in range(NT)], U, DK)
                    elif kind == "shift":
                        product(n, [(bank(n, g * T, (g + 1) * T), feature(wp, UP, DK, slice(g * P, (g + 1) * P))) for g in range(2)])
                    if i in CMP_AFTER:
                        j = CMP_AFTER[i]
                        kv = j // 2
                        if j % 2 == 0:
                            pe.wait_ge(blocks_ready, 2 * l + kv + 1)
                        n, s = first[L + f"cmp{j}"], slab_first[L + f"cmp{j}"]
                        wait_weights(pe, s)
                        product(n, [(bank(n, 30 * half, 30 * half + 30),
                                     [(slot(s, DK, 256)[:, k, half * P:half * P + P], (BLK, BLK2)[kv][:, j % 2 * DK + k, :]) for k in range(DK)])
                                    for half in range(2)])
                    if i == CMP2_AFTER:
                        s = slab_first[L + "cmp.out"]
                        wait_weights(pe, s)
                        w2 = slot(s, 4, 64)
                        n = first[L + "cmp.out"]
                        pe.wait_ge(hidden_ready, 2 * l + 1)
                        product(n, [(bank(n)[64 * g:64 * g + 64, 0:15], [(w2[:, half, :], HID[:, half, 15 * g:15 * g + 15]) for half in range(2)])
                                    for g in range(2)])
                        pe.wait_ge(hidden_ready, 2 * l + 2)
                        product(n + 1, [(bank(n + 1)[0:15, 64 * g:64 * g + 64], [(HID2[:, half, 15 * g:15 * g + 15], w2[:, 2 + half, :]) for half in range(2)])
                                        for g in range(2)])

                def win_evicted(steps):
                    for i in steps:
                        for m in range(WIN2[i][3]):
                            wait_evicted(pe, first[L + f"win{i}"] + m)

                win_evicted(range(2, 8))
                attention(L + "A", "A",
                          lambda i: [[(AQ[64 * g:64 * g + 64, i // 2, i % 2 * P:(i % 2 + 1) * P], AK[64 * g:64 * g + 64, i // 2, 0:(i % 2 + 1) * P])
                                      for g in range(2)]],
                          lambda i: [(slice(0, P), 0, [(AV[:, k, i // 2 * P:(i // 2 + 1) * P], 0, k * P, P) for k in range(i % 2 + 1)])])
                pe.wait_ge(squares_ready, tally.add("squares_ready") + 1)
                for i in range(2):
                    n = first[L + "A.norm"] + i
                    product(n, [(bank(n), [(ones, AQ[:, 2 * i:2 * i + 2, :])])])
                tally.add("normed", 1)
                pe.wait_ge(normed, tally.n["normed"])
                halves(L + "A.out", 4, OT, [])
                win_evicted((8, 10, 12, 13))
                wait_evicted(pe, first[L + "cmp.out"])
                wait_evicted(pe, first[L + "cmp.out"] + 1)

                def b_scores(i):
                    q = [BQ[64 * g:64 * g + 64, i // 2, i % 2 * P:(i % 2 + 1) * P] for g in range(2)]
                    n = (i % 2 + 1) * P
                    return [[(q[g], kk[64 * g:64 * g + 64, 0:m]) for g in range(2)] for kk, m in ((KCMP, blocks(i % 2)), (BKS, n), (BKW, n))]

                def b_values(i):
                    out = []
                    for g in range(2):
                        nb = blocks(i % 2)
                        terms = [(VCMP[0:nb, g, :], 0, g * P, nb)]
                        for b, vv in ((1, BVS), (2, BVW)):
                            terms += [(vv[:, k, 64 * g:64 * g + 64], b, (g * (i % 2 + 1) + k) * P, P) for k in range(i % 2 + 1)]
                        out.append((slice(64 * g, 64 * g + 64), 0, terms))
                    return out

                attention(L + "B", "B", b_scores, b_values)
                halves(L + "B.out", 4, OT, attention_numbers(first[L + "B"], "B")[3])
                win_evicted((11, 14, 15))
                attention(L + "C", "C",
                          lambda i: [[(CQ2[64 * g:64 * g + 64, i // 2, i % 2 * P:(i % 2 + 1) * P], CK2[64 * g:64 * g + 64, 0:(i % 2 + 1) * P])
                                      for g in range(2)]],
                          lambda i: [(slice(64 * g, 64 * g + 64), 0,
                                      [(CV2[:, k, 64 * g:64 * g + 64], 0, (g * (i % 2 + 1) + k) * P, P) for k in range(i % 2 + 1)])
                                     for g in range(2)])
                halves(L + "C.out", 4, OT, attention_numbers(first[L + "C"], "C")[3])
                pe.wait_ge(merged_ready, tally.add("merged_ready", 1) + 1)
                quarters(L + "wout", MRG)
                ffn(L + "ffn2")
                norm_x(first[L + "ple.norm"], 0)
                s = slab_first[L + "ple.p"]
                wait_weights(pe, s)
                pe.wait_ge(layer_in, 16 * (l + 1))
                for m in range(DK):
                    n = first[L + "ple.p"] + m
                    product(n, [(bank(n, 0, T), [(slot(s, 2, D)[:, k, m * P:(m + 1) * P], PIN[:, k, :]) for k in range(2)])])
                u_parts()
                quarters(L + "ple.gate", UP)
            norm_x(first["2.final.norm"])

        @block.scalar
        def _(act):
            tally = Tally()

            def link(ins):
                ins.then_inc(act_step, 1)
                act.wait_ge(act_step, tally.add("act_step") + 1)

            def evict(n, dst, src, func=ACT.Copy):
                wait_product(act, n)
                nc.scalar.activation(dst, src, func).then_inc(evicted[n % BANKS], 1)

            def norm(v=V, r=RSTD):
                act.wait_ge(mean_ready, tally.add("mean_ready") + 1)
                link(nc.scalar.activation(r, v, ACT.Ln))
                nc.scalar.activation(r, r, ACT.Exp, scale=-0.5).then_inc(rstd_ready, 1)

            def norm_x(n):
                wait_product(act, n)
                nc.scalar.activation(RSTD[:], bank(n, 0, T), ACT.Ln, bias=con("eps", 1), scale=1.0 / D).then_inc(evicted[n % BANKS], 1)
                wait_evicted(act, n)
                nc.scalar.activation(RSTD[:], RSTD[:], ACT.Exp, scale=-0.5).then_inc(rstd_ready, 1)

            def take_high(s):
                nc.scalar.activation(part(WH, s), RING[:, s % SLOTS, 0:pl.words[s]], ACT.Copy).then_inc(weights_high, 1)

            def feed_high(s):
                wait_weights(act, s)
                if pl.split[s] >= SLOTS:
                    wait_product(act, pl.slab_last[pl.splits[pl.split[s] - SLOTS]])
                take_high(s)

            feed = Feed(feed_high)

            def norm_u(n, s):
                feed.to(s)
                norm_x(n)
                full = tally.add("u_full", DK)
                for k in range(DK):
                    act.wait_ge(u_full, full + k + 1)
                    nc.scalar.activation(UH[:, k, :], U[:, k, :], ACT.Copy).then_inc(u_high, 1)

            def ffn(name):
                s0, p0 = slab_first[name + ".in"], first[name + ".in"]
                half = tally.add("half_read", DK)

                def high(r, j):
                    wait_weights(act, s0 + j, r)
                    if j < FK + 2 and (j >= 2 or not isinstance(r, int)):
                        wait_product(act, p0 + 2 * (j - 2) + 1, r)
                    elif j >= FK + 2 and j % 2 == 0:
                        act.wait_ge(half_read, half + (j - FK) // 2)
                    elif j >= FK + 2:
                        wait_product(act, first[name + ".out"] + (j - FK) // 2 - 1)
                    elif pl.split[s0 + j] >= SLOTS:
                        wait_product(act, pl.slab_last[pl.splits[pl.split[s0 + j] - SLOTS]])
                    take_high(s0 + j)

                def hidden_part(r, j):
                    wait_evicted(act, p0 + 2 * j + 1, r)
                    nc.scalar.activation(HH[:, bass.ds(r * UNROLL + j, 1), :], HF[:, j % 2:j % 2 + 1, :], ACT.Copy)\
                      .then_inc(hidden_high, 1)

                norm_u(first[name + ".norm"], s0)

                def pair(r, j):
                    n = p0 + 2 * j
                    high(r, j + 1)
                    wait_product(act, n, r)
                    if not isinstance(r, int) or j >= 2:
                        wait_evicted(act, n - 3, r)
                    nc.scalar.activation(SILU[:, j % 2, :], bank(n, 0, T), ACT.Silu).then_inc(evicted[n % BANKS], 1)
                    if j or not isinstance(r, int):
                        hidden_part(r, j - 1)

                rounds(act, FK, pair)
                high(0, FK + 1)
                hidden_part(0, FK - 1)
                for j in range(FK + 2, FK + 2 * DK):
                    high(0, j)
                feed.q += FK + 2 * DK - 1

            def attention(name, kind, scale=1.0, merged=None):
                units, n_s, n_t, n_b = ATTN[kind]
                s, t, f, o, _ = attention_numbers(first[name], kind)
                n_f = DK // units
                if merged:
                    for m in range(DK):
                        wait_evicted(act, first[merged] + m)
                base = tally.add("max_ready", units)
                for i in range(units + 1):
                    if i < units:
                        qt = par = i % 2
                        act.wait_ge(max_ready, base + i + 1)
                        for b in range(n_b):
                            cmp = kind == "B" and b == 0
                            nk = blocks(qt) if cmp else T if kind == "mem" else (qt + 1) * P
                            nk += kind == "C"
                            for g in range(2):
                                src = bank(s[i])[:, g * T:(g + 1) * T] if kind == "mem" else S[:, b, par, g, 0:nk]
                                last = nc.scalar.activation(S[:, b, par, g, 0:nk], src, ACT.Exp, bias=MX[:, par, b, g:g + 1],
                                                            scale=scale, accum_out=SUM[:, par, b, g:g + 1])
                        last.then_inc(evicted[s[i] % BANKS] if kind == "mem" else exp_done, 1)
                    if i >= 1:
                        u = i - 1
                        if u >= 2:
                            wait_product(act, o[u - 2])
                        for b in range(n_t):
                            cmp = kind == "B" and b == 0
                            keys = 1 if cmp else NT if kind == "mem" else u % 2 + 1
                            c = (1 if kind == "A" else 2) * keys * P
                            rows = slice(0, blocks(u % 2)) if cmp else slice(0, P)
                            evict(t[u] + b, PT[rows, b, u % 2, 0:c], bank(t[u] + b)[rows, 0:c])
                        for j in range(n_f):
                            evict(f[u] + j, GATE[:, u * n_f + j, :], bank(f[u] + j, 0, T), ACT.Sigmoid)

            def tables():
                act.wait_ge(angle_ready, 1)
                nc.scalar.activation(SIN[64:96, :], SIN[64:96, :], ACT.Sin)
                nc.scalar.activation(COS[64:96, :], COS[64:96, :], ACT.Sin).then_inc(rope_ready, 1)
                act.wait_ge(angle_ready, 2)
                link(nc.scalar.activation(LB[:, 2, :], LB[:, 1, :], ACT.Exp, scale=-1.0))
                nc.scalar.activation(LB[:, 2, :], LB[:, 2, :], ACT.Ln, bias=1.0).then_inc(rope_ready, 1)
                act.wait_ge(angle_ready, 3)
                nc.scalar.activation(LAM[:, 2:4, :], LAM[:, 0:2, :], ACT.Exp).then_inc(lambda_ready, 1)

            tables()
            for l, L in enumerate(block1):
                ffn(L + "ffn1")
                norm_u(first[L + "mix.norm"], slab_first[L + "win0"])
                HA, HB = HX[:, 0, :], HX[:, 1, :]
                for i, (c, width, count) in enumerate(WIN1):
                    feed.to(slab_first[L + f"win{i}"] + 1)
                    if i == 4:
                        act.wait_ge(hg_vec, tally.add("hg_vec") + 1)
                        link(nc.scalar.activation(HB, HA, ACT.Exp, scale=-1.0))
                        nc.scalar.activation(HB, HB, ACT.Ln, bias=1.0).then_inc(hg_act, 1)
                    if i == 5:
                        act.wait_ge(hg_vec, tally.add("hg_vec") + 1)
                        if l == 0:
                            nc.scalar.activation(HK, HK, ACT.Exp).then_inc(hg_act, 1)
                        else:
                            for h in range(HG_H):
                                k = HK[:, h * T:(h + 1) * T]
                                last = nc.scalar.activation(k, k, ACT.Exp, bias=LB[:, 4, h:h + 1])
                            last.then_inc(hg_act, 1)
                            act.wait_ge(hg_vec, tally.add("hg_vec") + 1)
                            link(nc.scalar.activation(HB, HA, ACT.Exp, scale=-1.0))
                            nc.scalar.activation(HB, HB, ACT.Ln, bias=1.0).then_inc(hg_act, 1)
                    if i >= PAIRS_AFTER:
                        level = i - PAIRS_AFTER
                        act.wait_ge(hg_vec, tally.add("hg_vec") + 1)
                        nc.scalar.activation(HX[:, level % 2, :], HX[:, level % 2, :], ACT.Exp).then_inc(hg_act, 1)
                    for m in range(count):
                        n = first[L + f"win{i}"] + m
                        if c == C_KR:
                            evict(n, KR[64:96, 0, :], bank(n)[64:96, 0:T])
                        elif C_HI <= c < C_HG:
                            evict(n, VH[:, m, c - C_HI:c - C_HI + 256], bank(n, 0, 256))
                        else:
                            for c0, dst, func in ((C_MQ, MQ, ACT.Copy), (C_HG, HGT, ACT.Silu),
                                                  (C_HF, Z.rearrange("p (h t) -> p h t", t=T), ACT.Copy),
                                                  (C_HQ, HQ, ACT.Silu), (C_KV, CKV, ACT.Copy), (C_Q, CQ, ACT.Copy)):
                                if c >= c0:
                                    evict(n, dst[:, (c - c0) // P + m, :], bank(n, 0, T), func)
                                    break
                    if i == LATENTS_AFTER:
                        norm(V[:], RSTD[:])
                        norm(V[:], RSTD[:])
                if l == 0:
                    evict(first["bias"], ROWS[0:BIAS_H, :], bank(first["bias"])[0:BIAS_H, :])
                for h in range(MLA_H):
                    evict(first[L + "uq"] + h, QH[0:QK, h, :], bank(first[L + "uq"] + h)[0:QK, 0:T])
                for h in range(MLA_H):
                    evict(first[L + "uk"] + h, KH[0:NOPE, h, :], bank(first[L + "uk"] + h)[0:NOPE, 0:T])
                gate0, gate1 = slab_first[L + "hg.gate0"], slab_first[L + "hg.gate1"]
                feed.to(gate0)
                for m in range(NT):
                    evict(first[L + "uv"] + m, VM[:, m, :], bank(first[L + "uv"] + m))
                for i in range(2):
                    evict(first[L + "hg.o"] + i, OT[:, 2 * i:2 * i + 2, :], bank(first[L + "hg.o"] + i))
                def hg_gate(m, s):
                    feed.to(s)
                    for m in (m, m + 1):
                        n = first[L + f"hg.gate{m // 4}"] + m % 4
                        evict(n, GATE[:, m, :], bank(n, 0, T), ACT.Sigmoid)

                hg_gate(0, gate0 + 1)
                hg_gate(2, gate1)
                norm(TMP[:], TMP[:])
                hg_gate(4, gate1 + 1)
                hg_gate(6, gate1 + 1)
                attention(L + "mla", "mla", merged=L + "hg.out")
                norm(V[:], RSTD[:])
                for i in range(8):
                    n = first[L + "mem.kv"] + i
                    if i < 4:
                        evict(n, MK[:, i, :], bank(n, 0, T))
                    else:
                        c = (i - 4) // 2 * 256
                        evict(n, MV[:, i % 2, c:c + 256], bank(n, 0, 256))
                attention(L + "mem", "mem", P ** -0.5, merged=L + "mla.out")
                ffn(L + "ffn2")
            norm_x(first["1.final.norm"])

            for l, L in enumerate(block2):
                ffn(L + "ffn1")
                norm_u(first[L + "mix.norm"], slab_first[L + "win0"])
                for i, (kind, c, width, count) in enumerate(WIN2):
                    n = first[L + f"win{i}"]
                    if i + 1 < len(WIN2):
                        feed.to(slab_first[L + f"win{i + 1 + (WIN2[i + 1][0] in ('gate', 'kv'))}"])
                    if kind in ("tiles", "pairs"):
                        for c0, dst, func in ((D_CQ, CQ2, ACT.Copy), (D_BQ, BQ, ACT.Copy),
                                              (D_AK, AK, ACT.Copy), (D_AQ, AQ, ACT.Copy)):
                            if c >= c0:
                                tile = (c - c0) // (64 if kind == "pairs" else P)
                                for m in range(2):
                                    evict(n + m, dst[:, tile + m, :], bank(n + m, 0, T), func)
                                break
                    elif kind == "tokens":
                        for m in range(NT):
                            evict(n + m, AV[:, m, c - D_AV:c - D_AV + 256], bank(n + m, 0, 256))
                    elif kind == "gate":
                        evict(n, BG, bank(n, 0, 24 * NT).rearrange("p (m c) -> p m c", m=NT), ACT.Sigmoid)
                    elif kind == "kv":
                        evict(n, CK2, bank(n, 0, T))
                        evict(n + 1, CV2, bank(n + 1, 0, NT * P).rearrange("p (m c) -> p m c", m=NT))
                    elif kind == "keys":
                        evict(n, BKS, bank(n, 0, T))
                        evict(n + 1, BKW, bank(n + 1, 0, T))
                    elif kind == "values":
                        for m in range(NT):
                            evict(n + m, BV[:, m], bank(n + m, 0, 256))
                    elif kind == "shift":
                        dst = KC2 if c == D_BKC else VC2
                        b3 = bank(n).rearrange("p (g t) -> p g t", g=2)
                        wait_product(act, n)
                        nc.scalar.activation(dst[0:64, :, :], b3[0:64], ACT.Copy)
                        nc.scalar.activation(dst[64:128, :, 0:T - 1], b3[64:128, :, 1:T], ACT.Copy)\
                          .then_inc(evicted[n % BANKS], 1)
                    if i in GELU_AFTER:
                        act.wait_ge(gelu_vec, tally.add("gelu_vec") + 1)
                        nc.scalar.activation(GY, GY, ACT.Exp, scale=-2.0 * (2.0 / np.pi) ** 0.5).then_inc(gelu_act, 1)
                    if i == CMP2_AFTER:
                        n = first[L + "cmp.out"]
                        evict(n, KCMP[:, 0:15], bank(n, 0, 15))
                        evict(n + 1, VCMP[0:15, :, :], bank(n + 1)[0:15, 0:P].rearrange("p (g d) -> p g d", g=2))
                attention(L + "A", "A")
                norm(TMP[:], TMP[:])
                attention(L + "B", "B", merged=L + "A.out")
                attention(L + "C", "C", merged=L + "B.out")
                ffn(L + "ffn2")
                norm_u(first[L + "ple.norm"], slab_first[L + "ple.gate"])
                for m in range(DK):
                    evict(first[L + "ple.p"] + m, PLE[:, m, :], bank(first[L + "ple.p"] + m, 0, T))
                for m in range(DK):
                    if m % 2 == 0:
                        feed.to(slab_first[L + "ple.gate"] + m // 2 + 1)
                    evict(first[L + "ple.gate"] + m, GATE[:, m, :], bank(first[L + "ple.gate"] + m, 0, T), ACT.Sigmoid)
            norm_x(first["2.final.norm"])

        @block.vector
        def _(dve):
            tally = Tally()
            v_ = nc.vector

            def link(ins):
                ins.then_inc(vec_step, 1)
                dve.wait_ge(vec_step, tally.add("vec_step") + 1)

            def norm_x(gain, dst, done=normed):
                dve.wait_ge(rstd_ready, tally.add("rstd_ready") + 1)
                for k in range(DK):
                    v_.scalar_tensor_tensor(dst[:, k, :], X[:, k, :], gain[:, k:k + 1], RSTD[:], ALU.mult, ALU.mult)\
                      .then_inc(done, 1)

            def add_squares(m):
                if m == 0:
                    link(v_.tensor_tensor(ACC, X[:, 0, :], X[:, 0, :], ALU.mult))
                    return
                link(v_.tensor_tensor(SQX, X[:, m, :], X[:, m, :], ALU.mult))
                added = v_.tensor_tensor(ACC, ACC, SQX, ALU.add)
                if m < DK - 1:
                    link(added)
                else:
                    added.then_inc(squares_ready, 1)

            def add_to_x(name, factor, m):
                n = first[name] + m
                wait_product(dve, n)
                v_.scalar_tensor_tensor(X[:, m, :], bank(n, 0, T), factor, X[:, m, :], ALU.mult, ALU.add)\
                  .then_inc(evicted[n % BANKS], 1)
                wait_evicted(dve, n)
                add_squares(m)

            def take_low(s, r=0):
                dve.wait_ge(weights_high, r * UNROLL + pl.split[s] + 1)
                v_.tensor_tensor(part(WL, s), RING[:, s % SLOTS, 0:pl.words[s]], part(WH, s).bitcast(FP), ALU.subtract)\
                  .then_inc(weights_low, 1)

            feed = Feed(take_low)

            def norm_u(gain, s):
                u = tally.add("u_high", DK)
                norm_x(gain, U, done=u_full)
                feed.to(s)
                for k in range(DK):
                    dve.wait_ge(u_high, u + k + 1)
                    v_.tensor_tensor(UL[:, k, :], U[:, k, :], UH[:, k, :].bitcast(FP), ALU.subtract).then_inc(u_low, 1)

            def ffn(name, gain):
                s0, p0 = slab_first[name + ".in"], first[name + ".in"]
                hidden = tally.add("hidden", FK)
                norm_u(gain, s0)
                dve.wait_ge(u_low, tally.n["u_high"])

                def low(r, j):
                    take_low(s0 + j, r)

                def hidden_part(r, j):
                    dve.wait_ge(hidden_high, r * UNROLL + hidden + j + 1)
                    v_.tensor_tensor(HL[:, bass.ds(r * UNROLL + j, 1), :], HF[:, j % 2:j % 2 + 1, :],
                                     HH[:, bass.ds(r * UNROLL + j, 1), :].bitcast(FP), ALU.subtract).then_inc(hidden_low, 1)

                def pair(r, j):
                    n = p0 + 2 * j
                    low(r, j + 1)
                    wait_evicted(dve, n, r)
                    wait_product(dve, n + 1, r)
                    if not isinstance(r, int) or j >= 2:
                        dve.wait_ge(hidden_low, r * UNROLL + hidden + j - 1)
                    v_.tensor_tensor(HF[:, j % 2, :], SILU[:, j % 2, :], bank(n + 1, 0, T), ALU.mult)\
                      .then_inc(evicted[(n + 1) % BANKS], 1)
                    if j or not isinstance(r, int):
                        hidden_part(r, j - 1)

                rounds(dve, FK, pair)
                low(0, FK + 1)
                hidden_part(0, FK - 1)
                for m in range(DK):
                    if m < DK - 1:
                        low(0, FK + 2 * m + 2)
                    add_to_x(name + ".out", 0.5, m)
                    if m < DK - 1:
                        low(0, FK + 2 * m + 3)
                feed.q += FK + 2 * DK - 1

            def merge(name, start=False, end=False):
                for m in range(DK):
                    n = first[name] + m
                    g = GATE[:, m, :]
                    wait_product(dve, n)
                    if start:
                        v_.tensor_tensor(MRG[:, m, :], bank(n, 0, T), g, ALU.mult).then_inc(evicted[n % BANKS], 1)
                    else:
                        v_.tensor_tensor(TMP[:, m % 2, 0:T], bank(n, 0, T), g, ALU.mult).then_inc(evicted[n % BANKS], 1)
                        wait_evicted(dve, n)
                        link(v_.tensor_tensor(MRG[:, m, :], MRG[:, m, :], TMP[:, m % 2, 0:T], ALU.add))
                if end:
                    v_.tensor_copy(MRG[:, DK - 1, T - 1:T], MRG[:, DK - 1, T - 1:T]).then_inc(merged_ready, 1)
                else:
                    for m in range(DK):
                        wait_evicted(dve, first[name] + m)

            def attention(name, kind, scale, window=None, lam=None, sinks=None):
                units, n_s, n_t, n_b = ATTN[kind]
                s, t, f, o, _ = attention_numbers(first[name], kind)
                exps = tally.add("exp_done", 0 if kind == "mem" else units)

                def scores(i):
                    qt = par = i % 2
                    for b in range(n_b):
                        n = s[i] + b
                        cmp = kind == "B" and b == 0
                        nk = blocks(qt) if cmp else T if kind == "mem" else (qt + 1) * P
                        if kind == "mem":
                            wait_product(dve, n)
                            sc = bank(n).rearrange("p (g t) -> p g t", g=2)[:, :, 0:nk]
                            link(v_.reduce_max(MX[:, par, b, :], sc, AX.X))
                            continue
                        if i >= 2:
                            wait_product(dve, t[i - 2] + b)
                        if n_s == n_b:
                            wait_product(dve, n)
                            sc = bank(n).rearrange("p (g t) -> p g t", g=2)[:, :, 0:nk]
                            v_.scalar_tensor_tensor(S[:, b, par, :, 0:nk], sc, scale, window(i, b), ALU.mult, ALU.add)\
                              .then_inc(evicted[n % BANKS], 1)
                        else:
                            for g in range(2):
                                n = s[i] + 2 * b + g
                                wait_product(dve, n)
                                v_.scalar_tensor_tensor(S[:, b, par, g, 0:nk], bank(n, 0, nk), scale, window(i, b)[:, g, :],
                                                        ALU.mult, ALU.add).then_inc(evicted[n % BANKS], 1)
                            wait_evicted(dve, n - 1)
                        if kind == "C":
                            link(v_.tensor_copy(S[:, b, par, :, nk:nk + 1], sinks[:, i // 2 * 2:i // 2 * 2 + 2].unsqueeze(2)))
                            nk += 1
                        wait_evicted(dve, n)
                        link(v_.reduce_max(MX[:, par, b, :], S[:, b, par, :, 0:nk], AX.X))
                    v_.tensor_scalar(MX[:, par, 0:n_b, :], MX[:, par, 0:n_b, :], -scale if kind == "mem" else -1.0, None, ALU.mult)\
                      .then_inc(max_ready, 1)

                def scale_probs(i):
                    qt = par = i % 2
                    if kind == "mem":
                        wait_evicted(dve, s[i])
                    else:
                        dve.wait_ge(exp_done, exps + i + 1)
                    link(v_.reciprocal(SUM[:, par, 0:n_b, :], SUM[:, par, 0:n_b, :]))
                    if kind == "A":
                        link(v_.tensor_scalar(SUM[:, par, 0, 1:2], SUM[:, par, 0, 1:2], lam, None, ALU.mult))
                        p0, p1 = S[:, 0, par, 0, 0:(qt + 1) * P], S[:, 0, par, 1, 0:(qt + 1) * P]
                        link(v_.tensor_scalar(p0, p0, SUM[:, par, 0, 0:1], None, ALU.mult))
                        v_.scalar_tensor_tensor(p0, p1, SUM[:, par, 0, 1:2], p0, ALU.mult, ALU.add).then_inc(probs_ready, 1)
                        return
                    if kind == "B":
                        gates = BG[:, qt, :].rearrange("p (g j b) -> p j b g", g=2, j=4)[:, i // 2]
                        link(v_.tensor_tensor(SUM[:, par, :, :], SUM[:, par, :, :], gates, ALU.mult))
                        if qt == 0:
                            link(v_.tensor_scalar(SUM[:, par, 0, :], SUM[:, par, 0, :], con("sees", 1), None, ALU.mult))
                    for b in range(n_b):
                        nk = blocks(qt) if kind == "B" and b == 0 else T if kind == "mem" else (qt + 1) * P
                        for g in range(2):
                            p = S[:, b, par, g, 0:nk]
                            last = v_.tensor_scalar(p, p, SUM[:, par, b, g:g + 1], None, ALU.mult)
                    last.then_inc(probs_ready, 1)

                def outputs(i):
                    wait_product(dve, o[i])
                    j, q = i // 2, slice(i % 2 * P, i % 2 * P + P)
                    if kind == "mem":
                        dst, src = OT[:, 2 * j:2 * j + 2, q], bank(o[i], 0, 2 * P).rearrange("p (g t) -> p g t", g=2)
                    else:
                        dst, src = OT[:, j, q], bank(o[i], 0, P)
                    v_.tensor_copy(dst, src).then_inc(evicted[o[i] % BANKS], 1)

                scores(0)
                for i in range(units):
                    if i + 1 < units:
                        scores(i + 1)
                    scale_probs(i)
                    if i >= 1:
                        outputs(i - 1)
                outputs(units - 1)
                return o

            def group_norm(name, squares, count, slabs=()):
                v_.tensor_tensor(squares, OT, OT, ALU.mult).then_inc(squares_ready, 1)
                for s in slabs[:1]:
                    feed.to(s)
                for i in range(2):
                    n = first[name] + i
                    wait_product(dve, n)
                    v_.tensor_scalar(TMP[:, i, :], bank(n), 1.0 / count, EPS, ALU.mult, ALU.add)\
                      .then_inc(evicted[n % BANKS], 1)
                    wait_evicted(dve, n)
                v_.tensor_copy(TMP[:, 0, 0:1], TMP[:, 0, 0:1]).then_inc(mean_ready, 1)
                for s in slabs[1:]:
                    feed.to(s)
                dve.wait_ge(rstd_ready, tally.add("rstd_ready") + 1)

            def tables():
                link(v_.tensor_copy(V[64:96, :], COS[64:96, :].bitcast(I32)))
                link(v_.tensor_scalar(V[64:96, :], V[64:96, :], con("freq", 1, slice(64, 96)), None, ALU.mult))
                for table, turn in ((SIN, 0.0), (COS, 0.25)):
                    a, n, r = V[64:96, :], TMP[64:96, 0, T:2 * T], table[64:96, :]
                    link(v_.tensor_scalar(n, a, 1.0 / (2.0 * np.pi), turn, ALU.mult, ALU.add))
                    link(v_.tensor_scalar(n, n, 12582912.0, None, ALU.add))
                    link(v_.tensor_scalar(n, n, -12582912.0, None, ALU.add))
                    link(v_.scalar_tensor_tensor(r, n, -TURN[0], a, ALU.mult, ALU.add))
                    link(v_.scalar_tensor_tensor(r, n, -TURN[1], r, ALU.mult, ALU.add))
                    link(v_.scalar_tensor_tensor(r, n, -TURN[2], r, ALU.mult, ALU.add))
                    link(v_.tensor_scalar(r, r, turn * 2.0 * np.pi, None, ALU.add))
                    link(v_.tensor_scalar(r, r, 3.1415925, -3.1415925, ALU.min, ALU.max))
                v_.memset(RESET, 1.0).then_inc(angle_ready, 1)
                link(v_.tensor_tensor(LB[:, 0, :], vec("lb1", HG_H), vec("lb0", HG_H), ALU.subtract))
                v_.scalar_tensor_tensor(LB[:, 1, :], LB[:, 0, :], -1.0, LB[:, 0, :], ALU.mult, ALU.max).then_inc(angle_ready, 1)
                dve.wait_ge(rope_ready, 2)
                link(v_.scalar_tensor_tensor(LB[:, 3, :], LB[:, 0, :], 0.0, LB[:, 2, :], ALU.min, ALU.subtract))
                link(v_.tensor_tensor(LB[:, 4, :], LB[:, 3, :], LB[:, 0, :], ALU.subtract))
                link(v_.tensor_tensor(LB[:, 5, :], LB[:, 4, :], LB[:, 3, :], ALU.subtract))
                for l in range(DEPTH):
                    pairs = vec(f"lambda{l}", 256).rearrange("p (a b d) -> p a b d", a=2, b=2)
                    prod = TMP[:, l, 0:P].rearrange("p (a d) -> p a d", a=2)
                    link(v_.tensor_tensor(prod, pairs[:, :, 0, :], pairs[:, :, 1, :], ALU.mult))
                    link(v_.reduce_sum(LAM[:, 0:2, l], prod, AX.X))
                v_.memset(RESET.rearrange("p (c t) -> p c t", t=CHUNK)[:, :, 0:1], 0.0).then_inc(angle_ready, 1)
                dve.wait_ge(lambda_ready, 1)
                link(v_.tensor_tensor(LAM[:, 4, :], LAM[:, 3, :], LAM[:, 2, :], ALU.subtract))
                for l in range(DEPTH):
                    link(v_.tensor_scalar(LAM[:, 5, l:l + 1], LAM[:, 4, l:l + 1], -LAM_INIT[l], None, ALU.add))
                v_.tensor_copy(TAB[0:BUCKETS, :], vec("rel_bias", BIAS_H, slice(0, BUCKETS)))
                v_.tensor_copy(TAB[BUCKETS:BUCKETS + 2, :], con("mask_rows", BIAS_H, slice(BUCKETS, BUCKETS + 2))).then_inc(setup_done, 1)

            dve.wait_ge(inputs_in, 48)
            tables()
            dve.wait_ge(x_in, 16)
            for m in range(DK):
                add_squares(m)
            heads = "p (h t) -> p h t"
            for l, L in enumerate(block1):
                ffn(L + "ffn1", vec(f"ffn1_norm{l}", DK))
                norm_u(vec(f"mix_norm{l}", DK), slab_first[L + "win0"])
                win0 = slab_first[L + "win0"]
                feed.to(win0 + 1)
                HA, HB = HX[:, 0, :], HX[:, 1, :]
                if l > 0:
                    link(v_.memset(RESET, 1.0))
                    link(v_.memset(RESET.rearrange("p (c t) -> p c t", t=CHUNK)[:, :, 0:1], 0.0))
                for i in range(4):
                    feed.to(win0 + i + 1)
                    for m in range(2):
                        wait_evicted(dve, first[L + f"win{i}"] + m)
                v_.scalar_tensor_tensor(HA, Z, -1.0, Z, ALU.mult, ALU.max).then_inc(hg_vec, 1)
                feed.to(win0 + 5)
                dve.wait_ge(hg_act, tally.add("hg_act") + 1)
                link(v_.scalar_tensor_tensor(GS, Z, 0.0, HB, ALU.min, ALU.subtract))
                v_.tensor_tensor(HK, GS, Z, ALU.subtract).then_inc(hg_vec, 1)
                feed.to(win0 + 6)
                dve.wait_ge(hg_act, tally.add("hg_act") + 1)
                g = GS
                if l > 0:
                    for h in range(HG_H):
                        c = slice(h * T, (h + 1) * T)
                        link(v_.tensor_scalar(Z[:, c], GS[:, c], LB[:, 5, h:h + 1], None, ALU.add))
                    v_.scalar_tensor_tensor(HA, Z, -1.0, Z, ALU.mult, ALU.max).then_inc(hg_vec, 1)
                    dve.wait_ge(hg_act, tally.add("hg_act") + 1)
                    link(v_.scalar_tensor_tensor(Z, Z, 0.0, HB, ALU.max, ALU.add))
                    for h in range(HG_H):
                        c = slice(h * T, (h + 1) * T)
                        link(v_.tensor_scalar(Z[:, c], Z[:, c], LB[:, 3, h:h + 1], None, ALU.add))
                    src, GC = Z, GS
                else:
                    src, GC = GS, Z
                v_.tensor_tensor_scan(GC, RESET, src, 0.0, ALU.mult, ALU.add).then_inc(pair_ready, 1)
                dve.wait_ge(pair_ready, l * (LEVELS + 1) + 1)

                def exponents(level):
                    x = HX[:, level % 2, :]
                    if level < 6:
                        n = 1 << level
                        gv = GC.rearrange("p (b two n) -> p b two n", two=2, n=n)
                        xv = x.rearrange("p (b two n) -> p b two n", two=2, n=n)
                        pivot = gv[:, :, 0, n - 1:n].broadcast_to([P, HG_H * T // (2 * n), n])
                        v_.tensor_tensor(xv[:, :, 1, :], gv[:, :, 1, :], pivot, ALU.subtract)
                        v_.tensor_tensor(xv[:, :, 0, :], pivot, gv[:, :, 0, :], ALU.subtract).then_inc(hg_vec, 1)
                        return
                    gv = GC.rearrange("p (h c n) -> p h c n", h=HG_H, n=CHUNK)
                    xv = x.rearrange("p (h c n) -> p h c n", h=HG_H, n=CHUNK)

                    def end(c):
                        return gv[:, :, c, CHUNK - 1:CHUNK].broadcast_to([P, HG_H, CHUNK])

                    if level == 6:
                        v_.tensor_copy(xv[:, :, 1, :], gv[:, :, 1, :])
                        v_.tensor_copy(xv[:, :, 3, :], gv[:, :, 3, :])
                        v_.tensor_tensor(xv[:, :, 0, :], end(0), gv[:, :, 0, :], ALU.subtract)
                        v_.tensor_tensor(xv[:, :, 2, :], end(2), gv[:, :, 2, :], ALU.subtract).then_inc(hg_vec, 1)
                    else:
                        link(v_.tensor_tensor(xv[:, :, 0, :], end(0), gv[:, :, 0, :], ALU.subtract))
                        v_.tensor_copy(xv[:, :, 2, :], gv[:, :, 2, :])
                        v_.tensor_tensor(xv[:, :, 3, :], gv[:, :, 3, :], end(2), ALU.add)
                        v_.tensor_tensor(xv[:, :, 1, :], end(1), gv[:, :, 1, :], ALU.subtract)
                        v_.tensor_tensor(xv[:, :, 0, :], xv[:, :, 0, :], end(1), ALU.add).then_inc(hg_vec, 1)

                def factors(level):
                    dve.wait_ge(hg_act, tally.add("hg_act") + 1)
                    n = 1 << level
                    xv = HX[:, level % 2, :].rearrange("p (b two n) -> p b two n", two=2, n=n)
                    kv = HK.rearrange("p (b two n) -> p b two n", two=2, n=n)
                    qv = HQ.rearrange("p h t -> p (h t)").rearrange("p (b two n) -> p b two n", two=2, n=n)
                    v_.tensor_tensor(xv[:, :, 0, :], xv[:, :, 0, :], kv[:, :, 0, :], ALU.mult)
                    v_.tensor_tensor(xv[:, :, 1, :], xv[:, :, 1, :], qv[:, :, 1, :], ALU.mult).then_inc(pair_ready, 1)

                def masked(level):
                    for tt in ((0, 1) if level < LEVELS else (0,)):
                        n = first[L + f"pairs{level}"] + tt
                        wait_product(dve, n)
                        a4 = bank(n).rearrange(heads, t=P)
                        dst = AT[:, :, 1, :] if level == LEVELS else AT[:, :, 2 * tt, :]
                        if level == LEVELS:
                            v_.tensor_copy(dst, a4).then_inc(evicted[n % BANKS], 1)
                            continue
                        mask = con(f"pair{level}", P).unsqueeze(1).broadcast_to([P, HG_H, P])
                        tmp = TMP[:, tt, :].rearrange(heads, t=P)
                        v_.tensor_tensor(dst if level == 0 else tmp, a4, mask, ALU.mult).then_inc(evicted[n % BANKS], 1)
                        wait_evicted(dve, n)
                        if level:
                            link(v_.tensor_tensor(dst, dst, tmp, ALU.add))

                def mean_square(n, count):
                    wait_product(dve, n)
                    v_.tensor_scalar(V[:], bank(n, 0, T), 1.0 / count, EPS, ALU.mult, ALU.add).then_inc(evicted[n % BANKS], 1)
                    wait_evicted(dve, n)
                    v_.tensor_copy(V[:, 0:1], V[:, 0:1]).then_inc(mean_ready, 1)

                def scale_tiles(a, kt, gain):
                    dve.wait_ge(rstd_ready, tally.add("rstd_ready") + 1)
                    for k in range(kt):
                        v_.scalar_tensor_tensor(a[:, k, :], a[:, k, :], gain[:, k:k + 1], RSTD[:], ALU.mult, ALU.mult)\
                          .then_inc(normed, 1)

                for level in range(LEVELS + 1):
                    if level < LEVELS:
                        feed.to(win0 + PAIRS_AFTER + level + 1)
                        if level >= 2:
                            wait_product(dve, first[L + f"pairs{level - 1}"] + 1)
                        exponents(level)
                    if level == LATENTS_AFTER - PAIRS_AFTER:
                        for i in (4, 5, 6, 7):
                            for m in range(WIN1[i][2]):
                                wait_evicted(dve, first[L + f"win{i}"] + m)
                        v_.tensor_tensor(LATENT_SQ[:, 0:3, :], CQ, CQ, ALU.mult).then_inc(squares_ready, 1)
                        v_.tensor_tensor(LATENT_SQ[:, 3:5, :], CKV, CKV, ALU.mult).then_inc(squares_ready, 1)
                        mean_square(first[L + "latent.norm"], 3 * P)
                        scale_tiles(CQ, 3, vec(f"q_lat_norm{l}", 3))
                        mean_square(first[L + "latent.norm"] + 1, 2 * P)
                        scale_tiles(CKV, 2, vec(f"kv_lat_norm{l}", 2))
                    masked(level)
                    if level < LEVELS:
                        factors(level)
                wait_evicted(dve, first[L + f"pairs{LEVELS}"])
                v_.tensor_copy(AT[:, 0, 0, 0:1], AT[:, 0, 0, 0:1]).then_inc(pairs_summed, 1)
                feed.to(slab_first[L + "hg.gate0"])
                cos2 = COS[64:96, :].unsqueeze(1).broadcast_to([ROPE, 2, T])
                sin2 = SIN[64:96, :].unsqueeze(1).broadcast_to([ROPE, 2, T])
                for m in range(4):
                    if m == 2:
                        feed.to(slab_first[L + "hg.gate0"] + 1)
                    n = first[L + "swap"] + m
                    q = QH[64:96, 2 * m:2 * m + 2, :]
                    turned = TMP[64:96, m % 2, :].rearrange("p (g t) -> p g t", g=2)
                    wait_product(dve, n)
                    v_.tensor_tensor(turned, bank(n)[64:96, :].rearrange("p (g t) -> p g t", g=2), sin2, ALU.mult)\
                      .then_inc(evicted[n % BANKS], 1)
                    wait_evicted(dve, n)
                    link(v_.tensor_tensor(q, q, cos2, ALU.mult))
                    link(v_.tensor_tensor(q, q, turned, ALU.add))
                n = first[L + "swap"] + 4
                wait_product(dve, n)
                v_.tensor_tensor(TMP[64:96, 0, 0:T], bank(n)[64:96, 0:T], SIN[64:96, :], ALU.mult).then_inc(evicted[n % BANKS], 1)
                link(v_.tensor_tensor(KR[64:96, 1, :], KR[64:96, 0, :], COS[64:96, :], ALU.mult))
                wait_evicted(dve, n)
                link(v_.tensor_tensor(KR[64:96, 1, :], KR[64:96, 1, :], TMP[64:96, 0, 0:T], ALU.add))
                v_.tensor_copy(KH[64:96, :, :], KR[64:96, 1, :].unsqueeze(1).broadcast_to([ROPE, MLA_H, T])).then_inc(roped, 1)
                wait_evicted(dve, first[L + "hg.o"])
                wait_evicted(dve, first[L + "hg.o"] + 1)
                group_norm(L + "hg.norm", HG_SQ, P, (slab_first[L + "hg.gate1"], slab_first[L + "hg.gate1"] + 1))
                link(v_.scalar_tensor_tensor(OT, OT, vec(f"hg_out_norm{l}", 1), TMP[:].rearrange("p a (b t) -> p (a b) t", t=T), ALU.mult, ALU.mult))
                for i in (10, 11):
                    for m in range(2):
                        wait_evicted(dve, first[L + f"win{i}"] + m)
                v_.tensor_tensor(OT, OT, HGT, ALU.mult).then_inc(normed, 1)
                dve.wait_ge(normed, l * (DK + 6) + 6)
                dve.wait_ge(mem_in, 16 * (l + 1))
                v_.tensor_tensor(MEM_SQ, MEM, MEM, ALU.mult).then_inc(squares_ready, 1)
                merge(L + "hg.out", start=True)
                causal = con("causal", 2 * P)

                def own(i, b):
                    return causal[:, (1 - i % 2) * P:2 * P].unsqueeze(1).broadcast_to([P, 2, (i % 2 + 1) * P])

                attention(L + "mla", "mla", QK ** -0.5, own)
                mean_square(first[L + "mem.norm"], D)
                scale_tiles(MEM, DK, vec(f"mem_norm{l}", DK))
                merge(L + "mla.out")
                attention(L + "mem", "mem", P ** -0.5)
                merge(L + "mem.out", end=True)
                for m in range(DK):
                    add_to_x(L + "wout", 1.0, m)
                ffn(L + "ffn2", vec(f"ffn2_norm{l}", DK))
            norm_x(vec("final1", DK), X)
            dve.wait_ge(normed, NORMED_1)
            for m in range(DK):
                add_squares(m)

            for l, L in enumerate(block2):
                ffn(L + "ffn1", vec(f"norm_g{l}0", DK))
                norm_u(vec(f"norm_g{l}1", DK), slab_first[L + "win0"])
                win0 = slab_first[L + "win0"]
                feed.to(win0 + 1)
                for kv in range(2):
                    feed.to(slab_first[L + f"win{2 + kv}"])
                    if kv == 1:
                        feed.to(slab_first[L + "win4"])
                    wait_evicted(dve, first[L + f"win{kv}"])
                    src = (KC2, VC2)[kv]
                    for half in range(2):
                        dst = (BLK, BLK2)[kv][:, 8 * half:8 * half + 8, :].rearrange("p l (g n) -> p l g n", g=2)
                        tok = src[:, :, 16 * half:16 * half + 240].rearrange("p g (n l two) -> p l g n two", l=8, two=2)[:, :, :, :, 0]
                        pos = vec(f"pos{l}{kv}", 16)[:, 8 * half:8 * half + 8].unsqueeze(2).unsqueeze(3).broadcast_to([P, 8, 2, 15])
                        last = v_.tensor_tensor(dst, tok, pos, ALU.add)
                    last.then_inc(blocks_ready, 1)
                for j in range(4):
                    feed.to(slab_first[L + f"win{5 + j}"])
                    n, x = first[L + f"cmp{j}"], (HID, HID2)[j // 2]
                    terms = bank(n, 0, 60).rearrange("p (a b) -> p a b", a=2)
                    wait_product(dve, n)
                    if j % 2 == 0:
                        v_.tensor_copy(x, terms).then_inc(evicted[n % BANKS], 1)
                    else:
                        v_.tensor_tensor(x, x, terms, ALU.add).then_inc(evicted[n % BANKS], 1)
                    wait_evicted(dve, n)
                for kv in range(2):
                    feed.to(slab_first[L + f"win{(10, 12)[kv]}"])
                    x = (HID, HID2)[kv]
                    if 2 * l + kv:
                        dve.wait_ge(hidden_ready, 2 * l + kv)
                    link(v_.tensor_tensor(GY, x, x, ALU.mult))
                    link(v_.tensor_scalar(GY, GY, 0.044715, 1.0, ALU.mult, ALU.add))
                    v_.tensor_tensor(GY, GY, x, ALU.mult).then_inc(gelu_vec, 1)
                    dve.wait_ge(gelu_act, tally.add("gelu_act") + 1)
                    link(v_.tensor_scalar(GY, GY, 1.0, None, ALU.add))
                    link(v_.reciprocal(GY, GY))
                    v_.tensor_tensor(x, x, GY, ALU.mult).then_inc(hidden_ready, 1)
                feed.to(slab_first[L + "win15"])
                if l == 0:
                    dve.wait_ge(windows_in, 16)

                def pair_window(h0):
                    def get(i, b):
                        if h0 == 4 and b == 0:
                            h = h0 + i // 2
                            return WIN[:, h:h + 5:4, (CMP_LEN - 1 + P * (1 - i % 2)):2 * P:CMP_STRIDE]
                        h = h0 + i // 2
                        return WIN[:, h:h + 5:4, (1 - i % 2) * P:2 * P]
                    return get

                def head_window(i, b):
                    return WIN[:, i // 2, (1 - i % 2) * P:2 * P].unsqueeze(1).broadcast_to([P, 2, (i % 2 + 1) * P])

                o = attention(L + "A", "A", 64 ** -0.5, head_window, lam=LAM[:, 5, l:l + 1])
                for i in range(6, 8):
                    wait_evicted(dve, o[i])
                group_norm(L + "A.norm", AQ, P)
                link(v_.tensor_scalar(OT, OT, vec(f"subln{l}", 1), 1.0 - LAM_INIT[l], ALU.mult, ALU.mult))
                v_.tensor_tensor(OT, OT, TMP[:].rearrange("p a (b t) -> p (a b) t", t=T), ALU.mult).then_inc(normed, 1)
                merge(L + "A.out", start=True)
                wait_evicted(dve, first[L + "win9"])
                attention(L + "B", "B", 64 ** -0.5, pair_window(4))
                merge(L + "B.out")
                attention(L + "C", "C", 64 ** -0.5, pair_window(12), sinks=vec(f"sinks{l}", 8))
                merge(L + "C.out", end=True)
                for m in range(DK):
                    add_to_x(L + "wout", 1.0, m)
                ffn(L + "ffn2", vec(f"norm_g{l}2", DK))
                norm_u(vec(f"norm_g{l}3", DK), slab_first[L + "ple.gate"])
                for m in range(DK):
                    if m % 2 == 0:
                        feed.to(slab_first[L + "ple.gate"] + m // 2 + 1)
                    wait_evicted(dve, first[L + "ple.gate"] + m)
                    link(v_.tensor_tensor(GATE[:, m, :], GATE[:, m, :], PLE[:, m, :], ALU.mult))
                    link(v_.tensor_tensor(X[:, m, :], X[:, m, :], GATE[:, m, :], ALU.add))
                    add_squares(m)
            norm_x(vec("final2", DK), U, done=result_ready)


_WEIGHTS = ["w_ffn1_in", "w_ffn1_out", "w_in", "w_uq", "w_uk", "w_uv", "w_o_mla", "w_o_hg", "w_mem_kv", "w_o_mem",
            "w_out", "w_ffn2_in", "w_ffn2_out", "ffn1_wi_2", "ffn1_wo_2", "w_in_2", "nsa_cmp_w1_2", "nsa_cmp_w2_2",
            "w_branch_2", "w_out_2", "ffn2_wi_2", "ffn2_wo_2", "w_ple_2", "w_ple_gate_2"]


def kernel(**inputs):
    import concourse.bacc as _bacc
    from concourse.bass_utils import run_bass_kernel_spmd as _run

    arrays = {name: np.ascontiguousarray(inputs[name]) for name in _WEIGHTS}
    arrays["cst"] = constants()[0]
    arrays["vec"] = pack_vectors(inputs)
    arrays["xT"] = np.ascontiguousarray(np.asarray(inputs["x"])[0].T)
    arrays["memT"] = np.ascontiguousarray(np.asarray(inputs["mem"])[0].T)
    arrays["pT"] = np.ascontiguousarray(np.asarray(inputs["p_2"])[:, 0].transpose(0, 2, 1))
    arrays["pos"] = np.ascontiguousarray(np.broadcast_to(np.asarray(inputs["positions"]), (ROPE, T)))

    nc = _bacc.Bacc("TRN2", target_bir_lowering=False, num_devices=1)
    w = {name: nc.dram_tensor(f"in_{name}", a.shape, mybir.dt.from_np(a.dtype), kind="ExternalInput").ap()
         for name, a in arrays.items()}
    out = nc.dram_tensor("out_xT", [D, T], FP, kind="ExternalOutput").ap()
    scratch_rows = nc.dram_tensor("bias_rows", [P, BIAS_H, 2 * T], FP, kind="Internal").ap()
    build(nc, w, VECS, out, scratch_rows)
    r = _run(nc, [{f"in_{name}": a for name, a in arrays.items()}], core_ids=[0])
    return np.ascontiguousarray(r.results[0]["out_xT"].T).reshape(1, T, D)
```
